# Optimizing a Trainium2 kernel written in Bass

```python
import jax, jax.numpy as jnp
from jax import lax
import numpy as np

D_MODEL = 2048
BATCH = 1
SEQ = 512
DEPTH = 1

A_HEADS = 8
A_HEAD_DIM = 128
A_WIDTH = A_HEADS * A_HEAD_DIM
Q_RANK = 512
IDX_HEADS = 16
IDX_DIM = 128
TOPK_MAX = 256
Q_BLOCK = 128
ROPE_THETA = 10000.0
G_HEADS = 8
G_KDIM = 128
G_VDIM = 128
G_WIDTH_K = G_HEADS * G_KDIM
G_WIDTH_V = G_HEADS * G_VDIM
CHUNK = 64
N_GROUPS = 4
EXP_PER_GROUP = 8
N_EXPERTS = N_GROUPS * EXP_PER_GROUP
TOPK_EXP = 2
D_EXPERT = 512
EPS = 1e-6
SEG_SIZES = (Q_RANK, A_HEAD_DIM, A_HEAD_DIM, IDX_DIM, IDX_HEADS, G_WIDTH_K, G_WIDTH_K, G_WIDTH_V, G_WIDTH_V, D_MODEL, D_MODEL)
D_IN = Q_RANK + 2 * A_HEAD_DIM + IDX_DIM + IDX_HEADS + 2 * G_WIDTH_K + 2 * G_WIDTH_V + 2 * D_MODEL

kernel_name = 'hybrid_dsa_hgrn2_hmoe'

def rmsnorm(x, g):
    x32 = x.astype(jnp.float32)
    y = x32 * lax.rsqrt(jnp.mean(x32 * x32, axis=-1, keepdims=True) + EPS)
    return (y * g.astype(jnp.float32)).astype(x.dtype)

def rope_tables(seq, dim):
    inv = 1.0 / (ROPE_THETA ** (jnp.arange(0, dim, 2, dtype=jnp.float32) / dim))
    ang = jnp.arange(seq, dtype=jnp.float32)[:, None] * inv[None, :]
    return jnp.cos(ang), jnp.sin(ang)

def apply_rope(x, cos, sin):
    x32 = x.astype(jnp.float32)
    x1, x2 = jnp.split(x32, 2, axis=-1)
    c = cos[None, :, None, :]
    s = sin[None, :, None, :]
    return jnp.concatenate([x1 * c - x2 * s, x2 * c + x1 * s], axis=-1).astype(x.dtype)

def split_cols(p):
    bounds = np.cumsum(SEG_SIZES)[:-1].tolist()
    return jnp.split(p, bounds, axis=-1)

def dsa_attention(c_q, k_att, v_att, k_idx, w_idx, g_cq, w_uq, w_qidx, cos, sin):
    b, s, _ = c_q.shape
    topk = min(TOPK_MAX, s // 4)
    nb = s // Q_BLOCK
    cqn = rmsnorm(c_q, g_cq)
    q = apply_rope((cqn @ w_uq).reshape(b, s, A_HEADS, A_HEAD_DIM), cos, sin)
    qi = apply_rope((cqn @ w_qidx).reshape(b, s, IDX_HEADS, IDX_DIM), cos, sin)
    k = apply_rope(k_att[:, :, None, :], cos, sin)[:, :, 0, :]
    ki = apply_rope(k_idx[:, :, None, :], cos, sin)[:, :, 0, :]
    wi = w_idx.astype(jnp.float32) * (IDX_HEADS ** -0.5 * IDX_DIM ** -0.5)
    key_pos = jnp.arange(s)
    scale = A_HEAD_DIM ** -0.5

    def blocks(t):
        return jnp.swapaxes(t.reshape((b, nb, Q_BLOCK) + t.shape[2:]), 0, 1)

    def one_block(args):
        qb, qib, wb, pos = args
        logits = jnp.einsum('bthd,bsd->bths', qib, ki, preferred_element_type=jnp.float32)
        score = jnp.einsum('bths,bth->bts', jax.nn.relu(logits), wb)
        causal = key_pos[None, :] <= pos[:, None]
        score = jnp.where(causal[None], score, -jnp.inf)
        _, idx = lax.top_k(score, topk)
        valid = idx <= pos[None, :, None]
        kg = jax.vmap(lambda kk, ii: kk[ii])(k, idx)
        vg = jax.vmap(lambda vv, ii: vv[ii])(v_att, idx)
        att = jnp.einsum('bthd,btkd->bthk', qb, kg, preferred_element_type=jnp.float32) * scale
        att = jnp.where(valid[:, :, None, :], att, -jnp.inf)
        p = jax.nn.softmax(att, axis=-1)
        return jnp.einsum('bthk,btkd->bthd', p.astype(vg.dtype), vg)

    pos_blocks = key_pos.reshape(nb, Q_BLOCK)
    out = lax.map(one_block, (blocks(q), blocks(qi), blocks(wi), pos_blocks))
    return jnp.swapaxes(out, 0, 1).reshape(b, s, A_WIDTH)

def hgrn2(hq, hf, hi, hg, lb, g_onorm):
    b, s, _ = hq.shape
    n = s // CHUNK
    f = lb + (1.0 - lb) * jax.nn.sigmoid(hf.astype(jnp.float32))
    log_f = jnp.log(f)
    k = 1.0 - f
    q = jax.nn.silu(hq.astype(jnp.float32))
    v = hi.astype(jnp.float32)

    def chunks(t, d):
        return t.reshape(b, n, CHUNK, G_HEADS, d).transpose(1, 0, 3, 2, 4)

    tri = jnp.tril(jnp.ones((CHUNK, CHUNK), dtype=bool))

    def step(state, inp):
        qc, kc, vc, gc = inp
        cum = jnp.cumsum(gc, axis=2)
        diff = cum[:, :, :, None, :] - cum[:, :, None, :, :]
        decay = jnp.exp(jnp.where(tri[None, None, :, :, None], diff, -jnp.inf))
        scores = jnp.einsum('bhtsd,bhsd->bhts', qc[:, :, :, None, :] * decay, kc)
        o = jnp.einsum('bhts,bhsv->bhtv', scores, vc) + jnp.einsum('bhtd,bhdv->bhtv', qc * jnp.exp(cum), state)
        last = cum[:, :, -1:, :]
        new_state = jnp.exp(last[:, :, 0, :])[..., None] * state + jnp.einsum('bhsd,bhsv->bhdv', kc * jnp.exp(last - cum), vc)
        return new_state, o

    s0 = jnp.zeros((b, G_HEADS, G_KDIM, G_VDIM), jnp.float32)
    _, o = lax.scan(step, s0, (chunks(q, G_KDIM), chunks(k, G_KDIM), chunks(v, G_VDIM), chunks(log_f, G_KDIM)))
    o = o.transpose(1, 0, 3, 2, 4).reshape(b, s, G_WIDTH_V).astype(hq.dtype)
    return rmsnorm(o, g_onorm) * jax.nn.silu(hg)

def hier_moe(h, w_grp, b_grp, w_exp, b_exp, w_gate, w_up, w_down):
    b, s, d = h.shape
    n = b * s
    t = h.reshape(n, d)
    p_grp = jax.nn.softmax((t @ w_grp).astype(jnp.float32) + b_grp.astype(jnp.float32), axis=-1)
    grp = jnp.argmax(p_grp, axis=-1)
    p_g = jnp.max(p_grp, axis=-1, keepdims=True)
    logit_e = ((t @ w_exp).astype(jnp.float32) + b_exp.astype(jnp.float32)).reshape(n, N_GROUPS, EXP_PER_GROUP)
    logit_e = logit_e[jnp.arange(n), grp]
    p_e, e_idx = lax.top_k(jax.nn.softmax(logit_e, axis=-1), TOPK_EXP)
    gate = p_g * p_e / jnp.sum(p_e, axis=-1, keepdims=True)
    eid = (grp[:, None] * EXP_PER_GROUP + e_idx).reshape(-1)
    order = jnp.argsort(eid)
    tok = order // TOPK_EXP
    xs = t[tok]
    sizes = jnp.bincount(eid, length=N_EXPERTS).astype(jnp.int32)
    a = lax.ragged_dot(xs, w_gate, sizes)
    u = lax.ragged_dot(xs, w_up, sizes)
    y = lax.ragged_dot(jax.nn.silu(a) * u, w_down, sizes)
    y = y * gate.reshape(-1)[order][:, None].astype(y.dtype)
    return jax.ops.segment_sum(y, tok, num_segments=n).reshape(b, s, d)

def setup_inputs(seed: int = 0) -> dict:
    key = jax.random.key(seed)
    ks = jax.random.split(key, 20)
    f32 = jnp.float32

    def nrm(k, shape, fan_in):
        return jax.random.normal(k, shape, f32) * (fan_in ** -0.5)

    def gain(k, shape):
        return 1.0 + 0.02 * jax.random.normal(k, shape, f32)

    return {
        'x': jax.random.normal(ks[0], (BATCH, SEQ, D_MODEL), f32),
        'g_norm1': gain(ks[1], (DEPTH, D_MODEL)),
        'w_in': nrm(ks[2], (DEPTH, D_MODEL, D_IN), D_MODEL),
        'g_cq': gain(ks[3], (DEPTH, Q_RANK)),
        'w_uq': nrm(ks[4], (DEPTH, Q_RANK, A_WIDTH), Q_RANK),
        'w_qidx': nrm(ks[5], (DEPTH, Q_RANK, IDX_HEADS * IDX_DIM), Q_RANK),
        'lb_logits': 0.5 * jax.random.normal(ks[6], (DEPTH + 1, G_WIDTH_K), f32),
        'g_hnorm': gain(ks[7], (DEPTH, G_WIDTH_V)),
        'w_pa': nrm(ks[8], (DEPTH, A_WIDTH, D_MODEL), A_WIDTH),
        'w_pb': nrm(ks[9], (DEPTH, G_WIDTH_V, D_MODEL), G_WIDTH_V),
        'w_o': nrm(ks[10], (DEPTH, D_MODEL, D_MODEL), D_MODEL),
        'g_norm2': gain(ks[11], (DEPTH, D_MODEL)),
        'w_grp': nrm(ks[12], (DEPTH, D_MODEL, N_GROUPS), D_MODEL),
        'b_grp': 0.01 * jax.random.normal(ks[13], (DEPTH, N_GROUPS), f32),
        'w_exp': nrm(ks[14], (DEPTH, D_MODEL, N_EXPERTS), D_MODEL),
        'b_exp': 0.01 * jax.random.normal(ks[15], (DEPTH, N_EXPERTS), f32),
        'w_gate': nrm(ks[16], (DEPTH, N_EXPERTS, D_MODEL, D_EXPERT), D_MODEL),
        'w_up': nrm(ks[17], (DEPTH, N_EXPERTS, D_MODEL, D_EXPERT), D_MODEL),
        'w_down': nrm(ks[18], (DEPTH, N_EXPERTS, D_EXPERT, D_MODEL), D_EXPERT),
        'g_final': gain(ks[19], (D_MODEL,)),
    }

def reference(x, g_norm1, w_in, g_cq, w_uq, w_qidx, lb_logits, g_hnorm, w_pa, w_pb, w_o, g_norm2, w_grp, b_grp, w_exp, b_exp, w_gate, w_up, w_down, g_final):
    s = x.shape[1]
    cos, sin = rope_tables(s, A_HEAD_DIM)
    lb_all = jnp.cumsum(jax.nn.softmax(lb_logits.astype(jnp.float32), axis=0), axis=0)
    for l in range(DEPTH):
        h = rmsnorm(x, g_norm1[l])
        c_q, k_att, v_att, k_idx, w_idx, hq, hf, hi, hg, ga, gb = split_cols(h @ w_in[l])
        y_att = dsa_attention(c_q, k_att, v_att, k_idx, w_idx, g_cq[l], w_uq[l], w_qidx[l], cos, sin)
        y_rec = hgrn2(hq, hf, hi, hg, lb_all[l], g_hnorm[l])
        merged = jax.nn.sigmoid(ga) * (y_att @ w_pa[l]) + jax.nn.sigmoid(gb) * (y_rec @ w_pb[l])
        x = x + merged @ w_o[l]
        x = x + hier_moe(rmsnorm(x, g_norm2[l]), w_grp[l], b_grp[l], w_exp[l], b_exp[l], w_gate[l], w_up[l], w_down[l])
    return rmsnorm(x, g_final)


_drawn_inputs = setup_inputs


def setup_inputs(seed=0):
    import zlib

    import numpy as np

    out = dict(_drawn_inputs(seed))
    spreads = {}
    factors = {'g_cq': 3.757,
     'g_hnorm': 11.854,
     'b_grp': 21.154,
     'b_exp': 20.382,
     'g_final': 8.48,
     'g_norm2': 2.999}
    for name, (base, spread) in spreads.items():
        noise = np.random.default_rng([zlib.crc32(name.encode()), seed]).standard_normal(out[name].shape)
        drawn = base * np.exp(spread * noise) if base else spread * noise
        out[name] = __import__('jax').numpy.asarray(drawn.astype(out[name].dtype))
    for name, factor in factors.items():
        out[name] = (out[name] * factor).astype(out[name].dtype)
    return out
```

```python
import math
from contextlib import ExitStack

import numpy as np

import concourse.bass as bass
from concourse import mybir

F32 = mybir.dt.float32
U32 = mybir.dt.uint32
ALU = mybir.AluOpType
ACT = mybir.ActivationFunctionType
AX = mybir.AxisListType

P = 128
D, T = 2048, 512
KD, NT = D // P, T // P
A_HEADS, HEAD_D = 8, 128
Q_RANK = 512
IDX_HEADS, IDX_D = 16, 128
TOPK = 128
G_HEADS = 8
N_GROUPS, PER_GROUP = 4, 8
N_EXP = N_GROUPS * PER_GROUP
D_EXP = 512
EPS = 1e-6
A_WIDTH = A_HEADS * HEAD_D
G_WIDTH = G_HEADS * 128
FILL = -3.0e38
TAKEN = -3.4e38
OUT = -1.0e30

C_CQ = 0
C_K = C_CQ + Q_RANK
C_HQ = C_K + 3 * 128 + IDX_HEADS
C_HF, C_HI, C_HG = C_HQ + G_WIDTH, C_HQ + 2 * G_WIDTH, C_HQ + 3 * G_WIDTH
C_GA = C_HQ + 4 * G_WIDTH
C_GB = C_GA + D
D_IN = C_GB + D
MISC = C_HQ - C_K

SLOTS = 8
CHUNK = 2048
TILES = N_EXP + 8
OVER = N_EXP
LEVELS = 7
NO_ROW = 60000

RING = 0
HT = RING + SLOTS * CHUNK
YATT = HT + KD * T
YREC = YATT + A_HEADS * T
U = YREC + G_HEADS * T
TAB = U + 17920
SMALL = TAB + 3 * P + 8 * P + T
TOTAL = SMALL + 592


def panels():
    order = [("cq", 4, 0), ("misc", 4, 4), ("uq0", 1, 0), ("uq1", 1, 4),
             ("qi0", 1, 0), ("qi1", 1, 4), ("qi2", 1, 0), ("qi3", 1, 4),
             ("ga0", 4, 0), ("ga1", 4, 0), ("ga2", 4, 0),
             ("hq0", 4, 0), ("hf0", 4, 4), ("hi0", 4, 0), ("ga3", 4, 0), ("gb0", 4, 0),
             ("hq1", 4, 0), ("hf1", 4, 4), ("hi1", 4, 0), ("gb1", 4, 0), ("gb2", 4, 0),
             ("gb3", 4, 0), ("hg0", 4, 0), ("hg1", 4, 4)]
    for b in range(4):
        order += [(f"pa{b}", 2, 0), (f"pb{b}", 2, 4)]
    order += [(f"wo{b}", 4, 4 * (b % 2)) for b in range(4)]
    found, start = {}, 0
    for name, chunks, bank in order:
        found[name] = (start, chunks, bank)
        start += chunks
    return found, start


def attention_steps():
    idx = lambda t: [("idx", t, h) for h in range(IDX_HEADS)]
    att = lambda t: [("att", t, h) for h in range(A_HEADS)]
    return idx(1) + att(0) + idx(2) + att(1) + idx(3) + att(2) + att(3)


def build(nc, x, gains, w_in, w_uq, w_qidx, w_pa, w_pb, w_o, g_norm2,
          w_grp, b_grp, w_exp, b_exp, w_gate, w_up, w_down, g_final, t_const, t_rope, t_causal,
          t_route, t_rows, out):
    PANEL, FRONT = panels()
    STEPS = attention_steps()
    IDX_N = sum(s[0] == "idx" for s in STEPS)
    ATT_N = sum(s[0] == "att" for s in STEPS)

    gates_d = nc.dram_tensor("gates_exp", (2, 4, P, CHUNK), F32, kind="Internal").ap()
    h2_d = nc.dram_tensor("h2_rows", (T, D), F32, kind="Internal").ap()
    y2_d = nc.dram_tensor("expert_rows", (2 * T, D), F32, kind="Internal").ap()
    slots_d = nc.dram_tensor("slot_rows", ((TILES + 1) * P, 2), U32, kind="Internal").ap()

    ctx = ExitStack()
    with ctx:
        mem = ctx.enter_context(nc.sbuf_tensor("mem", [P, TOTAL], F32))
        ctx.enter_context(nc.allow_non_contiguous_dma("columns of gains, and slot tables"))
        banks = [ctx.enter_context(nc.psum_tensor(f"bank{i}", [P, 512], F32)) for i in range(8)]

        def at(start, *shape):
            n = math.prod(shape)
            v = mem[:, start:start + n]
            if len(shape) == 2:
                v = v.rearrange("p (a b) -> p a b", a=shape[0])
            if len(shape) == 3:
                v = v.rearrange("p (a b c) -> p a b c", a=shape[0], b=shape[1])
            return v

        def sem(name):
            return ctx.enter_context(nc.semaphore(name))

        ring = [at(RING + s * CHUNK, 4, 512) for s in range(SLOTS)]
        hT = at(HT, KD, T)
        yattT = at(YATT, A_HEADS, T)
        yrecT = at(YREC, G_HEADS, T)
        ident, ones, before = at(TAB, P), at(TAB + P, P), at(TAB + 2 * P, P)
        level_mask, restart = at(TAB + 3 * P, 8 * P), at(TAB + 11 * P, T)
        cur = [SMALL]

        def small(n):
            cur[0] += n
            assert cur[0] <= TOTAL
            return mem[:, cur[0] - n:cur[0]]

        g1c, gqc, ghc, lbx = small(KD), small(Q_RANK // P), small(G_HEADS), small(2 * G_HEADS)
        lb, one_lb = small(G_HEADS), small(G_HEADS)
        ssum, mean, rinv = small(NT), small(NT), small(NT)
        wi = small(NT * IDX_HEADS).rearrange("p (t h) -> p t h", t=NT)
        smax, nmax, rsum, rrec = small(32), small(32), small(32), small(32)
        top8, decay = small(8), small(4)
        xt = at(U + 4096, NT, D)
        junk = at(YATT, NT, D)
        qT, qiT = at(U, A_HEADS, T), at(U + 4096, IDX_HEADS, T)
        cqT = at(U + 12288, 4, T)
        kT, kiT, vtok = at(U + 14336, T), at(U + 14848, T), at(U + 15360, NT, P)
        stage = at(U + 15872, 4, 512)
        cos2, sin2 = at(YATT, T), at(YATT + T, T)
        cq_sq, cq_rms = at(YATT + 2 * T, 4, T), at(YATT + 6 * T, T)
        rope_a, rope_b = at(YREC, 2, T), at(YREC + 2 * T, 2, T)
        relu, score = at(YREC, 2, T), at(YREC + 2 * T, T)
        masked, probs = at(YREC + 3 * T, 2, T), at(YREC + 5 * T, 2, T)
        causal = at(YREC + 7 * T, T)
        bias, probsT = at(U + 12288, 2, T), at(U + 13312, 2, T)
        hq, hk, hc, hv = (at(U + 2048 * i, 4, T) for i in range(4))
        QK = 9 * 256
        qk = [at(U + 8192 + QK * i, 9, 256) for i in range(2)]
        lev = at(U + 12800, 8 * P)
        intra, keT, state = (at(U + 13824 + 256 * i, 2, P) for i in range(3))
        mT = at(U, KD, T)
        gate_a, gate_b = at(U + 8192, 4, 512), at(U + 10240, 4, 512)
        g2b, gfb = at(U + 12288, D), at(U + 14336, D)
        x1 = at(HT, NT, D)
        h2 = at(YATT, NT, D)
        h2T = at(U, KD, T)
        wr = at(U + 8192, KD, 36)
        rt = U + 8192 + KD * 36
        xg = [at(U + D * i, D) for i in range(2)]
        xgT = [at(U + 4096 + D * i, KD, P) for i in range(2)]
        act_e, act_h, actT = at(U + 10240, 512), at(U + 10752, 512), at(U + 11264, 4, P)
        yb = [at(YATT + D * i, D) for i in range(2)]
        yfin = [at(RING + 2 * D * i, 2, D) for i in range(4)]

        w_loaded = [sem(f"w_loaded{s}") for s in range(SLOTS)]
        x_loaded = [sem(f"x_loaded{t}") for t in range(NT)]
        small_loaded, rope_loaded, causal_loaded = sem("small_loaded"), sem("rope_loaded"), sem("causal_loaded")
        gate_stored, gate_loaded, late_loaded = sem("gate_stored"), sem("gate_loaded"), sem("late_loaded")
        h2_stored, slots_cleared, slots_written = sem("h2_stored"), sem("slots_cleared"), sem("slots_written")
        slots_loaded, yb_sent = sem("slots_loaded"), [sem(f"yb_sent{i}") for i in range(2)]
        xg_loaded = [sem(f"xg_loaded{i}") for i in range(2)]
        yfin_loaded = [sem(f"yfin_loaded{i}") for i in range(4)]
        out_stored = sem("out_stored")
        chunks_done, xT_ps, ssq_ps = sem("chunks_done"), sem("xT_ps"), sem("ssq_ps")
        logits_ps, probsT_ps, att_ps = sem("logits_ps"), sem("probsT_ps"), sem("att_ps")
        tree_ps, keT_ps, state_ps, rec_ps = sem("tree_ps"), sem("keT_ps"), sem("state_ps"), sem("rec_ps")
        recsq_ps, h2T_ps, router_ps, rank_ps = sem("recsq_ps"), sem("h2T_ps"), sem("router_ps"), sem("rank_ps")
        xgT_ps, actT_ps = sem("xgT_ps"), sem("actT_ps")
        squared, rooted, hT_act, cq_squared = sem("squared"), sem("rooted"), sem("hT_act"), sem("cq_squared")
        relu_done, exp_done, probsT_sb, att_sb = sem("relu_done"), sem("exp_done"), sem("probsT_sb"), sem("att_sb")
        gate_exp, hq_exp, hf_exp, hf_ln, hv_sb = (sem("gate_exp"), sem("hq_exp"), sem("hf_exp"), sem("hf_ln"),
                                                  sem("hv_sb"))
        tree_exp, keT_sb, rec_sb, rec_squared = sem("tree_exp"), sem("keT_sb"), sem("rec_sb"), sem("rec_squared")
        hg_exp, h2T_act, route_exp = sem("hg_exp"), sem("h2T_act"), sem("route_exp")
        xgT_act, silu_exp, actT_sb, y_act = sem("xgT_act"), sem("silu_exp"), sem("actT_sb"), sem("y_act")
        fin_act, lb_exp = sem("fin_act"), sem("lb_exp")
        v_seq = sem("v_seq")
        mean_ready, h_ready, hT_dve = sem("mean_ready"), sem("h_ready"), sem("hT_dve")
        cq_raw, cq_norm, v_copied, rope_mul = sem("cq_raw"), sem("cq_norm"), sem("v_copied"), sem("rope_mul")
        scored, att_masked, nmax_ready, probs_ready = (sem("scored"), sem("att_masked"), sem("nmax_ready"),
                                                       sem("probs_ready"))
        hq_ready, hf_ready, tree_arg = sem("hq_ready"), sem("hf_ready"), sem("tree_arg")
        tree_masked, intra_ready, state_ready = sem("tree_masked"), sem("intra_ready"), sem("state_ready")
        rec_normed, hg_ready, merge_read, merged_ready = (sem("rec_normed"), sem("hg_ready"), sem("merge_read"),
                                                          sem("merged_ready"))
        x1_ready, h2_ready, h2T_dve = sem("x1_ready"), sem("h2_ready"), sem("h2T_dve")
        route_arg, picked, placed, slots_ready = sem("route_arg"), sem("picked"), sem("placed"), sem("slots_ready")
        xgT_dve, act_ready, y_dve, fin_dve = sem("xgT_dve"), sem("act_ready"), sem("y_dve"), sem("fin_dve")
        silu_seq, fin_args, fin_mean, lb_arg = sem("silu_seq"), sem("fin_args"), sem("fin_mean"), sem("lb_arg")
        roped, qk_ready, xg_clear = sem("roped"), sem("qk_ready"), sem("xg_clear")
        slots_filled, tile_rows = sem("slots_filled"), sem("tile_rows")

        cur = [rt]

        def route(*shape):
            n = math.prod(shape)
            cur[0] += n
            return at(cur[0] - n, *shape)

        rowc = route(36 + 4 * 32)
        lg, le = route(NT, 8), route(NT, N_EXP)
        g8, gi8 = route(NT, 8), route(NT, 8).bitcast(U32)
        gneg, gsum, gexp, gidx = route(NT), route(NT), route(NT, 4), route(NT)
        gout = route(NT, 4)
        e8, ei8 = route(NT, 8), route(NT, 8).bitcast(U32)
        eidx = route(2, NT)
        diff, den, gate1, gate2 = route(NT), route(NT), route(NT), route(NT)
        pick = route(2, NT, N_EXP)
        both = route(NT, N_EXP)
        rank, count = route(NT, N_EXP), route(N_EXP)
        extra, upto, base, delta = route(N_EXP), route(N_EXP), route(N_EXP), route(N_EXP)
        pos, posp = route(NT, N_EXP), route(NT, N_EXP)
        slot = route(2, NT)
        assert cur[0] <= U + 12288
        cur = [U + 16384]
        slot_u = route(2 * NT).bitcast(U32)
        rows_u = route(2 * NT, 2).bitcast(U32)
        fill_u = route((TILES + 1) * 2).bitcast(U32)
        table_u = route(TILES + 1, 2).bitcast(U32)
        gather_u = [route(1).bitcast(U32) for _ in range(2)]
        scatter_u = [route(1).bitcast(U32) for _ in range(2)]
        ctrl_f, ctrl_u = route(16), route(16).bitcast(U32)
        ones_e, passed = route(N_EXP), route(1)
        gate1k, gate2k = route(NT), route(NT)
        fsum, fmean = route(NT), route(NT)
        assert cur[0] <= TAB

        block = ctx.enter_context(nc.Block())

        def step_count(kind, n):
            return sum(s[0] == kind for s in STEPS[:n])

        att_fill = [0] * len(STEPS)
        for n, (kind, t, h) in enumerate(STEPS):
            att_fill[n] = int(h % 3 == 2) if kind == "idx" else (4 if h == 2 and t < 3 else h % 2)
        rec_fill = [2] * 16

        def gate_ends(fill, names):
            total = [sum(fill[:n + 1]) for n in range(len(fill))]
            ends = {}
            for j, name in enumerate(names):
                at_step = next((n for n, k in enumerate(total) if k >= 16 * (j + 1)), None)
                ends.setdefault(at_step, []).append(name)
            return ends

        ATT_GATES, REC_GATES = ["ga0", "ga1", "ga2"], [["ga3", "gb0"], ["gb1", "gb2"]]
        GATE_NO = {n: i for i, n in enumerate(["ga0", "ga1", "ga2", "ga3", "gb0", "gb1", "gb2", "gb3"])}

        @block.sync
        def _(sp):
            def load(n, width, src):
                if n >= SLOTS:
                    sp.wait_ge(chunks_done, n - SLOTS + 1)
                dst = ring[n % SLOTS] if width == 512 else \
                    mem[:, RING + n % SLOTS * CHUNK:RING + n % SLOTS * CHUNK + 4 * width] \
                    .rearrange("p (k n) -> p k n", k=4)
                sp.dma_start(dst, src.rearrange("(k p) n -> p k n", p=P)).then_inc(w_loaded[n % SLOTS], 16)

            col = {"cq": (w_in, C_CQ, 512), "misc": (w_in, C_K, MISC)}
            for b in range(4):
                if b < 2:
                    col[f"uq{b}"] = (w_uq, 512 * b, 512)
                    for name, c0 in (("hq", C_HQ), ("hf", C_HF), ("hi", C_HI), ("hg", C_HG)):
                        col[f"{name}{b}"] = (w_in, c0 + 512 * b, 512)
                col[f"qi{b}"] = (w_qidx, 512 * b, 512)
                col[f"ga{b}"], col[f"gb{b}"] = (w_in, C_GA + 512 * b, 512), (w_in, C_GB + 512 * b, 512)
                col[f"pa{b}"], col[f"pb{b}"] = (w_pa, 512 * b, 512), (w_pb, 512 * b, 512)
                col[f"wo{b}"] = (w_o, 512 * b, 512)
            for name, (start, chunks, _) in PANEL.items():
                w, c0, width = col[name]
                for g in range(chunks):
                    load(start + g, width, w[g * 512:(g + 1) * 512, c0:c0 + width])

            def expert_weights(n0, used, expert):
                for c in range(12):
                    s = (n0 + c) % SLOTS
                    sp.wait_ge(chunks_done, used + c - SLOTS + 1)
                    if c < 8:
                        w = w_gate if c < 4 else w_up
                        src = w[bass.ds(expert, 1), c % 4 * 512:(c % 4 + 1) * 512, :]
                    else:
                        src = w_down[bass.ds(expert, 1), :, (c - 8) * 512:(c - 7) * 512]
                    sp.dma_start(ring[s], src.rearrange("e (k p) n -> p (e k) n", p=P)).then_inc(w_loaded[s], 16)

            with sp.Fori(0, N_EXP // 2) as i:
                for j in range(2):
                    expert_weights(FRONT + 12 * j, i * 24 + (FRONT + 12 * j), i * 2 + j)
            sp.wait_ge(slots_ready, 1)
            over = sp.value_load(ctrl_u[0:1, 0:1], min_val=0, max_val=7)
            with sp.If(over > 0):
                with sp.Fori(0, 4) as i:
                    for j in range(2):
                        e = sp.value_load(ctrl_u[0:1, bass.ds(i * 2 + (1 + j), 1)], min_val=0, max_val=N_EXP - 1)
                        expert_weights(FRONT + 12 * j, i * 24 + (FRONT + 12 * (N_EXP + j)), e)
                for j in range(2):
                    sp.wait_ge(yb_sent[j], 16 * (1 + TILES // 2))
                sp.wait_ge(xg_loaded[0], 16 * (1 + TILES // 2))
            for j in range(2):
                sp.wait_ge(yb_sent[j], 16 * (1 + N_EXP // 2))
            sp.wait_ge(xg_loaded[0], 16 * (1 + N_EXP // 2))
            for t in range(NT):
                sp.dma_start(yfin[t], y2_d[2 * P * t:2 * P * (t + 1), :].rearrange("(p c) d -> p c d", c=2)) \
                    .then_inc(yfin_loaded[t], 16)
            for t in range(NT):
                sp.wait_ge(fin_dve, t + 1)
                sp.dma_start(out[0, t * P:(t + 1) * P, :], x1[:, t, :]).then_inc(out_stored, 16)
            sp.wait_ge(out_stored, 16 * NT)

        @block.gpsimd
        def _(pool):
            pool.dma_start(mem[:, TAB:SMALL], t_const).then_inc(small_loaded, 16)
            pool.dma_start(mem[:, SMALL:SMALL + KD + 4 + 3 * G_HEADS], gains).then_inc(small_loaded, 16)
            pool.wait_ge(squared, 4)
            pool.dma_start(at(YATT, 2 * T), t_rope).then_inc(rope_loaded, 16)
            pool.dma_start(causal, t_causal).then_inc(causal_loaded, 16)

            outs = [kT, kiT] + [qT[:, h, :] for h in range(A_HEADS)] + [qiT[:, h, :] for h in range(IDX_HEADS)]
            for n, o in enumerate(outs):
                pool.wait_ge(rope_mul, n + 1)
                nc.gpsimd.tensor_tensor(o, rope_a[:, n % 2, :], rope_b[:, n % 2, :], ALU.add).then_inc(roped, 1)

            for n in range(16):
                b, f, pair = n // 8, n % 8 // 2, n % 2
                buf, tok = qk[n % 2], slice(pair * 256, pair * 256 + 256)
                pool.wait_ge(tree_exp, n + 1)
                for m in range(LEVELS):
                    h = P >> (m + 1)
                    v = buf[:, m, :].rearrange("p (b s h) -> p b s h", s=2, h=h)
                    q4 = hq[:, f, tok].rearrange("p (b s h) -> p b s h", s=2, h=h)
                    k4 = hk[:, f, tok].rearrange("p (b s h) -> p b s h", s=2, h=h)
                    nc.gpsimd.tensor_tensor(v[:, :, 1, :], v[:, :, 1, :], q4[:, :, 1, :], ALU.mult)
                    nc.gpsimd.tensor_tensor(v[:, :, 0, :], v[:, :, 0, :], k4[:, :, 0, :], ALU.mult)
                nc.gpsimd.tensor_tensor(buf[:, 7, :], buf[:, 7, :], hk[:, f, tok], ALU.mult)
                nc.gpsimd.tensor_tensor(buf[:, 8, :], buf[:, 8, :], hq[:, f, tok], ALU.mult).then_inc(qk_ready, 1)

            pool.wait_ge(x1_ready, 16)
            nc.gpsimd.memset(passed, 0.0)
            nc.gpsimd.memset(fill_u, NO_ROW).then_inc(slots_filled, 1)
            pool.wait_ge(slots_filled, 1)
            pool.dma_start(slots_d.rearrange("(p n) c -> p (n c)", p=P), fill_u).then_inc(slots_cleared, 16)
            pool.dma_start(rows_u, t_rows.rearrange("p (n c) -> p n c", c=2)).then_inc(slots_cleared, 16)
            for t in range(2):
                pool.wait_ge(h2_ready, t + 1)
                pool.dma_start(h2_d[t * P:(t + 1) * P, :], h2[:, t, :]).then_inc(yb_sent[t], 16)
            pool.wait_ge(slots_cleared, 32)
            pool.wait_ge(placed, 1)
            for n in range(2 * NT):
                pool.indirect_dma_start(out=slots_d, out_offset=bass.IndirectOffsetOnAxis(ap=slot_u[:, n:n + 1], axis=0),
                                        in_=rows_u[:, n, :], in_offset=None).then_inc(slots_written, 16)
            pool.wait_ge(slots_written, 16 * 2 * NT)
            pool.dma_start(table_u, slots_d.rearrange("(n p) c -> p n c", p=P)).then_inc(slots_loaded, 16)
            pool.wait_ge(slots_loaded, 16)
            pool.wait_ge(router_ps, 1)
            for i in range(2):
                nc.gpsimd.memset(xg[i], 0.0).then_inc(xg_clear, 1)
            pool.wait_ge(xg_clear, 2)
            pool.wait_ge(h2_stored, 32)
            for i in range(2):
                pool.wait_ge(yb_sent[i], 16)

            last_row, last_result = pool.to_reg(T - 1), pool.to_reg(2 * T - 1)

            def gather(j):
                pool.indirect_dma_start(out=xg[j], out_offset=None, in_=h2_d,
                                        in_offset=bass.IndirectOffsetOnAxis(ap=gather_u[j], axis=0),
                                        bounds_check=last_row, oob_is_err=False).then_inc(xg_loaded[j], 16)

            def scatter(j):
                pool.indirect_dma_start(out=y2_d, out_offset=bass.IndirectOffsetOnAxis(ap=scatter_u[j], axis=0),
                                        in_=yb[j], in_offset=None,
                                        bounds_check=last_result, oob_is_err=False).then_inc(yb_sent[j], 16)

            nc.gpsimd.tensor_copy(gather_u[0], table_u[:, 0:1, 0]).then_inc(tile_rows, 1)
            pool.wait_ge(tile_rows, 1)
            gather(0)

            def indices_ready(n):
                pool.wait_ge(tile_rows, n)
                nc.gpsimd.tensor_tensor(passed, passed, passed, ALU.mult).then_inc(tile_rows, 1)

            def pair_of_tiles(i, first):
                for j in range(2):
                    tile = i * 2 + (first + j)
                    pool.wait_ge(xgT_ps, tile * 4 + 4)
                    nc.gpsimd.tensor_copy(gather_u[1 - j], table_u[:, bass.ds(tile + 1, 1), 0]) \
                        .then_inc(tile_rows, 1)
                    indices_ready(tile * 4 + 2)
                    gather(1 - j)
                    pool.wait_ge(yb_sent[j], i * 16 + 16 * (first // 2 + 1))
                    pool.wait_ge(y_act, tile * 2 + 2)
                    pool.wait_ge(y_dve, tile * 2 + 2)
                    nc.gpsimd.tensor_copy(scatter_u[j], table_u[:, bass.ds(tile, 1), 1]).then_inc(tile_rows, 1)
                    indices_ready(tile * 4 + 4)
                    scatter(j)

            with pool.Fori(0, N_EXP // 2) as i:
                pair_of_tiles(i, 0)
            over = pool.value_load(ctrl_u[0:1, 0:1], min_val=0, max_val=7)
            with pool.If(over > 0):
                with pool.Fori(0, (TILES - OVER) // 2) as i:
                    pair_of_tiles(i, OVER)

        @block.tensor
        def _(pe):
            def chunk(n):
                pe.wait_ge(w_loaded[n % SLOTS], 16 * (n // SLOTS + 1))
                return ring[n % SLOTS]

            EMPTY = {
                "cq": [(hT_act, 6), (hT_dve, 6)], "misc": [(hT_act, 8), (hT_dve, 8)],
                "uq0": [(cq_norm, 4)], "uq1": [(rope_mul, 2), (v_copied, 2)],
                "qi0": [(rope_mul, 6)], "qi1": [(rope_mul, 10)], "qi2": [(rope_mul, 14)], "qi3": [(rope_mul, 18)],
                "ga0": [(rope_mul, 22)], "ga1": [(gate_exp, 4)], "ga2": [(gate_exp, 8)],
                "hq0": [(gate_exp, 12)], "hf0": [(att_masked, ATT_N), (att_sb, ATT_N)],
                "hi0": [(hq_ready, 1)], "ga3": [(hv_sb, 4)], "gb0": [(gate_exp, 16)],
                "hq1": [(gate_exp, 20)], "hf1": [(tree_masked, 32), (state_ready, 12), (rec_sb, 4)],
                "hi1": [(hq_ready, 2)], "gb1": [(hv_sb, 8)], "gb2": [(gate_exp, 24)], "gb3": [(gate_exp, 28)],
                "hg0": [(gate_exp, 32)], "hg1": [(rec_normed, 1)],
                "pa0": [(hg_ready, 4)], "pb0": [(hg_ready, 8)],
            }
            for b in range(1, 4):
                EMPTY[f"pa{b}"], EMPTY[f"pb{b}"] = [(merge_read, 8 * b - 4)], [(merge_read, 8 * b)]
            EMPTY["wo0"], EMPTY["wo1"] = [(merge_read, 28)], [(merge_read, 32)]
            EMPTY["wo2"], EMPTY["wo3"] = [(x1_ready, 4)], [(x1_ready, 8)]

            def by_feature(name, rhs, ready=None):
                start, chunks, bank = PANEL[name]
                for s, v in EMPTY[name]:
                    pe.wait_ge(s, v)
                for g in range(chunks):
                    w = chunk(start + g)
                    for s, v in (ready(g) if ready else []):
                        pe.wait_ge(s, v)
                    for kk in range(4):
                        k = 4 * g + kk
                        for f in range(4):
                            last = nc.tensor.matmul(banks[bank + f][:, :], lhsT=w[:, kk, f * P:(f + 1) * P],
                                                    rhs=rhs[:, k, :], start=k == 0, stop=k == 4 * chunks - 1)
                        if kk == 3:
                            last.then_inc(chunks_done, 1)
                        yield

            def by_token(name, lhs, ready=None):
                start, chunks, bank = PANEL[name]
                for s, v in EMPTY[name]:
                    pe.wait_ge(s, v)
                for g in range(chunks):
                    w = chunk(start + g)
                    for s, v in (ready(g) if ready else []):
                        pe.wait_ge(s, v)
                    for kk in range(4):
                        k = 4 * g + kk
                        for t in range(NT):
                            last = nc.tensor.matmul(banks[bank + t][:, :], lhsT=lhs[:, k, t * P:(t + 1) * P],
                                                    rhs=w[:, kk, :], start=k == 0, stop=k == 4 * chunks - 1)
                    last.then_inc(chunks_done, 1)

            def finish(work):
                for _ in work:
                    pass

            def some(work, n):
                for _ in range(n):
                    next(work, None)

            pe.wait_ge(small_loaded, 16 * 2)
            for k in range(KD):
                if k >= 8:
                    pe.wait_ge(hT_act if k % 2 else hT_dve, (k - 8) // 2 + 1)
                for t in range(NT):
                    if k == 0:
                        pe.wait_ge(h_ready, t + 1)
                    last = nc.tensor.transpose(banks[k % 8][:, t * P:(t + 1) * P], xt[:, t, k * P:(k + 1) * P], ident)
                last.then_inc(xT_ps, 1)

            finish(by_feature("cq", hT, lambda g: [(hT_act, min(8, 2 * g + 2)), (hT_dve, min(8, 2 * g + 2))]))

            start, _, _ = PANEL["misc"]
            for s, v in EMPTY["misc"]:
                pe.wait_ge(s, v)
            for g in range(4):
                chunk(start + g)
                base_w = RING + (start + g) % SLOTS * CHUNK
                w = mem[:, base_w:base_w + 4 * MISC].rearrange("p (k n) -> p k n", k=4)
                for kk in range(4):
                    k = 4 * g + kk
                    first, end = k == 0, k == KD - 1
                    nc.tensor.matmul(banks[4][:, :], lhsT=w[:, kk, 0:P], rhs=hT[:, k, :], start=first, stop=end)
                    nc.tensor.matmul(banks[5][:, :], lhsT=w[:, kk, 2 * P:3 * P], rhs=hT[:, k, :],
                                     start=first, stop=end)
                    for t in range(NT):
                        tok = hT[:, k, t * P:(t + 1) * P]
                        nc.tensor.matmul(banks[6][:, t * P:(t + 1) * P], lhsT=tok, rhs=w[:, kk, P:2 * P],
                                         start=first and t == 0, stop=end, skip_group_check=True)
                        last = nc.tensor.matmul(banks[7][:, t * 16:(t + 1) * 16], lhsT=tok,
                                                rhs=w[:, kk, 3 * P:3 * P + 16],
                                                start=first and t == 0, stop=end, skip_group_check=True)
                last.then_inc(chunks_done, 1)
                if g == 1:
                    pe.wait_ge(cq_squared, 4)
                    for f in range(4):
                        last = nc.tensor.matmul(banks[0][:, :], lhsT=ones, rhs=cq_sq[:, f, :],
                                                start=f == 0, stop=f == 3)
                    last.then_inc(ssq_ps, 1)

            for name in ("uq0", "uq1", "qi0", "qi1", "qi2", "qi3"):
                finish(by_feature(name, cqT))

            def gates(names):
                for name in names:
                    yield from by_feature(name, hT)

            filler = gates(ATT_GATES)
            m = 0

            def transpose_probs(m, t):
                pe.wait_ge(probs_ready, m + 1)
                if m >= 1:
                    pe.wait_ge(probsT_sb, m)
                for s in range(t + 1):
                    last = nc.tensor.transpose(banks[6][:, s * P:(s + 1) * P], probs[:, m % 2, s * P:(s + 1) * P],
                                               ident)
                last.then_inc(probsT_ps, 1)

            def values(m, t):
                pe.wait_ge(probsT_sb, m + 1)
                if m >= 1:
                    pe.wait_ge(att_sb, m)
                for s in range(t + 1):
                    last = nc.tensor.matmul(banks[7][:, 0:P], lhsT=vtok[:, s, :],
                                            rhs=probsT[:, m % 2, s * P:(s + 1) * P], start=s == 0, stop=s == t)
                last.then_inc(att_ps, 1)

            att_tile = [s[1] for s in STEPS if s[0] == "att"]
            pe.wait_ge(roped, 2 + A_HEADS + IDX_HEADS)
            pe.wait_ge(v_copied, 2)
            for n, (kind, t, h) in enumerate(STEPS):
                if n >= 2:
                    if STEPS[n - 2][0] == "idx":
                        pe.wait_ge(relu_done, step_count("idx", n - 1))
                    else:
                        pe.wait_ge(att_masked, step_count("att", n - 1))
                keys, q, kk = (t + 1) * P, (qiT if kind == "idx" else qT), (kiT if kind == "idx" else kT)
                nc.tensor.matmul(banks[4 + n % 2][:, 0:keys], lhsT=q[:, h, t * P:(t + 1) * P], rhs=kk[:, 0:keys],
                                 start=True, stop=True).then_inc(logits_ps, 1)
                some(filler, att_fill[n])
                if kind == "att":
                    if m >= 1:
                        transpose_probs(m - 1, att_tile[m - 1])
                    if m >= 2:
                        values(m - 2, att_tile[m - 2])
                    m += 1
            transpose_probs(m - 1, att_tile[m - 1])
            values(m - 2, att_tile[m - 2])
            values(m - 1, att_tile[m - 1])
            finish(filler)

            for b in range(2):
                finish(by_feature(f"hq{b}", hT))
                finish(by_feature(f"hf{b}", hT))
                by_token(f"hi{b}", hT)
                filler = gates(REC_GATES[b])
                pe.wait_ge(hf_exp, 4 * (b + 1))
                pe.wait_ge(hv_sb, 4 * (b + 1))

                def outputs(n):
                    f, c = n % 16 // 4, n % 4
                    pe.wait_ge(intra_ready, n + 1)
                    if c == 0 and n >= 4:
                        pe.wait_ge(rec_sb, n // 4)
                    last = nc.tensor.matmul(banks[7][:, c * P:(c + 1) * P], lhsT=hv[:, c, f * P:(f + 1) * P],
                                            rhs=intra[:, n % 2, :], start=True, stop=c == 0)
                    if c:
                        pe.wait_ge(state_ready, n // 4 * 3 + c)
                        last = nc.tensor.matmul(banks[7][:, c * P:(c + 1) * P], lhsT=state[:, c % 2, :],
                                                rhs=qk[n // 2 % 2][:, 8, n % 2 * P:(n % 2 + 1) * P],
                                                start=False, stop=True)
                    last.then_inc(rec_ps, 1)

                for i in range(16):
                    n = 16 * b + i
                    f, c = i // 4, i % 4
                    buf, tok = qk[n // 2 % 2], slice(n % 2 * P, (n % 2 + 1) * P)
                    pe.wait_ge(qk_ready, n // 2 + 1)
                    pe.wait_ge(hf_ready, b + 1)
                    if n >= 1:
                        pe.wait_ge(tree_masked, 2 * n)
                    for m in range(4):
                        last = nc.tensor.matmul(banks[4][:, m * P:(m + 1) * P], lhsT=buf[:, m, tok],
                                                rhs=buf[:, m, tok], start=True, stop=True)
                    last.then_inc(tree_ps, 1)
                    for m in range(4, LEVELS):
                        nc.tensor.matmul(banks[5][:, (m - 4) * P:(m - 3) * P], lhsT=buf[:, m, tok],
                                         rhs=buf[:, m, tok], start=True, stop=True)
                    nc.tensor.matmul(banks[5][:, 3 * P:4 * P], lhsT=hk[:, f, c * P:(c + 1) * P],
                                     rhs=hq[:, f, c * P:(c + 1) * P], start=True, stop=True).then_inc(tree_ps, 1)
                    if c < 3:
                        if n // 4 * 3 + c >= 1:
                            pe.wait_ge(state_ready, n // 4 * 3 + c)
                        nc.tensor.transpose(banks[6][:, 0:P], buf[:, 7, tok], ident).then_inc(keT_ps, 1)
                    if i >= 1:
                        outputs(n - 1)
                    some(filler, rec_fill[i])
                    if c < 3:
                        pe.wait_ge(keT_sb, n // 4 * 3 + c + 1)
                        nc.tensor.matmul(banks[6][:, 0:P], lhsT=keT[:, n % 2, :], rhs=hv[:, c, f * P:(f + 1) * P],
                                         start=True, stop=True).then_inc(state_ps, 1)
                outputs(16 * b + 15)
                finish(filler)

            finish(by_feature("gb3", hT))
            pe.wait_ge(rec_squared, G_HEADS)
            for h in range(G_HEADS):
                last = nc.tensor.matmul(banks[4][:, :], lhsT=ones, rhs=at(U + h * T, T), start=h == 0,
                                        stop=h == G_HEADS - 1)
            last.then_inc(recsq_ps, 1)
            finish(by_feature("hg0", hT))
            finish(by_feature("hg1", hT))

            for b in range(4):
                finish(by_feature(f"pa{b}", yattT))
                finish(by_feature(f"pb{b}", yrecT, (lambda g: [(hg_ready, 4 * g + 4)]) if b == 0 else None))
            for b in range(4):
                by_token(f"wo{b}", mT, (lambda g: [(merged_ready, 4 * g + 4)]) if b == 0 else None)

            for k in range(KD):
                if k >= 8:
                    pe.wait_ge(h2T_act if k % 2 else h2T_dve, (k - 8) // 2 + 1)
                for t in range(NT):
                    if k == 0:
                        pe.wait_ge(h2_ready, t + 1)
                    last = nc.tensor.transpose(banks[k % 8][:, t * P:(t + 1) * P], h2[:, t, k * P:(k + 1) * P], ident)
                last.then_inc(h2T_ps, 1)
            pe.wait_ge(h2T_act, 8)
            pe.wait_ge(h2T_dve, 8)
            pe.wait_ge(late_loaded, 16 * 5)
            for t in range(NT):
                for k in range(KD):
                    last = nc.tensor.matmul(banks[0][:, t * 64:t * 64 + 36], lhsT=h2T[:, k, t * P:(t + 1) * P],
                                            rhs=wr[:, k, :], start=k == 0, stop=k == KD - 1)
            last.then_inc(router_ps, 1)
            pe.wait_ge(picked, 1)
            for t in range(NT):
                for u in range(t + 1):
                    last = nc.tensor.matmul(banks[1][:, t * N_EXP:(t + 1) * N_EXP], lhsT=before if u == t else ones,
                                            rhs=both[:, u, :], start=u == 0, stop=u == t)
            for u in range(NT):
                last = nc.tensor.matmul(banks[1][:, NT * N_EXP:(NT + 1) * N_EXP], lhsT=ones, rhs=both[:, u, :],
                                        start=u == 0, stop=u == NT - 1)
            last.then_inc(rank_ps, 1)

            def transpose_rows(j, tile):
                for g in range(4):
                    if g >= 2:
                        pe.wait_ge(xgT_act if g % 2 == 0 else xgT_dve, tile * 2 + 1)
                    for kk in range(4):
                        k = 4 * g + kk
                        last = nc.tensor.transpose(banks[2 + g % 2][:, kk * P:(kk + 1) * P],
                                                   xg[j][:, k * P:(k + 1) * P], ident)
                    last.then_inc(xgT_ps, 1)

            def pair_of_tiles(i, first):
                for j in range(2):
                    tile = i * 2 + (first + j)
                    n0 = FRONT + 12 * j
                    due = [i * 48 + 16 * ((FRONT + 12 * (first + j) + c) // SLOTS + 1) for c in range(12)]
                    pe.wait_ge(xgT_act, tile * 2 + 2)
                    pe.wait_ge(xgT_dve, tile * 2 + 2)
                    for part in range(2):
                        for g in range(4):
                            c = 4 * part + g
                            s = (n0 + c) % SLOTS
                            pe.wait_ge(w_loaded[s], due[c])
                            for kk in range(4):
                                k = 4 * g + kk
                                last = nc.tensor.matmul(banks[part][:, :], lhsT=xgT[j][:, k, :], rhs=ring[s][:, kk, :],
                                                        start=k == 0, stop=k == KD - 1)
                            last.then_inc(chunks_done, 1)
                    pe.wait_ge(xg_loaded[1 - j], i * 16 + 16 * (first // 2 + 1 + j))
                    transpose_rows(1 - j, tile + 1)
                    pe.wait_ge(act_ready, tile + 1)
                    for f in range(4):
                        last = nc.tensor.transpose(banks[0][:, f * P:(f + 1) * P], act_h[:, f * P:(f + 1) * P], ident)
                    last.then_inc(actT_ps, 1)
                    pe.wait_ge(actT_sb, tile + 1)
                    for cb in range(4):
                        c = 8 + cb
                        s = (n0 + c) % SLOTS
                        pe.wait_ge(w_loaded[s], due[c])
                        for kk in range(4):
                            last = nc.tensor.matmul(banks[4 + cb][:, :], lhsT=actT[:, kk, :], rhs=ring[s][:, kk, :],
                                                    start=kk == 0, stop=kk == 3)
                        last.then_inc(chunks_done, 1)

            pe.wait_ge(xg_loaded[0], 16)
            transpose_rows(0, 0)
            with pe.Fori(0, N_EXP // 2) as i:
                pair_of_tiles(i, 0)
            over = pe.value_load(ctrl_u[0:1, 0:1], min_val=0, max_val=7)
            with pe.If(over > 0):
                with pe.Fori(0, (TILES - OVER) // 2) as i:
                    pair_of_tiles(i, OVER)

        @block.scalar
        def _(act):
            for t in range(NT):
                act.dma_start(xt[:, t, :], x[0, t * P:(t + 1) * P, :]).then_inc(x_loaded[t], 16)
            for t in range(NT):
                act.wait_ge(x_loaded[t], 16)
                nc.scalar.activation(junk[:, t, :], xt[:, t, :], ACT.Square, accum_out=ssum[:, t:t + 1]) \
                    .then_inc(squared, 1)
            act.wait_ge(mean_ready, 1)
            nc.scalar.activation(mean, mean, ACT.Sqrt).then_inc(rooted, 1)
            act.wait_ge(small_loaded, 16 * 2)
            for k in range(1, KD, 2):
                act.wait_ge(xT_ps, k + 1)
                nc.scalar.activation(hT[:, k, :], banks[k % 8][:, :], ACT.Copy, scale=g1c[:, k:k + 1]) \
                    .then_inc(hT_act, 1)
            act.wait_ge(lb_arg, 1)
            nc.scalar.activation(lb, lb, ACT.Exp).then_inc(lb_exp, 1)
            for f in range(4):
                act.wait_ge(cq_raw, f + 1)
                nc.scalar.activation(cq_sq[:, f, :], cqT[:, f, :], ACT.Square).then_inc(cq_squared, 1)
            act.wait_ge(mean_ready, 2)
            nc.scalar.activation(cq_rms, cq_rms, ACT.Sqrt).then_inc(rooted, 1)

            def gate_panel(name):
                start, chunks, bank = PANEL[name]
                n = GATE_NO[name]
                act.wait_ge(chunks_done, start + chunks)
                if n:
                    act.wait_ge(gate_stored, 16 * n)
                for f in range(4):
                    nc.scalar.activation(stage[:, f, :], banks[bank + f][:, :], ACT.Exp, scale=-1.0) \
                        .then_inc(gate_exp, 1)
                act.wait_ge(gate_exp, 4 * (n + 1))
                act.dma_start(gates_d[n // 4, n % 4], at(U + 15872, CHUNK)).then_inc(gate_stored, 16)

            ends = gate_ends(att_fill, ATT_GATES)
            i_n = m = 0

            def copy_probs(m, t):
                act.wait_ge(probsT_ps, m + 1)
                if m >= 2:
                    act.wait_ge(att_ps, m - 1)
                nc.scalar.activation(probsT[:, m % 2, 0:(t + 1) * P], banks[6][:, 0:(t + 1) * P], ACT.Copy) \
                    .then_inc(probsT_sb, 1)

            def copy_att(m, t, h):
                act.wait_ge(att_ps, m + 1)
                nc.scalar.activation(yattT[:, h, t * P:(t + 1) * P], banks[7][:, 0:P], ACT.Copy).then_inc(att_sb, 1)

            att = [s for s in STEPS if s[0] == "att"]
            for n, (kind, t, h) in enumerate(STEPS):
                keys = (t + 1) * P
                if kind == "idx":
                    act.wait_ge(logits_ps, n + 1)
                    if i_n >= 2:
                        act.wait_ge(scored, i_n - 1)
                    nc.scalar.activation(relu[:, i_n % 2, 0:keys], banks[4 + n % 2][:, 0:keys], ACT.Relu) \
                        .then_inc(relu_done, 1)
                    i_n += 1
                else:
                    act.wait_ge(nmax_ready, m + 1)
                    if m >= 2:
                        act.wait_ge(probsT_ps, m - 1)
                    nc.scalar.activation(probs[:, m % 2, 0:keys], masked[:, m % 2, 0:keys], ACT.Exp,
                                         bias=nmax[:, m:m + 1], scale=HEAD_D ** -0.5,
                                         accum_out=rsum[:, m:m + 1]).then_inc(exp_done, 1)
                    if m >= 1:
                        copy_probs(m - 1, att[m - 1][1])
                    if m >= 2:
                        copy_att(m - 2, att[m - 2][1], att[m - 2][2])
                    m += 1
                for name in ends.get(n, []):
                    gate_panel(name)
            copy_probs(m - 1, att[m - 1][1])
            copy_att(m - 2, att[m - 2][1], att[m - 2][2])
            copy_att(m - 1, att[m - 1][1], att[m - 1][2])
            for name in ends.get(None, []):
                gate_panel(name)

            def tree_exps(u):
                f, pair = u % 8 // 2, u % 2
                buf = qk[u % 2]
                act.wait_ge(tree_arg, u + 1)
                nc.scalar.activation(buf[:, 0:8, :], buf[:, 0:8, :], ACT.Exp)
                nc.scalar.activation(buf[:, 8, :], hc[:, f, pair * 256:pair * 256 + 256], ACT.Exp)
                ends_at = hc[:, f, pair * 256:pair * 256 + 256].rearrange("p (c t) -> p c t", c=2)[:, :, P - 1]
                nc.scalar.activation(decay[:, u % 2 * 2:u % 2 * 2 + 2], ends_at, ACT.Exp).then_inc(tree_exp, 1)

            for b in range(2):
                start, chunks, bank = PANEL[f"hq{b}"]
                act.wait_ge(chunks_done, start + chunks)
                for f in range(4):
                    nc.scalar.activation(hq[:, f, :], banks[bank + f][:, :], ACT.Exp, scale=-1.0).then_inc(hq_exp, 1)
                start, chunks, bank = PANEL[f"hf{b}"]
                act.wait_ge(chunks_done, start + chunks)
                for f in range(4):
                    nc.scalar.activation(hk[:, f, :], banks[bank + f][:, :], ACT.Exp, scale=-1.0).then_inc(hf_exp, 1)
                act.wait_ge(hf_ready, b + 1)
                nc.scalar.activation(hc, hc, ACT.Ln).then_inc(hf_ln, 1)
                start, chunks, bank = PANEL[f"hi{b}"]
                act.wait_ge(chunks_done, start + chunks)
                for t in range(NT):
                    nc.scalar.activation(hv[:, t, :], banks[bank + t][:, :], ACT.Copy).then_inc(hv_sb, 1)
                ends = gate_ends(rec_fill, REC_GATES[b])
                tree_exps(8 * b)

                def copy_rec(h):
                    act.wait_ge(rec_ps, 4 * h + 4)
                    nc.scalar.activation(yrecT[:, h, :], banks[7][:, :], ACT.Copy).then_inc(rec_sb, 1)

                for i in range(16):
                    n = 16 * b + i
                    if n % 4 < 3:
                        act.wait_ge(keT_ps, n // 4 * 3 + n % 4 + 1)
                        nc.scalar.activation(keT[:, n % 2, :], banks[6][:, 0:P], ACT.Copy).then_inc(keT_sb, 1)
                    if i % 4 == 0 and i:
                        copy_rec(n // 4 - 1)
                    if i % 2 == 0 and i < 14:
                        tree_exps(n // 2 + 1)
                    for name in ends.get(i, []):
                        gate_panel(name)
                copy_rec(4 * b + 3)
                for name in ends.get(None, []):
                    gate_panel(name)

            for h in range(G_HEADS):
                act.wait_ge(rec_sb, h + 1)
                nc.scalar.activation(at(U + h * T, T), yrecT[:, h, :], ACT.Square).then_inc(rec_squared, 1)
            gate_panel("gb3")
            act.wait_ge(mean_ready, 3)
            nc.scalar.activation(lev[:, 0:T], lev[:, 0:T], ACT.Sqrt).then_inc(rooted, 1)
            hg_tmp = [hc, hv]
            for b in range(2):
                start, chunks, bank = PANEL[f"hg{b}"]
                act.wait_ge(chunks_done, start + chunks)
                for f in range(4):
                    nc.scalar.activation(hg_tmp[b][:, f, :], banks[bank + f][:, :], ACT.Exp, scale=-1.0) \
                        .then_inc(hg_exp, 1)
            for t in range(NT):
                act.dma_start(x1[:, t, :], x[0, t * P:(t + 1) * P, :]).then_inc(x_loaded[t], 16)
            act.wait_ge(hg_ready, 8)
            act.dma_start(g2b, g_norm2[0].partition_broadcast(P)).then_inc(late_loaded, 16)
            act.dma_start(gfb, g_final.partition_broadcast(P)).then_inc(late_loaded, 16)
            act.wait_ge(gate_stored, 16 * 8)
            for b in range(4):
                if b:
                    act.wait_ge(merged_ready, 4 * b)
                act.dma_start(at(U + 8192, CHUNK), gates_d[0, b]).then_inc(gate_loaded, 16)
                act.dma_start(at(U + 10240, CHUNK), gates_d[1, b]).then_inc(gate_loaded, 16)
            act.wait_ge(merged_ready, 16)
            act.dma_start(wr[:, :, 0:N_GROUPS], w_grp[0].rearrange("(k p) n -> p k n", p=P)).then_inc(late_loaded, 16)
            act.dma_start(wr[:, :, N_GROUPS:36], w_exp[0].rearrange("(k p) n -> p k n", p=P)).then_inc(late_loaded, 16)
            act.dma_start(rowc[:, 36:36 + 4 * 32], t_route).then_inc(late_loaded, 16)
            act.dma_start(rowc[:, 0:N_GROUPS], b_grp[0].partition_broadcast(P)).then_inc(late_loaded, 16)
            act.dma_start(rowc[:, N_GROUPS:36], b_exp[0].partition_broadcast(P)).then_inc(late_loaded, 16)
            act.wait_ge(x1_ready, 16)
            for t in range(NT):
                nc.scalar.activation(h2[:, t, :], x1[:, t, :], ACT.Square, accum_out=ssum[:, t:t + 1]) \
                    .then_inc(squared, 1)
            act.wait_ge(mean_ready, 4)
            nc.scalar.activation(mean, mean, ACT.Sqrt).then_inc(rooted, 1)
            for t in range(NT):
                act.wait_ge(h2_ready, t + 1)
                if t >= 2:
                    act.dma_start(h2_d[t * P:(t + 1) * P, :], h2[:, t, :]).then_inc(h2_stored, 16)
            for k in range(1, KD, 2):
                act.wait_ge(h2T_ps, k + 1)
                nc.scalar.activation(h2T[:, k, :], banks[k % 8][:, :], ACT.Copy).then_inc(h2T_act, 1)
            act.wait_ge(route_arg, 1)
            for t in range(NT):
                nc.scalar.activation(gexp[:, t, :], lg[:, t, 0:4], ACT.Exp, bias=gneg[:, t:t + 1],
                                     accum_out=gsum[:, t:t + 1]).then_inc(route_exp, 1)
            act.wait_ge(route_arg, 2)
            nc.scalar.activation(diff, diff, ACT.Exp).then_inc(route_exp, 1)

            def transposed_rows(j, tile):
                for g in (0, 2):
                    act.wait_ge(xgT_ps, tile * 4 + (g + 1))
                    nc.scalar.activation(xgT[j][:, 4 * g:4 * g + 4, :],
                                         banks[2][:, :].rearrange("p (k n) -> p k n", k=4), ACT.Copy) \
                        .then_inc(xgT_act, 1)

            def pair_of_tiles(i, first):
                for j in range(2):
                    tile = i * 2 + (first + j)
                    used = i * 24 + (FRONT + 12 * (first + j))
                    act.wait_ge(chunks_done, used + 4)
                    nc.scalar.activation(act_e, banks[0][:, :], ACT.Exp, scale=-1.0).then_inc(silu_exp, 1)
                    transposed_rows(1 - j, tile + 1)
                    act.wait_ge(actT_ps, tile + 1)
                    nc.scalar.activation(actT, banks[0][:, :].rearrange("p (k n) -> p k n", k=4), ACT.Copy) \
                        .then_inc(actT_sb, 1)
                    act.wait_ge(yb_sent[j], i * 16 + 16 * (first // 2 + 1))
                    for cb in (0, 2):
                        act.wait_ge(chunks_done, used + (8 + cb + 1))
                        nc.scalar.activation(yb[j][:, cb * 512:(cb + 1) * 512], banks[4 + cb][:, :], ACT.Copy) \
                            .then_inc(y_act, 1)

            transposed_rows(0, 0)
            with act.Fori(0, N_EXP // 2) as i:
                pair_of_tiles(i, 0)
            over = act.value_load(ctrl_u[0:1, 0:1], min_val=0, max_val=7)
            with act.If(over > 0):
                with act.Fori(0, (TILES - OVER) // 2) as i:
                    pair_of_tiles(i, OVER)
            for t in range(NT):
                act.wait_ge(fin_args, t + 1)
                nc.scalar.activation(yfin[t][:, 0, :], x1[:, t, :], ACT.Square, accum_out=fsum[:, t:t + 1]) \
                    .then_inc(squared, 1)
                act.wait_ge(fin_mean, t + 1)
                nc.scalar.activation(fmean[:, t:t + 1], fmean[:, t:t + 1], ACT.Sqrt).then_inc(fin_act, 1)

        @block.vector
        def _(dve):
            V = nc.vector
            seq = [0]

            def then(ins):
                seq[0] += 1
                ins.then_inc(v_seq, 1)
                dve.wait_ge(v_seq, seq[0])

            def here(ins, s, n):
                ins.then_inc(s, 1)
                dve.wait_ge(s, n)

            dve.wait_ge(squared, 4)
            V.tensor_scalar(mean, ssum, 1.0 / D, EPS, ALU.mult, ALU.add).then_inc(mean_ready, 1)
            dve.wait_ge(rooted, 1)
            then(V.reciprocal(rinv, mean))
            for t in range(NT):
                V.tensor_scalar(xt[:, t, :], xt[:, t, :], rinv[:, t:t + 1], None, ALU.mult).then_inc(h_ready, 1)
            dve.wait_ge(small_loaded, 16 * 2)
            for k in range(0, KD, 2):
                dve.wait_ge(xT_ps, k + 1)
                V.tensor_scalar(hT[:, k, :], banks[k % 8][:, :], g1c[:, k:k + 1], None, ALU.mult).then_inc(hT_dve, 1)
            V.tensor_tensor(lb, lbx[:, 8:16], lbx[:, 0:8], ALU.subtract).then_inc(lb_arg, 1)
            dve.wait_ge(chunks_done, PANEL["cq"][1])
            for f in range(4):
                V.tensor_copy(cqT[:, f, :], banks[f][:, :]).then_inc(cq_raw, 1)
            dve.wait_ge(ssq_ps, 1)
            V.tensor_scalar(cq_rms, banks[0][:, :], 1.0 / Q_RANK, EPS, ALU.mult, ALU.add).then_inc(mean_ready, 1)
            dve.wait_ge(rooted, 2)
            then(V.reciprocal(cq_rms, cq_rms))
            for f in range(4):
                V.scalar_tensor_tensor(out=cqT[:, f, :], in0=cqT[:, f, :], scalar=gqc[:, f:f + 1], in1=cq_rms,
                                       op0=ALU.mult, op1=ALU.mult).then_inc(cq_norm, 1)

            dve.wait_ge(rope_loaded, 16)
            turned = [0]

            def rope(ps):
                n = turned[0]
                turned[0] += 1
                if n >= 2:
                    dve.wait_ge(roped, n - 1)
                V.tensor_tensor(rope_a[:, n % 2, :], ps[:, :], cos2, ALU.mult)
                V.tensor_tensor(rope_b[0:64, n % 2, :], ps[64:128, :], sin2[64:128, :], ALU.mult)
                V.tensor_tensor(rope_b[64:128, n % 2, :], ps[0:64, :], sin2[0:64, :], ALU.mult).then_inc(rope_mul, 1)

            dve.wait_ge(chunks_done, PANEL["misc"][0] + 4)
            rope(banks[4])
            rope(banks[5])
            V.tensor_copy(vtok, banks[6][:, :].rearrange("p (t n) -> p t n", t=NT)).then_inc(v_copied, 1)
            V.tensor_scalar(wi, banks[7][:, 0:64].rearrange("p (t n) -> p t n", t=NT),
                            IDX_HEADS ** -0.5 * IDX_D ** -0.5, None, ALU.mult).then_inc(v_copied, 1)
            for name in ("uq0", "uq1", "qi0", "qi1", "qi2", "qi3"):
                start, chunks, bank = PANEL[name]
                dve.wait_ge(chunks_done, start + chunks)
                for f in range(4):
                    rope(banks[bank + f])
            dve.wait_ge(roped, turned[0])
            dve.wait_ge(causal_loaded, 16)
            dve.wait_ge(v_copied, 2)

            i_n = m = 0

            def normalise(m, t):
                dve.wait_ge(exp_done, m + 1)
                then(V.reciprocal(rrec[:, m:m + 1], rsum[:, m:m + 1]))
                keys = (t + 1) * P
                V.tensor_scalar(probs[:, m % 2, 0:keys], probs[:, m % 2, 0:keys], rrec[:, m:m + 1], None,
                                ALU.mult).then_inc(probs_ready, 1)

            att = [s for s in STEPS if s[0] == "att"]
            for n, (kind, t, h) in enumerate(STEPS):
                keys = (t + 1) * P
                if kind == "idx":
                    dve.wait_ge(relu_done, i_n + 1)
                    acc = causal[:, T - keys:T] if h == 0 else score[:, 0:keys]
                    here(V.scalar_tensor_tensor(out=score[:, 0:keys], in0=relu[:, i_n % 2, 0:keys],
                                                scalar=wi[:, t, h:h + 1], in1=acc, op0=ALU.mult, op1=ALU.add),
                         scored, i_n + 1)
                    i_n += 1
                    if h == IDX_HEADS - 1:
                        for _ in range(TOPK // 8):
                            then(V.max(out=top8, in_=score[:, 0:keys]))
                            then(V.match_replace(out=score[:, 0:keys], in_to_replace=top8,
                                                 in_values=score[:, 0:keys], imm_value=TAKEN))
                        then(V.tensor_scalar(bias[:, t % 2, 0:keys], score[:, 0:keys], (FILL + TAKEN) / 2, OUT,
                                             ALU.is_gt, ALU.mult))
                else:
                    dve.wait_ge(logits_ps, n + 1)
                    b = causal[:, T - keys:T] if t == 0 else bias[:, t % 2, 0:keys]
                    here(V.tensor_tensor_reduce(out=masked[:, m % 2, 0:keys], in0=banks[4 + n % 2][:, 0:keys], in1=b,
                                                scale=1.0, scalar=FILL, op0=ALU.add, op1=ALU.max,
                                                accum_out=smax[:, m:m + 1]), att_masked, m + 1)
                    V.tensor_scalar(nmax[:, m:m + 1], smax[:, m:m + 1], -HEAD_D ** -0.5, None, ALU.mult) \
                        .then_inc(nmax_ready, 1)
                    if m >= 1:
                        normalise(m - 1, att[m - 1][1])
                    m += 1
            normalise(m - 1, att[m - 1][1])

            def tree_args(u):
                f, pair = u % 8 // 2, u % 2
                buf, tok = qk[u % 2], slice(pair * 256, pair * 256 + 256)
                if u >= 2:
                    dve.wait_ge(rec_ps, 2 * (u - 1))
                for m in range(LEVELS):
                    h = P >> (m + 1)
                    c = hc[:, f, tok].rearrange("p (b s h) -> p b s h", s=2, h=h)
                    o = buf[:, m, :].rearrange("p (b s h) -> p b s h", s=2, h=h)
                    mid = c[:, :, 0, h - 1:h].to_broadcast([P, 256 // (2 * h), h])
                    V.tensor_tensor(o[:, :, 1, :], c[:, :, 1, :], mid, ALU.subtract)
                    V.tensor_tensor(o[:, :, 0, :], mid, c[:, :, 0, :], ALU.subtract)
                c = hc[:, f, tok].rearrange("p (b t) -> p b t", t=P)
                V.tensor_tensor(buf[:, 7, :].rearrange("p (b t) -> p b t", t=P),
                                c[:, :, P - 1:P].to_broadcast([P, 2, P]), c, ALU.subtract).then_inc(tree_arg, 1)

            for b in range(2):
                dve.wait_ge(hq_exp, 4 * (b + 1))
                then(V.tensor_scalar(hq, hq, 1.0, None, ALU.add))
                then(V.reciprocal(hq, hq))
                bank = PANEL[f"hq{b}"][2]
                for f in range(4):
                    ins = V.tensor_tensor(hq[:, f, :], banks[bank + f][:, :], hq[:, f, :], ALU.mult)
                ins.then_inc(hq_ready, 1)
                dve.wait_ge(hf_exp, 4 * (b + 1))
                if b == 0:
                    dve.wait_ge(lb_exp, 1)
                    then(V.tensor_scalar(lb, lb, 1.0, None, ALU.add))
                    then(V.reciprocal(lb, lb))
                    then(V.tensor_scalar(one_lb, lb, -1.0, 1.0, ALU.mult, ALU.add))
                then(V.tensor_scalar(hk, hk, 1.0, None, ALU.add))
                then(V.reciprocal(hk, hk))
                for f in range(4):
                    h = 4 * b + f
                    ins = V.tensor_scalar(hc[:, f, :], hk[:, f, :], one_lb[:, h:h + 1], lb[:, h:h + 1],
                                          ALU.mult, ALU.add)
                then(ins)
                here(V.tensor_scalar(hk, hc, -1.0, 1.0, ALU.mult, ALU.add), hf_ready, b + 1)
                dve.wait_ge(hf_ln, b + 1)
                for f in range(4):
                    ins = V.tensor_tensor_scan(out=hc[:, f, :], data0=restart, data1=hc[:, f, :], initial=0.0,
                                               op0=ALU.mult, op1=ALU.add)
                then(ins)
                tree_args(8 * b)
                for i in range(16):
                    n = 16 * b + i
                    c = n % 4
                    for half in range(2):
                        dve.wait_ge(tree_ps, 2 * n + half + 1)
                        here(V.tensor_tensor(lev[:, half * 512:(half + 1) * 512], banks[4 + half][:, :],
                                             level_mask[:, half * 512:(half + 1) * 512], ALU.mult),
                             tree_masked, 2 * n + half + 1)
                    if n >= 2:
                        dve.wait_ge(rec_ps, n - 1)
                    here(V.tensor_reduce(intra[:, n % 2, :], lev.rearrange("p (m t) -> p t m", m=8), AX.X, ALU.add),
                         intra_ready, n + 1)
                    if i % 2 == 0 and i < 14:
                        tree_args(n // 2 + 1)
                    if c < 3:
                        dve.wait_ge(state_ps, n // 4 * 3 + c + 1)
                        if n:
                            dve.wait_ge(rec_ps, n)
                        if c == 0:
                            V.tensor_copy(state[:, 1, :], banks[6][:, 0:P]).then_inc(state_ready, 1)
                        else:
                            k = n // 2 % 2 * 2 + n % 2
                            V.scalar_tensor_tensor(out=state[:, (c + 1) % 2, :], in0=state[:, c % 2, :],
                                                   scalar=decay[:, k:k + 1], in1=banks[6][:, 0:P],
                                                   op0=ALU.mult, op1=ALU.add).then_inc(state_ready, 1)
            dve.wait_ge(recsq_ps, 1)
            then(V.tensor_scalar(lev[:, 0:T], banks[4][:, :], 1.0 / G_WIDTH, EPS, ALU.mult, ALU.add))
            here(V.tensor_copy(lev[:, T:T + 1], lev[:, 0:1]), mean_ready, 3)
            dve.wait_ge(rooted, 3)
            then(V.reciprocal(lev[:, 0:T], lev[:, 0:T]))
            for h in range(G_HEADS):
                ins = V.scalar_tensor_tensor(out=yrecT[:, h, :], in0=yrecT[:, h, :], scalar=ghc[:, h:h + 1],
                                             in1=lev[:, 0:T], op0=ALU.mult, op1=ALU.mult)
            here(ins, rec_normed, 1)
            hg_tmp = [hc, hv]
            for b in range(2):
                for f in range(4):
                    h = 4 * b + f
                    e = hg_tmp[b][:, f, :]
                    dve.wait_ge(hg_exp, h + 1)
                    then(V.tensor_scalar(e, e, 1.0, None, ALU.add))
                    then(V.reciprocal(e, e))
                    then(V.tensor_tensor(e, banks[PANEL[f"hg{b}"][2] + f][:, :], e, ALU.mult))
                    V.tensor_tensor(yrecT[:, h, :], yrecT[:, h, :], e, ALU.mult).then_inc(hg_ready, 1)

            for b in range(4):
                dve.wait_ge(gate_loaded, 32 * (b + 1))
                both_gates = at(U + 8192, 2 * CHUNK)
                then(V.tensor_scalar(both_gates, both_gates, 1.0, None, ALU.add))
                then(V.reciprocal(both_gates, both_gates))
                for k, (name, g) in enumerate((("pa", gate_a), ("pb", gate_b))):
                    start, chunks, bank = PANEL[f"{name}{b}"]
                    dve.wait_ge(chunks_done, start + chunks)
                    for f in range(4):
                        if k == 0:
                            V.tensor_tensor(mT[:, 4 * b + f, :], banks[bank + f][:, :], g[:, f, :], ALU.mult) \
                                .then_inc(merge_read, 1)
                        else:
                            here(V.tensor_tensor(g[:, f, :], banks[bank + f][:, :], g[:, f, :], ALU.mult),
                                 merge_read, 8 * b + 4 + f + 1)
                            V.tensor_tensor(mT[:, 4 * b + f, :], mT[:, 4 * b + f, :], g[:, f, :], ALU.add) \
                                .then_inc(merged_ready, 1)
            for t in range(NT):
                dve.wait_ge(x_loaded[t], 32)
            for b in range(4):
                start, chunks, bank = PANEL[f"wo{b}"]
                dve.wait_ge(chunks_done, start + chunks)
                for t in range(NT):
                    cols = x1[:, t, b * 512:(b + 1) * 512]
                    V.tensor_tensor(cols, banks[bank + t][:, :], cols, ALU.add).then_inc(x1_ready, 1)
            dve.wait_ge(squared, 8)
            V.tensor_scalar(mean, ssum, 1.0 / D, EPS, ALU.mult, ALU.add).then_inc(mean_ready, 1)
            dve.wait_ge(rooted, 4)
            then(V.reciprocal(rinv, mean))
            dve.wait_ge(late_loaded, 16 * 7)
            for t in range(NT):
                V.scalar_tensor_tensor(out=h2[:, t, :], in0=x1[:, t, :], scalar=rinv[:, t:t + 1], in1=g2b,
                                       op0=ALU.mult, op1=ALU.mult).then_inc(h2_ready, 1)
            for k in range(0, KD, 2):
                dve.wait_ge(h2T_ps, k + 1)
                V.tensor_copy(h2T[:, k, :], banks[k % 8][:, :]).then_inc(h2T_dve, 1)

            def over_tokens(v, n):
                return v.unsqueeze(1).to_broadcast([P, NT, n])

            iota32, e128 = rowc[:, 36:68], rowc[:, 68:100]
            step128 = rowc[:, 100:132]
            dve.wait_ge(router_ps, 1)
            logits = banks[0][:, 0:NT * 64].rearrange("p (t n) -> p t n", t=NT)
            then(V.memset(lg, FILL))
            V.tensor_tensor(lg[:, :, 0:4], logits[:, :, 0:4], over_tokens(rowc[:, 0:4], 4), ALU.add)
            then(V.tensor_tensor(le, logits[:, :, 4:36], over_tokens(rowc[:, 4:36], 32), ALU.add))
            for t in range(NT):
                ins = V.max(out=g8[:, t, :], in_=lg[:, t, :])
            then(ins)
            for t in range(NT):
                V.max_index(out=gi8[:, t, :], in_max=g8[:, t, :], in_values=lg[:, t, :])
            here(V.tensor_scalar(gneg, g8[:, :, 0], -1.0, None, ALU.mult), route_arg, 1)
            then(V.tensor_copy(gidx, gi8[:, :, 0]))
            then(V.tensor_tensor(gout, over_tokens(iota32[:, 0:4], 4), gidx.unsqueeze(2).to_broadcast([P, NT, 4]),
                                 ALU.not_equal))
            then(V.tensor_scalar(gout, gout, OUT, None, ALU.mult))
            then(V.tensor_tensor(le.rearrange("p t (g e) -> p t g e", g=4), le.rearrange("p t (g e) -> p t g e", g=4),
                                 gout.unsqueeze(3).to_broadcast([P, NT, 4, 8]), ALU.add))
            for t in range(NT):
                ins = V.max(out=e8[:, t, :], in_=le[:, t, :])
            then(ins)
            for t in range(NT):
                ins = V.max_index(out=ei8[:, t, :], in_max=e8[:, t, :], in_values=le[:, t, :])
            then(ins)
            here(V.tensor_tensor(diff, e8[:, :, 1], e8[:, :, 0], ALU.subtract), route_arg, 2)
            for c in range(2):
                then(V.tensor_copy(eidx[:, c, :], ei8[:, :, c]))
                then(V.tensor_tensor(pick[:, c], over_tokens(iota32, 32),
                                     eidx[:, c, :].unsqueeze(2).to_broadcast([P, NT, 32]), ALU.is_equal))
            here(V.tensor_tensor(both, pick[:, 0], pick[:, 1], ALU.add), picked, 1)
            dve.wait_ge(route_exp, 5)
            then(V.tensor_scalar(den, diff, 1.0, None, ALU.add))
            then(V.tensor_tensor(den, den, gsum, ALU.mult))
            then(V.reciprocal(gate1, den))
            then(V.tensor_tensor(gate2, gate1, diff, ALU.mult))
            dve.wait_ge(x1_ready, 16)
            V.tensor_copy(gate1k, gate1)
            V.tensor_copy(gate2k, gate2)
            dve.wait_ge(rank_ps, 1)
            V.tensor_copy(rank, banks[1][:, 0:NT * N_EXP].rearrange("p (t e) -> p t e", t=NT))
            then(V.tensor_copy(count, banks[1][:, NT * N_EXP:(NT + 1) * N_EXP]))
            then(V.tensor_scalar(extra, count, float(P), None, ALU.is_gt))
            then(V.scalar_tensor_tensor(out=extra, in0=count, scalar=2.0 * P, in1=extra, op0=ALU.is_gt, op1=ALU.add))
            then(V.scalar_tensor_tensor(out=extra, in0=count, scalar=3.0 * P, in1=extra, op0=ALU.is_gt, op1=ALU.add))
            then(V.memset(ones_e, 1.0))
            then(V.tensor_tensor_scan(out=upto, data0=ones_e, data1=extra, initial=0.0, op0=ALU.mult, op1=ALU.add))
            then(V.tensor_tensor(base, upto, extra, ALU.subtract))
            then(V.scalar_tensor_tensor(out=delta, in0=base, scalar=float(P), in1=step128, op0=ALU.mult, op1=ALU.add))
            then(V.scalar_tensor_tensor(out=pos, in0=rank, scalar=float(P), in1=over_tokens(delta, 32),
                                        op0=ALU.is_ge, op1=ALU.mult))
            then(V.tensor_tensor(pos, pos, rank, ALU.add))
            then(V.tensor_tensor(pos, pos, over_tokens(e128, 32), ALU.add))
            for c in range(2):
                then(V.tensor_tensor(posp, pos, pick[:, c], ALU.mult))
                then(V.tensor_reduce(slot[:, c, :], posp, AX.X, ALU.add))
            then(V.tensor_copy(slot_u.rearrange("p (c t) -> p c t", c=2), slot))
            V.tensor_copy(ctrl_f[:, 0:1], upto[:, N_EXP - 1:N_EXP])
            for k in range(TILES - OVER):
                then(V.tensor_scalar(posp[:, 0, :], upto, float(k), None, ALU.is_le))
                then(V.tensor_reduce(ctrl_f[:, 1 + k:2 + k], posp[:, 0, :], AX.X, ALU.add))
            then(V.tensor_scalar(ctrl_f[:, 1:9], ctrl_f[:, 1:9], float(N_EXP - 1), None, ALU.min))
            here(V.tensor_copy(ctrl_u[:, 0:9], ctrl_f[:, 0:9]), placed, 1)
            V.memset(top8, 0.0).then_inc(slots_ready, 1)

            def transposed_rows(j, tile):
                for g in (1, 3):
                    dve.wait_ge(xgT_ps, tile * 4 + (g + 1))
                    V.tensor_copy(xgT[j][:, 4 * g:4 * g + 4, :], banks[3][:, :].rearrange("p (k n) -> p k n", k=4)) \
                        .then_inc(xgT_dve, 1)

            def pair_of_tiles(i, first):
                for j in range(2):
                    tile = i * 2 + (first + j)
                    used = i * 24 + (FRONT + 12 * (first + j))

                    def next_step(ins, k):
                        ins.then_inc(silu_seq, 1)
                        dve.wait_ge(silu_seq, tile * 3 + k)

                    dve.wait_ge(silu_exp, tile + 1)
                    next_step(V.tensor_scalar(act_e, act_e, 1.0, None, ALU.add), 1)
                    next_step(V.reciprocal(act_e, act_e), 2)
                    next_step(V.tensor_tensor(act_e, banks[0][:, :], act_e, ALU.mult), 3)
                    dve.wait_ge(chunks_done, used + 8)
                    V.tensor_tensor(act_h, banks[1][:, :], act_e, ALU.mult).then_inc(act_ready, 1)
                    transposed_rows(1 - j, tile + 1)
                    dve.wait_ge(yb_sent[j], i * 16 + 16 * (first // 2 + 1))
                    for cb in (1, 3):
                        dve.wait_ge(chunks_done, used + (8 + cb + 1))
                        V.tensor_copy(yb[j][:, cb * 512:(cb + 1) * 512], banks[4 + cb][:, :]).then_inc(y_dve, 1)

            transposed_rows(0, 0)
            with dve.Fori(0, N_EXP // 2) as i:
                pair_of_tiles(i, 0)
            over = dve.value_load(ctrl_u[0:1, 0:1], min_val=0, max_val=7)
            with dve.If(over > 0):
                with dve.Fori(0, (TILES - OVER) // 2) as i:
                    pair_of_tiles(i, OVER)

            for t in range(NT):
                dve.wait_ge(yfin_loaded[t], 16)
                then(V.scalar_tensor_tensor(out=x1[:, t, :], in0=yfin[t][:, 0, :], scalar=gate1k[:, t:t + 1],
                                            in1=x1[:, t, :], op0=ALU.mult, op1=ALU.add))
                here(V.scalar_tensor_tensor(out=x1[:, t, :], in0=yfin[t][:, 1, :], scalar=gate2k[:, t:t + 1],
                                            in1=x1[:, t, :], op0=ALU.mult, op1=ALU.add), fin_args, t + 1)
                dve.wait_ge(squared, 9 + t)
                V.tensor_scalar(fmean[:, t:t + 1], fsum[:, t:t + 1], 1.0 / D, EPS, ALU.mult, ALU.add) \
                    .then_inc(fin_mean, 1)
                dve.wait_ge(fin_act, t + 1)
                then(V.reciprocal(fmean[:, t:t + 1], fmean[:, t:t + 1]))
                V.scalar_tensor_tensor(out=x1[:, t, :], in0=x1[:, t, :], scalar=fmean[:, t:t + 1], in1=gfb,
                                       op0=ALU.mult, op1=ALU.mult).then_inc(fin_dve, 1)


INPUTS = ["x", "w_in", "w_uq", "w_qidx", "w_pa", "w_pb", "w_o", "g_norm2", "w_grp", "b_grp", "w_exp", "b_exp", "w_gate", "w_up", "w_down", "g_final"]


def tables():
    f = np.float32
    i = np.arange(P)
    levels = []
    for m in range(LEVELS):
        h = P >> (m + 1)
        same = i[:, None] // (2 * h) == i[None, :] // (2 * h)
        levels.append(same & (i[:, None] % (2 * h) < h) & (i[None, :] % (2 * h) >= h))
    levels.append(i[:, None] == i[None, :])
    restart = np.broadcast_to((np.arange(T) % P != 0).astype(f), (P, T))
    const = np.concatenate([np.eye(P), np.ones((P, P)), i[:, None] < i[None, :], *levels, restart], 1).astype(f)
    inv = (1.0 / (f(10000.0) ** (np.arange(0, HEAD_D, 2, dtype=f) / f(HEAD_D)))).astype(f)
    ang = (np.arange(T, dtype=f)[None, :] * inv[:, None]).astype(f)
    cos, sin = np.cos(ang), np.sin(ang)
    rope = np.concatenate([np.concatenate([cos, cos], 0), np.concatenate([sin, -sin], 0)], 1).astype(f)
    causal = np.zeros((P, T), f)
    causal[:, T - P:][i[None, :] > i[:, None]] = FILL
    e = np.arange(N_EXP, dtype=f)
    route = np.concatenate([e, e * P, (OVER - 1 - e) * P, 0 * e])
    route = np.broadcast_to(route, (P, 4 * N_EXP)).astype(f)
    rows = np.zeros((P, 2, NT, 2), np.uint32)
    for c in range(2):
        for t in range(NT):
            rows[:, c, t, 0] = t * P + i
            rows[:, c, t, 1] = 2 * (t * P + i) + c
    return {"t_const": const, "t_rope": rope, "t_causal": causal, "t_route": np.ascontiguousarray(route),
            "t_rows": rows.reshape(P, -1)}


def layout(inputs):
    arrays = {n: np.ascontiguousarray(inputs[n]) for n in INPUTS}
    for n in ("w_in", "w_uq", "w_qidx", "w_pa", "w_pb", "w_o", "w_gate", "w_up", "w_down"):
        arrays[n] = arrays[n][0]
    columns = [np.asarray(inputs[n])[0] for n in ("g_norm1", "g_cq", "g_hnorm")] + list(np.asarray(inputs["lb_logits"]))
    arrays["gains"] = np.ascontiguousarray(np.concatenate([c.reshape(-1, P) for c in columns], 0).T)
    arrays.update(tables())
    return arrays


def kernel(**inputs):
    import concourse.bacc as bacc
    from concourse.bass_utils import run_bass_kernel_spmd

    arrays = layout(inputs)
    nc = bacc.Bacc("TRN2", target_bir_lowering=False, num_devices=1)
    args = {n: nc.dram_tensor(n, a.shape, mybir.dt.from_np(a.dtype), kind="ExternalInput").ap()
            for n, a in arrays.items()}
    out = nc.dram_tensor("out", (1, T, D), F32, kind="ExternalOutput").ap()
    build(nc, **args, out=out)
    r = run_bass_kernel_spmd(nc, [arrays], core_ids=[0])
    return r.results[0]["out"]
```

```python
import math
from contextlib import ExitStack

import numpy as np

import concourse.bass as bass
from concourse import mybir

F32 = mybir.dt.float32
F32R = mybir.dt.float32r
U32 = mybir.dt.uint32
ALU = mybir.AluOpType
ACT = mybir.ActivationFunctionType
AX = mybir.AxisListType

P = 128
D, T = 2048, 512
KD, NT = D // P, T // P
A_HEADS, HEAD_D = 8, 128
Q_RANK = 512
IDX_HEADS, IDX_D = 16, 128
TOPK = 128
G_HEADS = 8
N_GROUPS, PER_GROUP = 4, 8
N_EXP = N_GROUPS * PER_GROUP
D_EXP = 512
EPS = 1e-6
A_WIDTH = A_HEADS * HEAD_D
G_WIDTH = G_HEADS * 128
FILL = -3.0e38
TAKEN = -3.4e38
OUT = -1.0e30

C_CQ = 0
C_K = C_CQ + Q_RANK
C_HQ = C_K + 3 * 128 + IDX_HEADS
C_HF, C_HI, C_HG = C_HQ + G_WIDTH, C_HQ + 2 * G_WIDTH, C_HQ + 3 * G_WIDTH
C_GA = C_HQ + 4 * G_WIDTH
C_GB = C_GA + D
D_IN = C_GB + D
MISC = C_HQ - C_K

CK = 2
CHUNK = CK * 512
SLOTS = 4
SPLIT_SLOTS = 2
E_SLOTS = 12
E_SPLIT_SLOTS = 6
AHEAD = 5
E_CHUNKS = 2 * KD // CK + D_EXP // P // CK * (D // 512)
PANEL_GATE = 4 * 512
R = 64
TILES = N_EXP + 2 * T // R - 1
OVER = N_EXP
LEVELS = 7
NO_ROW = 60000

RING = 0
YATT = RING + SLOTS * CHUNK
YREC = YATT + A_HEADS * T
U = YREC + G_HEADS * T
TAB = U + 17920
SMALL = TAB + 3 * P + 8 * P + T
TOTAL = SMALL + 592
HIGH, LOW = 0, KD * T
W_PARTS = 2 * KD * T
TOTAL_PARTS = W_PARTS + 2 * SPLIT_SLOTS * CHUNK


def panels():
    order = [("cq", 4, 0), ("misc", 4, 4), ("uq0", 1, 0), ("uq1", 1, 4),
             ("qi0", 1, 0), ("qi1", 1, 4), ("qi2", 1, 0), ("qi3", 1, 4),
             ("ga0", 4, 0), ("ga1", 4, 0), ("ga2", 4, 0),
             ("hq0", 4, 0), ("hf0", 4, 4), ("hi0", 4, 0), ("ga3", 4, 0), ("gb0", 4, 0),
             ("hq1", 4, 0), ("hf1", 4, 4), ("hi1", 4, 0), ("gb1", 4, 0), ("gb2", 4, 0),
             ("gb3", 4, 0), ("hg0", 4, 0), ("hg1", 4, 4)]
    for b in range(4):
        order += [(f"pa{b}", 2, 0), (f"pb{b}", 2, 4)]
    order += [(f"wo{b}", 4, 4 * (b % 2)) for b in range(4)]
    found, start = {}, 0
    for name, chunks, bank in order:
        chunks *= 4 // CK
        found[name] = (start, chunks, bank)
        start += chunks
    return found, start


def split_chunks(panel):
    return [n for name, (start, chunks, _) in panel.items() if name[:2] not in ("uq", "qi", "pa", "pb")
            for n in range(start, start + chunks)]


def attention_steps():
    idx = lambda t: [("idx", t, h) for h in range(IDX_HEADS)]
    att = lambda t: [("att", t, h) for h in range(A_HEADS)]
    return idx(1) + att(0) + idx(2) + att(1) + idx(3) + att(2) + att(3)


def build(nc, x, gains, w_in, w_uq, w_qidx, w_pa, w_pb, w_o, g_norm2,
          w_grp, b_grp, w_exp, b_exp, w_gate, w_up, w_down, g_final, t_const, t_rope, t_causal,
          t_route, t_rows, out):
    PANEL, FRONT = panels()
    SPLIT = split_chunks(PANEL)
    SPLIT_NO = {n: m for m, n in enumerate(SPLIT)}
    STEPS = attention_steps()
    IDX_N = sum(s[0] == "idx" for s in STEPS)
    ATT_N = sum(s[0] == "att" for s in STEPS)

    gates_d = nc.dram_tensor("gates", (2, 4, P, PANEL_GATE), F32, kind="Internal").ap()
    h2_d = nc.dram_tensor("h2_rows", (T, D), F32, kind="Internal").ap()
    y2_d = nc.dram_tensor("expert_rows", (2 * T, D), F32, kind="Internal").ap()
    slots_d = nc.dram_tensor("slot_rows", ((TILES + 1) * R, 2), U32, kind="Internal").ap()

    ctx = ExitStack()
    with ctx:
        mem = ctx.enter_context(nc.sbuf_tensor("mem", [P, TOTAL], F32))
        parts = ctx.enter_context(nc.sbuf_tensor("parts", [P, TOTAL_PARTS], F32R))
        ctx.enter_context(nc.allow_non_contiguous_dma("columns of gains, and slot tables"))
        banks = [ctx.enter_context(nc.psum_tensor(f"bank{i}", [P, 512], F32)) for i in range(8)]

        def at(start, *shape):
            n = math.prod(shape)
            v = mem[:, start:start + n]
            if len(shape) == 2:
                v = v.rearrange("p (a b) -> p a b", a=shape[0])
            if len(shape) == 3:
                v = v.rearrange("p (a b c) -> p a b c", a=shape[0], b=shape[1])
            return v

        def sem(name):
            return ctx.enter_context(nc.semaphore(name))

        def part(start, k, n):
            return parts[:, start:start + k * n].rearrange("p (k n) -> p k n", k=k)

        ring = [at(RING + s * CHUNK, CK, 512) for s in range(SLOTS)]
        hT = [part(HIGH, KD, T), part(LOW, KD, T)]
        w_high = [W_PARTS + s * CHUNK for s in range(SPLIT_SLOTS)]
        w_low = [W_PARTS + (SPLIT_SLOTS + s) * CHUNK for s in range(SPLIT_SLOTS)]
        yattT = at(YATT, A_HEADS, T)
        yrecT = at(YREC, G_HEADS, T)
        ident, ones, before = at(TAB, P), at(TAB + P, P), at(TAB + 2 * P, P)
        level_mask, restart = at(TAB + 3 * P, 8 * P), at(TAB + 11 * P, T)
        cur = [SMALL]

        def small(n):
            cur[0] += n
            assert cur[0] <= TOTAL
            return mem[:, cur[0] - n:cur[0]]

        g1c, gqc, ghc, lbx = small(KD), small(Q_RANK // P), small(G_HEADS), small(2 * G_HEADS)
        lb, one_lb = small(G_HEADS), small(G_HEADS)
        ssum, mean, rinv = small(NT), small(NT), small(NT)
        wi = small(NT * IDX_HEADS).rearrange("p (t h) -> p t h", t=NT)
        smax, nmax, rsum, rrec = small(32), small(32), small(32), small(32)
        top8, decay = small(8), small(4)
        xt = at(U + 4096, NT, D)
        junk = at(YATT, NT, D)
        qT, qiT = at(U, A_HEADS, T), at(U + 4096, IDX_HEADS, T)
        cqT = at(U + 12288, 4, T)
        kT, kiT, vtok = at(U + 14336, T), at(U + 14848, T), at(U + 15360, NT, P)
        stage = at(U + 15872, 4, 512)
        cos2, sin2 = at(YATT, T), at(YATT + T, T)
        cq_sq, cq_rms = at(YATT + 2 * T, 4, T), at(YATT + 6 * T, T)
        rope_a, rope_b = at(YREC, 2, T), at(YREC + 2 * T, 2, T)
        relu, score = at(YREC, 2, T), at(YREC + 2 * T, T)
        masked, probs = at(YREC + 3 * T, 2, T), at(YREC + 5 * T, 2, T)
        causal = at(YREC + 7 * T, T)
        bias, probsT = at(U + 12288, 2, T), at(U + 13312, 2, T)
        hq, hk, hc, hv = (at(U + 2048 * i, 4, T) for i in range(4))
        QK = 9 * 256
        qk = [at(U + 8192 + QK * i, 9, 256) for i in range(2)]
        lev = at(U + 12800, 8 * P)
        intra, keT, state = (at(U + 13824 + 256 * i, 2, P) for i in range(3))
        mT = at(U, KD, T)
        gate_a, gate_b = at(U + 8192, 4, 512), at(U + 10240, 4, 512)
        g2b, gfb = at(U + 12288, D), at(U + 14336, D)
        x1 = at(YATT, NT, D)
        h2 = at(U, NT, D)
        h2T = at(U + 8192, 4, T)
        wr = at(U + 10240, KD, 36)
        rt = U + 10240 + KD * 36
        xg_all, act_all = at(U, D), at(U + 10752, 512)
        xg, yb = xg_all[0:R], at(U + 2 * D, D)[0:R]
        xgT = [part(0, KD, R), part(D, KD, R)]
        act_e, act_h = at(U + 10240, 512)[0:R], act_all[0:R]
        actT = [part(2 * D, 4, R), part(2 * D + 512, 4, R)]
        e_ring = [at(a, CK, 512) for a in [RING + s * CHUNK for s in range(SLOTS)] +
                  [U + a for a in (12288, 13312, 8192, 9216, 2048, 3072, 6144, 7168)]]
        e_parts = 2 * D + 1024
        e_high = [part(e_parts + 2 * s * CHUNK, CK, 512) for s in range(E_SPLIT_SLOTS)]
        e_low = [part(e_parts + (2 * s + 1) * CHUNK, CK, 512) for s in range(E_SPLIT_SLOTS)]
        assert e_parts + 2 * E_SPLIT_SLOTS * CHUNK <= TOTAL_PARTS
        yfin = [at(a, 2, D) for a in (RING, U, U + 2 * D, U + 4 * D)]

        w_loaded = [sem(f"w_loaded{s}") for s in range(SLOTS)]
        x_loaded = [sem(f"x_loaded{t}") for t in range(NT)]
        small_loaded, rope_loaded, causal_loaded = sem("small_loaded"), sem("rope_loaded"), sem("causal_loaded")
        gate_stored, gate_loaded, late_loaded = sem("gate_stored"), sem("gate_loaded"), sem("late_loaded")
        h2_stored, slots_cleared, slots_written = sem("h2_stored"), sem("slots_cleared"), sem("slots_written")
        slots_loaded, yb_sent, xg_loaded = sem("slots_loaded"), sem("yb_sent"), sem("xg_loaded")
        e_loaded = [sem(f"e_loaded{s}") for s in range(E_SLOTS)]
        yfin_loaded = [sem(f"yfin_loaded{i}") for i in range(4)]
        out_stored = sem("out_stored")
        chunks_done, xT_ps, ssq_ps = sem("chunks_done"), sem("xT_ps"), sem("ssq_ps")
        logits_ps, probsT_ps, att_ps = sem("logits_ps"), sem("probsT_ps"), sem("att_ps")
        tree_ps, keT_ps, state_ps, rec_ps = sem("tree_ps"), sem("keT_ps"), sem("state_ps"), sem("rec_ps")
        recsq_ps, h2T_ps, router_ps, rank_ps = sem("recsq_ps"), sem("h2T_ps"), sem("router_ps"), sem("rank_ps")
        xgT_ps, actT_ps, e_done = sem("xgT_ps"), sem("actT_ps"), sem("e_done")
        squared, rooted, hT_act, cq_squared = sem("squared"), sem("rooted"), sem("hT_act"), sem("cq_squared")
        relu_done, exp_done, probsT_sb, att_sb = sem("relu_done"), sem("exp_done"), sem("probsT_sb"), sem("att_sb")
        gate_sigmoid, hq_ready, hf_sigmoid, hf_ln, hv_sb = (sem("gate_sigmoid"), sem("hq_ready"), sem("hf_sigmoid"),
                                                        sem("hf_ln"), sem("hv_sb"))
        tree_exp, keT_sb, rec_sb, rec_squared = sem("tree_exp"), sem("keT_sb"), sem("rec_sb"), sem("rec_squared")
        hg_silu, h2T_act, route_exp = sem("hg_silu"), sem("h2T_act"), sem("route_exp")
        xgT_high, silu_done, actT_high, y_act = sem("xgT_high"), sem("silu_done"), sem("actT_high"), sem("y_act")
        fin_act, lb_exp = sem("fin_act"), sem("lb_exp")
        high_ready, merged_high, e_high_ready = sem("high_ready"), sem("merged_high"), sem("e_high_ready")
        v_seq = sem("v_seq")
        mean_ready, h_ready, hT_dve = sem("mean_ready"), sem("h_ready"), sem("hT_dve")
        cq_raw, cq_norm, v_copied, rope_mul = sem("cq_raw"), sem("cq_norm"), sem("v_copied"), sem("rope_mul")
        scored, att_masked, nmax_ready, probs_ready = (sem("scored"), sem("att_masked"), sem("nmax_ready"),
                                                       sem("probs_ready"))
        hf_ready, tree_arg = sem("hf_ready"), sem("tree_arg")
        tree_masked, intra_ready, state_ready = sem("tree_masked"), sem("intra_ready"), sem("state_ready")
        rec_normed, hg_ready, merge_read, merged_ready = (sem("rec_normed"), sem("hg_ready"), sem("merge_read"),
                                                          sem("merged_ready"))
        x1_ready, h2_ready, h2T_dve = sem("x1_ready"), sem("h2_ready"), sem("h2T_dve")
        route_arg, picked, placed, slots_ready = sem("route_arg"), sem("picked"), sem("placed"), sem("slots_ready")
        xgT_low, act_ready, y_dve, fin_dve = sem("xgT_low"), sem("act_ready"), sem("y_dve"), sem("fin_dve")
        actT_low = sem("actT_low")
        fin_args, fin_mean, lb_arg = sem("fin_args"), sem("fin_mean"), sem("lb_arg")
        low_ready, merged_sum, e_low_ready = sem("low_ready"), sem("merged_sum"), sem("e_low_ready")
        roped, qk_ready, xg_clear = sem("roped"), sem("qk_ready"), sem("xg_clear")
        slots_filled, tile_rows = sem("slots_filled"), sem("tile_rows")

        cur = [rt]

        def route(*shape):
            n = math.prod(shape)
            cur[0] += n
            return at(cur[0] - n, *shape)

        rowc = route(36 + 4 * 32)
        lg, le = route(NT, 8), route(NT, N_EXP)
        g8, gi8 = route(NT, 8), route(NT, 8).bitcast(U32)
        gneg, gsum, gexp, gidx = route(NT), route(NT), route(NT, 4), route(NT)
        gout = route(NT, 4)
        e8, ei8 = route(NT, 8), route(NT, 8).bitcast(U32)
        eidx = route(2, NT)
        diff, den, gate1, gate2 = route(NT), route(NT), route(NT), route(NT)
        pick = route(2, NT, N_EXP)
        both = route(NT, N_EXP)
        rank, count = route(NT, N_EXP), route(N_EXP)
        extra, upto, base, delta = route(N_EXP), route(N_EXP), route(N_EXP), route(N_EXP)
        pos, posp = route(NT, N_EXP), route(NT, N_EXP)
        slot = route(2, NT)
        assert cur[0] <= U + 12288
        cur = [U + 16384]
        slot_u = route(2 * NT).bitcast(U32)
        rows_u = route(2 * NT, 2).bitcast(U32)
        fill_u = route((TILES + 1) * R // P * 2).bitcast(U32)
        assert (TILES + 1) * R % P == 0
        table_u = route(TILES + 1, 2).bitcast(U32)
        gather_u, scatter_u = route(1).bitcast(U32), route(1).bitcast(U32)
        ctrl_f, ctrl_u = route(16), route(16).bitcast(U32)
        ones_e, passed = route(N_EXP), route(1)
        gate1k, gate2k = route(NT), route(NT)
        fsum, fmean = route(NT), route(NT)
        assert cur[0] <= TAB

        block = ctx.enter_context(nc.Block())

        def step_count(kind, n):
            return sum(s[0] == kind for s in STEPS[:n])

        att_fill = [0] * len(STEPS)
        for n, (kind, t, h) in enumerate(STEPS):
            att_fill[n] = int(h % 4 == 3) if kind == "idx" else (4 if h < 2 else h % 2) if t < 3 else \
                int(h in (2, 4, 6))
        rec_fill = [2] * 16

        def gate_ends(fill, names):
            total = [sum(fill[:n + 1]) for n in range(len(fill))]
            ends = {}
            for j, name in enumerate(names):
                at_step = next((n for n, k in enumerate(total) if k >= 16 * (j + 1)), None)
                ends.setdefault(at_step, []).append(name)
            return ends

        ATT_GATES, REC_GATES = ["ga0", "ga1", "ga2"], [["ga3", "gb0"], ["gb1", "gb2"]]
        def filled(fill, first, n):
            return PANEL[first][0] + min(sum(fill[:n]), 16 * (2 if fill is rec_fill else 3)) // CK

        def next_splits(done):
            taken = sum(n < done for n in SPLIT)
            return sum(n < done + SLOTS for n in SPLIT[:taken + SPLIT_SLOTS])

        GATE_NO = {n: i for i, n in enumerate(["ga0", "ga1", "ga2", "ga3", "gb0", "gb1", "gb2", "gb3"])}

        @block.sync
        def _(sp):
            def load(n, width, src):
                if n - SLOTS in SPLIT_NO:
                    sp.wait_ge(low_ready, SPLIT_NO[n - SLOTS] + 1)
                elif n >= SLOTS:
                    sp.wait_ge(chunks_done, n - SLOTS + 1)
                dst = at(RING + n % SLOTS * CHUNK, CK, width)
                sp.dma_start(dst, src.rearrange("(k p) n -> p k n", p=P)).then_inc(w_loaded[n % SLOTS], 16)

            col = {"cq": (w_in, C_CQ, 512), "misc": (w_in, C_K, MISC)}
            for b in range(4):
                if b < 2:
                    col[f"uq{b}"] = (w_uq, 512 * b, 512)
                    for name, c0 in (("hq", C_HQ), ("hf", C_HF), ("hi", C_HI), ("hg", C_HG)):
                        col[f"{name}{b}"] = (w_in, c0 + 512 * b, 512)
                col[f"qi{b}"] = (w_qidx, 512 * b, 512)
                col[f"ga{b}"], col[f"gb{b}"] = (w_in, C_GA + 512 * b, 512), (w_in, C_GB + 512 * b, 512)
                col[f"pa{b}"], col[f"pb{b}"] = (w_pa, 512 * b, 512), (w_pb, 512 * b, 512)
                col[f"wo{b}"] = (w_o, 512 * b, 512)
            for name, (start, chunks, _) in PANEL.items():
                w, c0, width = col[name]
                for g in range(chunks):
                    load(start + g, width, w[g * CK * P:(g + 1) * CK * P, c0:c0 + width])

            def expert_weights(tile, expert):
                for c in range(E_CHUNKS):
                    s = c % E_SLOTS
                    if isinstance(tile, int) and tile == 0 and c < E_SLOTS:
                        for r, v in ROOM[c]:
                            sp.wait_ge(r, v)
                    else:
                        sp.wait_ge(e_low_ready, tile * E_CHUNKS + (c - E_SLOTS + 1))
                    if c < 16:
                        w = w_gate if c < 8 else w_up
                        src = w[bass.ds(expert, 1), c % 8 * CK * P:(c % 8 + 1) * CK * P, :]
                    else:
                        cb, half = (c - 16) // 2, c % 2
                        src = w_down[bass.ds(expert, 1), half * CK * P:(half + 1) * CK * P, cb * 512:(cb + 1) * 512]
                    sp.dma_start(e_ring[s], src.rearrange("e (k p) n -> p (e k) n", p=P)).then_inc(e_loaded[s], 16)

            ROOM = [[(low_ready, len(SPLIT))]] * 4 + [[(h2_ready, 4)]] * 2 + [[(router_ps, KD)]] * 2 + \
                [[(h2_stored, 48), (h2T_ps, KD)]] * 4
            expert_weights(0, 0)
            with sp.Fori(1, N_EXP) as tile:
                expert_weights(tile, tile)
            sp.wait_ge(slots_ready, 1)
            over = sp.value_load(ctrl_u[0:1, 0:1], min_val=0, max_val=TILES - OVER)
            with sp.If(over > 0):
                with sp.Fori(0, TILES - OVER) as i:
                    e = sp.value_load(ctrl_u[0:1, bass.ds(i + 1, 1)], min_val=0, max_val=N_EXP - 1)
                    expert_weights(i + OVER, e)
                sp.wait_ge(yb_sent, 16 * (1 + TILES))
                sp.wait_ge(xg_loaded, 16 * (1 + TILES))
            sp.wait_ge(yb_sent, 16 * (1 + N_EXP))
            sp.wait_ge(xg_loaded, 16 * (1 + N_EXP))
            for t in range(NT):
                sp.dma_start(yfin[t], y2_d[2 * P * t:2 * P * (t + 1), :].rearrange("(p c) d -> p c d", c=2)) \
                    .then_inc(yfin_loaded[t], 16)
            for t in range(NT):
                sp.wait_ge(fin_dve, t + 1)
                sp.dma_start(out[0, t * P:(t + 1) * P, :], x1[:, t, :]).then_inc(out_stored, 16)
            sp.wait_ge(out_stored, 16 * NT)

        @block.gpsimd
        def _(pool):
            pool.dma_start(mem[:, TAB:SMALL], t_const).then_inc(small_loaded, 16)
            pool.dma_start(mem[:, SMALL:SMALL + KD + 4 + 3 * G_HEADS], gains).then_inc(small_loaded, 16)
            pool.wait_ge(squared, 4)
            pool.dma_start(at(YATT, 2 * T), t_rope).then_inc(rope_loaded, 16)
            pool.dma_start(causal, t_causal).then_inc(causal_loaded, 16)

            outs = [kT, kiT] + [qT[:, h, :] for h in range(A_HEADS)] + [qiT[:, h, :] for h in range(IDX_HEADS)]
            for n, o in enumerate(outs):
                pool.wait_ge(rope_mul, n + 1)
                nc.gpsimd.tensor_tensor(o, rope_a[:, n % 2, :], rope_b[:, n % 2, :], ALU.add).then_inc(roped, 1)

            for n in range(16):
                b, f, pair = n // 8, n % 8 // 2, n % 2
                buf, tok = qk[n % 2], slice(pair * 256, pair * 256 + 256)
                pool.wait_ge(tree_exp, n + 1)
                for m in range(LEVELS):
                    h = P >> (m + 1)
                    v = buf[:, m, :].rearrange("p (b s h) -> p b s h", s=2, h=h)
                    q4 = hq[:, f, tok].rearrange("p (b s h) -> p b s h", s=2, h=h)
                    k4 = hk[:, f, tok].rearrange("p (b s h) -> p b s h", s=2, h=h)
                    nc.gpsimd.tensor_tensor(v[:, :, 1, :], v[:, :, 1, :], q4[:, :, 1, :], ALU.mult)
                    nc.gpsimd.tensor_tensor(v[:, :, 0, :], v[:, :, 0, :], k4[:, :, 0, :], ALU.mult)
                nc.gpsimd.tensor_tensor(buf[:, 7, :], buf[:, 7, :], hk[:, f, tok], ALU.mult)
                nc.gpsimd.tensor_tensor(buf[:, 8, :], buf[:, 8, :], hq[:, f, tok], ALU.mult).then_inc(qk_ready, 1)

            pool.wait_ge(x1_ready, 16)
            nc.gpsimd.memset(passed, 0.0)
            nc.gpsimd.memset(fill_u, NO_ROW).then_inc(slots_filled, 1)
            pool.wait_ge(slots_filled, 1)
            pool.dma_start(slots_d.rearrange("(p n) c -> p (n c)", p=P), fill_u).then_inc(slots_cleared, 16)
            pool.dma_start(rows_u, t_rows.rearrange("p (n c) -> p n c", c=2)).then_inc(slots_cleared, 16)
            pool.wait_ge(h2_ready, 3)
            pool.dma_start(h2_d[2 * P:3 * P, :], h2[:, 2, :]).then_inc(yb_sent, 16)
            pool.wait_ge(slots_cleared, 32)
            pool.wait_ge(placed, 1)
            for n in range(2 * NT):
                pool.indirect_dma_start(out=slots_d, out_offset=bass.IndirectOffsetOnAxis(ap=slot_u[:, n:n + 1], axis=0),
                                        in_=rows_u[:, n, :], in_offset=None).then_inc(slots_written, 16)
            pool.wait_ge(slots_written, 16 * 2 * NT)
            pool.dma_start(table_u[0:R], slots_d.rearrange("(n p) c -> p n c", p=R)).then_inc(slots_loaded, 16)
            pool.wait_ge(slots_loaded, 16)
            pool.wait_ge(h2T_ps, KD)
            pool.wait_ge(h2_stored, 48)
            pool.wait_ge(yb_sent, 16)
            nc.gpsimd.memset(xg, 0.0).then_inc(xg_clear, 1)
            pool.wait_ge(xg_clear, 1)

            last_row, last_result = pool.to_reg(T - 1), pool.to_reg(2 * T - 1)

            def gather():
                pool.indirect_dma_start(out=xg, out_offset=None, in_=h2_d,
                                        in_offset=bass.IndirectOffsetOnAxis(ap=gather_u[0:R], axis=0),
                                        bounds_check=last_row, oob_is_err=False).then_inc(xg_loaded, 16)

            nc.gpsimd.tensor_copy(gather_u[0:R], table_u[0:R, 0:1, 0]).then_inc(tile_rows, 1)
            pool.wait_ge(tile_rows, 1)
            gather()

            def indices_ready(n):
                pool.wait_ge(tile_rows, n)
                nc.gpsimd.tensor_tensor(passed, passed, passed, ALU.mult).then_inc(tile_rows, 1)

            def send_tile(tile):
                pool.wait_ge(xgT_ps, tile * 2 + 2)
                nc.gpsimd.tensor_copy(gather_u[0:R], table_u[0:R, bass.ds(tile + 1, 1), 0]).then_inc(tile_rows, 1)
                indices_ready(tile * 4 + 2)
                gather()
                pool.wait_ge(yb_sent, tile * 16 + 16)
                pool.wait_ge(y_act, tile * 2 + 2)
                pool.wait_ge(y_dve, tile * 2 + 2)
                nc.gpsimd.tensor_copy(scatter_u[0:R], table_u[0:R, bass.ds(tile, 1), 1]).then_inc(tile_rows, 1)
                indices_ready(tile * 4 + 4)
                pool.indirect_dma_start(out=y2_d, out_offset=bass.IndirectOffsetOnAxis(ap=scatter_u[0:R], axis=0),
                                        in_=yb, in_offset=None,
                                        bounds_check=last_result, oob_is_err=False).then_inc(yb_sent, 16)

            with pool.Fori(0, N_EXP) as tile:
                send_tile(tile)
            over = pool.value_load(ctrl_u[0:1, 0:1], min_val=0, max_val=TILES - OVER)
            with pool.If(over > 0):
                with pool.Fori(0, TILES - OVER) as i:
                    send_tile(i + OVER)

        @block.tensor
        def _(pe):
            def chunk(n):
                if n not in SPLIT_NO:
                    pe.wait_ge(w_loaded[n % SLOTS], 16 * (n // SLOTS + 1))
                    return [ring[n % SLOTS]]
                m = SPLIT_NO[n]
                pe.wait_ge(low_ready, m + 1)
                return [part(w_high[m % SPLIT_SLOTS], CK, 512), part(w_low[m % SPLIT_SLOTS], CK, 512)]

            def pairs(w, x):
                return [(w[0], x[0]), (w[0], x[1]), (w[1], x[0])] if len(w) == 2 else [(w[0], x[0])]

            EMPTY = {
                "cq": [(hT_dve, 12)], "misc": [(hT_dve, 16)],
                "uq0": [(cq_norm, 4)], "uq1": [(rope_mul, 2), (v_copied, 2)],
                "qi0": [(rope_mul, 6)], "qi1": [(rope_mul, 10)], "qi2": [(rope_mul, 14)], "qi3": [(rope_mul, 18)],
                "ga0": [(rope_mul, 22)], "ga1": [(gate_sigmoid, 4)], "ga2": [(gate_sigmoid, 8)],
                "hq0": [(gate_sigmoid, 12)], "hf0": [(att_masked, ATT_N), (att_sb, ATT_N)],
                "hi0": [(hq_ready, 4)], "ga3": [(hv_sb, 4)], "gb0": [(gate_sigmoid, 16)],
                "hq1": [(gate_sigmoid, 20)], "hf1": [(tree_masked, 32), (state_ready, 12), (rec_sb, 4)],
                "hi1": [(hq_ready, 8)], "gb1": [(hv_sb, 8)], "gb2": [(gate_sigmoid, 24)], "gb3": [(gate_sigmoid, 28)],
                "hg0": [(gate_sigmoid, 32)], "hg1": [(rec_normed, 1)],
                "pa0": [(hg_silu, 4)], "pb0": [(hg_silu, 8)],
            }
            for b in range(1, 4):
                EMPTY[f"pa{b}"], EMPTY[f"pb{b}"] = [(merge_read, 8 * b - 4)], [(merge_read, 8 * b)]
            EMPTY["wo0"], EMPTY["wo1"] = [(merge_read, 28)], [(merge_read, 32)]
            EMPTY["wo2"], EMPTY["wo3"] = [(x1_ready, 4)], [(x1_ready, 8)]

            def by_feature(name, rhs, ready=None):
                start, chunks, bank = PANEL[name]
                for s, v in EMPTY[name]:
                    pe.wait_ge(s, v)
                for g in range(chunks):
                    w = chunk(start + g)
                    for s, v in (ready(g) if ready else []):
                        pe.wait_ge(s, v)
                    for kk in range(CK):
                        k = CK * g + kk
                        for f in range(4):
                            products = pairs(w, rhs)
                            for i, (ww, xx) in enumerate(products):
                                last = nc.tensor.matmul(banks[bank + f][:, :], lhsT=ww[:, kk, f * P:(f + 1) * P],
                                                        rhs=xx[:, k, :], start=k == 0 and i == 0,
                                                        stop=k == CK * chunks - 1 and i == len(products) - 1)
                        if kk == CK - 1:
                            last.then_inc(chunks_done, 1)
                        yield

            def by_token(name, lhs, ready=None):
                start, chunks, bank = PANEL[name]
                for s, v in EMPTY[name]:
                    pe.wait_ge(s, v)
                for g in range(chunks):
                    w = chunk(start + g)
                    for s, v in (ready(g) if ready else []):
                        pe.wait_ge(s, v)
                    for kk in range(CK):
                        k = CK * g + kk
                        for t in range(NT):
                            products = pairs(w, lhs)
                            for i, (ww, xx) in enumerate(products):
                                last = nc.tensor.matmul(banks[bank + t][:, :], lhsT=xx[:, k, t * P:(t + 1) * P],
                                                        rhs=ww[:, kk, :], start=k == 0 and i == 0,
                                                        stop=k == CK * chunks - 1 and i == len(products) - 1)
                    last.then_inc(chunks_done, 1)

            def finish(work):
                for _ in work:
                    pass

            def some(work, n):
                for _ in range(n):
                    next(work, None)

            pe.wait_ge(small_loaded, 16 * 2)
            for k in range(KD):
                if k >= 8:
                    pe.wait_ge(hT_dve, k - 7)
                for t in range(NT):
                    if k == 0:
                        pe.wait_ge(h_ready, t + 1)
                    last = nc.tensor.transpose(banks[k % 8][:, t * P:(t + 1) * P], xt[:, t, k * P:(k + 1) * P], ident)
                last.then_inc(xT_ps, 1)

            finish(by_feature("cq", hT, lambda g: [(hT_dve, CK * g + CK)]))

            start, _, _ = PANEL["misc"]
            for s, v in EMPTY["misc"]:
                pe.wait_ge(s, v)
            for g in range(KD // CK):
                chunk(start + g)
                slot = SPLIT_NO[start + g] % SPLIT_SLOTS
                w = [part(w_high[slot], CK, MISC), part(w_low[slot], CK, MISC)]
                for kk in range(CK):
                    k = CK * g + kk
                    for i, (ww, xx) in enumerate(pairs(w, hT)):
                        first, end = k == 0 and i == 0, k == KD - 1 and i == 2
                        nc.tensor.matmul(banks[4][:, :], lhsT=ww[:, kk, 0:P], rhs=xx[:, k, :], start=first, stop=end)
                        nc.tensor.matmul(banks[5][:, :], lhsT=ww[:, kk, 2 * P:3 * P], rhs=xx[:, k, :],
                                         start=first, stop=end)
                        for t in range(NT):
                            tok = xx[:, k, t * P:(t + 1) * P]
                            nc.tensor.matmul(banks[6][:, t * P:(t + 1) * P], lhsT=tok, rhs=ww[:, kk, P:2 * P],
                                             start=first and t == 0, stop=end, skip_group_check=True)
                            last = nc.tensor.matmul(banks[7][:, t * 16:(t + 1) * 16], lhsT=tok,
                                                    rhs=ww[:, kk, 3 * P:3 * P + 16],
                                                    start=first and t == 0, stop=end, skip_group_check=True)
                last.then_inc(chunks_done, 1)
                if g == 3:
                    pe.wait_ge(cq_squared, 4)
                    for f in range(4):
                        last = nc.tensor.matmul(banks[0][:, :], lhsT=ones, rhs=cq_sq[:, f, :],
                                                start=f == 0, stop=f == 3)
                    last.then_inc(ssq_ps, 1)

            for name in ("uq0", "uq1", "qi0", "qi1", "qi2", "qi3"):
                finish(by_feature(name, [cqT]))

            def gates(names):
                for name in names:
                    yield from by_feature(name, hT)

            filler = gates(ATT_GATES)
            m = 0

            def transpose_probs(m, t):
                pe.wait_ge(probs_ready, m + 1)
                if m >= 1:
                    pe.wait_ge(probsT_sb, m)
                for s in range(t + 1):
                    last = nc.tensor.transpose(banks[6][:, s * P:(s + 1) * P], probs[:, m % 2, s * P:(s + 1) * P],
                                               ident)
                last.then_inc(probsT_ps, 1)

            def values(m, t):
                pe.wait_ge(probsT_sb, m + 1)
                if m >= 1:
                    pe.wait_ge(att_sb, m)
                for s in range(t + 1):
                    last = nc.tensor.matmul(banks[7][:, 0:P], lhsT=vtok[:, s, :],
                                            rhs=probsT[:, m % 2, s * P:(s + 1) * P], start=s == 0, stop=s == t)
                last.then_inc(att_ps, 1)

            att_tile = [s[1] for s in STEPS if s[0] == "att"]
            pe.wait_ge(roped, 2 + A_HEADS + IDX_HEADS)
            pe.wait_ge(v_copied, 2)
            for n, (kind, t, h) in enumerate(STEPS):
                if n >= 2:
                    if STEPS[n - 2][0] == "idx":
                        pe.wait_ge(relu_done, step_count("idx", n - 1))
                    else:
                        pe.wait_ge(att_masked, step_count("att", n - 1))
                keys, q, kk = (t + 1) * P, (qiT if kind == "idx" else qT), (kiT if kind == "idx" else kT)
                nc.tensor.matmul(banks[4 + n % 2][:, 0:keys], lhsT=q[:, h, t * P:(t + 1) * P], rhs=kk[:, 0:keys],
                                 start=True, stop=True).then_inc(logits_ps, 1)
                some(filler, att_fill[n])
                if kind == "att":
                    if m >= 1:
                        transpose_probs(m - 1, att_tile[m - 1])
                    if m >= 2:
                        values(m - 2, att_tile[m - 2])
                    m += 1
            transpose_probs(m - 1, att_tile[m - 1])
            values(m - 2, att_tile[m - 2])
            values(m - 1, att_tile[m - 1])
            finish(filler)

            for b in range(2):
                finish(by_feature(f"hq{b}", hT))
                finish(by_feature(f"hf{b}", hT))
                by_token(f"hi{b}", hT)
                filler = gates(REC_GATES[b])
                pe.wait_ge(hf_sigmoid, 4 * (b + 1))
                pe.wait_ge(hv_sb, 4 * (b + 1))

                def outputs(n):
                    f, c = n % 16 // 4, n % 4
                    pe.wait_ge(intra_ready, n + 1)
                    if c == 0 and n >= 4:
                        pe.wait_ge(rec_sb, n // 4)
                    last = nc.tensor.matmul(banks[7][:, c * P:(c + 1) * P], lhsT=hv[:, c, f * P:(f + 1) * P],
                                            rhs=intra[:, n % 2, :], start=True, stop=c == 0)
                    if c:
                        pe.wait_ge(state_ready, n // 4 * 3 + c)
                        last = nc.tensor.matmul(banks[7][:, c * P:(c + 1) * P], lhsT=state[:, c % 2, :],
                                                rhs=qk[n // 2 % 2][:, 8, n % 2 * P:(n % 2 + 1) * P],
                                                start=False, stop=True)
                    last.then_inc(rec_ps, 1)

                for i in range(16):
                    n = 16 * b + i
                    f, c = i // 4, i % 4
                    buf, tok = qk[n // 2 % 2], slice(n % 2 * P, (n % 2 + 1) * P)
                    pe.wait_ge(qk_ready, n // 2 + 1)
                    pe.wait_ge(hf_ready, b + 1)
                    if n >= 1:
                        pe.wait_ge(tree_masked, 2 * n)
                    for m in range(4):
                        last = nc.tensor.matmul(banks[4][:, m * P:(m + 1) * P], lhsT=buf[:, m, tok],
                                                rhs=buf[:, m, tok], start=True, stop=True)
                    last.then_inc(tree_ps, 1)
                    for m in range(4, LEVELS):
                        nc.tensor.matmul(banks[5][:, (m - 4) * P:(m - 3) * P], lhsT=buf[:, m, tok],
                                         rhs=buf[:, m, tok], start=True, stop=True)
                    nc.tensor.matmul(banks[5][:, 3 * P:4 * P], lhsT=hk[:, f, c * P:(c + 1) * P],
                                     rhs=hq[:, f, c * P:(c + 1) * P], start=True, stop=True).then_inc(tree_ps, 1)
                    if c < 3:
                        if n // 4 * 3 + c >= 1:
                            pe.wait_ge(state_ready, n // 4 * 3 + c)
                        nc.tensor.transpose(banks[6][:, 0:P], buf[:, 7, tok], ident).then_inc(keT_ps, 1)
                    if i >= 1:
                        outputs(n - 1)
                    some(filler, rec_fill[i])
                    if c < 3:
                        pe.wait_ge(keT_sb, n // 4 * 3 + c + 1)
                        nc.tensor.matmul(banks[6][:, 0:P], lhsT=keT[:, n % 2, :], rhs=hv[:, c, f * P:(f + 1) * P],
                                         start=True, stop=True).then_inc(state_ps, 1)
                outputs(16 * b + 15)
                finish(filler)

            finish(by_feature("gb3", hT))
            pe.wait_ge(rec_squared, G_HEADS)
            for h in range(G_HEADS):
                last = nc.tensor.matmul(banks[4][:, :], lhsT=ones, rhs=at(U + h * T, T), start=h == 0,
                                        stop=h == G_HEADS - 1)
            last.then_inc(recsq_ps, 1)
            finish(by_feature("hg0", hT))
            finish(by_feature("hg1", hT))

            for b in range(4):
                finish(by_feature(f"pa{b}", [yattT]))
                finish(by_feature(f"pb{b}", [yrecT], (lambda g: [(hg_ready, CK * g + CK)]) if b == 0 else None))
            for b in range(4):
                by_token(f"wo{b}", hT, (lambda g: [(merged_ready, CK * g + CK)]) if b == 0 else None)

            def router(k):
                pe.wait_ge(h2T_act if k % 2 else h2T_dve, k // 2 + 1)
                for t in range(NT):
                    last = nc.tensor.matmul(banks[4 + t][:, 0:36], lhsT=h2T[:, k % 4, t * P:(t + 1) * P],
                                            rhs=wr[:, k, :], start=k == 0, stop=k == KD - 1)
                last.then_inc(router_ps, 1)

            pe.wait_ge(late_loaded, 16 * 5)
            pe.wait_ge(x1_ready, 16)
            for k in range(KD):
                if k >= 4:
                    pe.wait_ge(h2T_act if k % 2 else h2T_dve, (k - 4) // 2 + 1)
                for t in range(NT):
                    if k == 0:
                        pe.wait_ge(h2_ready, t + 1)
                    last = nc.tensor.transpose(banks[k % 4][:, t * P:(t + 1) * P], h2[:, t, k * P:(k + 1) * P], ident)
                last.then_inc(h2T_ps, 1)
                if k >= 2:
                    router(k - 2)
            router(KD - 2)
            router(KD - 1)
            pe.wait_ge(picked, 1)
            for t in range(NT):
                for u in range(t + 1):
                    last = nc.tensor.matmul(banks[1][:, t * N_EXP:(t + 1) * N_EXP], lhsT=before if u == t else ones,
                                            rhs=both[:, u, :], start=u == 0, stop=u == t)
            for u in range(NT):
                last = nc.tensor.matmul(banks[1][:, NT * N_EXP:(NT + 1) * N_EXP], lhsT=ones, rhs=both[:, u, :],
                                        start=u == 0, stop=u == NT - 1)
            last.then_inc(rank_ps, 1)

            def transpose_r(bank, i, rows):
                n = P if i == 0 else R
                return nc.tensor.transpose(bank[:, i * R:i * R + n], rows[0:n], ident[0:n, 0:n])

            def transpose_rows(tile, g):
                for kk in range(8):
                    k = 8 * g + kk
                    last = transpose_r(banks[2 + g], kk, xg_all[:, k * P:(k + 1) * P])
                last.then_inc(xgT_ps, 1)

            def products(bank, x, k, slot, kk, ks):
                both = pairs([e_high[slot], e_low[slot]], x)
                for i, (ww, xx) in enumerate(both):
                    last = nc.tensor.matmul(banks[bank][0:R, :], lhsT=xx[:, k, :], rhs=ww[:, kk, :],
                                            start=k == 0 and i == 0, stop=k == ks - 1 and i == len(both) - 1)
                return last

            def expert_tile(tile):
                for c in range(16):
                    pe.wait_ge(e_low_ready, tile * E_CHUNKS + (c + 1))
                    if c in (0, 4):
                        pe.wait_ge(xgT_low, tile * 2 + (c // 4 + 1))
                    for kk in range(CK):
                        last = products(c // 8, xgT, CK * (c % 8) + kk, c % E_SPLIT_SLOTS, kk, KD)
                    last.then_inc(e_done, 1)
                pe.wait_ge(xg_loaded, tile * 16 + 32)
                transpose_rows(tile + 1, 0)
                pe.wait_ge(act_ready, tile + 1)
                for f in range(4):
                    last = transpose_r(banks[0], f, act_all[:, f * P:(f + 1) * P])
                last.then_inc(actT_ps, 1)
                transpose_rows(tile + 1, 1)
                pe.wait_ge(actT_low, tile + 1)
                for c in range(16, E_CHUNKS):
                    pe.wait_ge(e_low_ready, tile * E_CHUNKS + (c + 1))
                    for kk in range(CK):
                        last = products(4 + (c - 16) // 2, actT, CK * (c % 2) + kk, c % E_SPLIT_SLOTS, kk, 4)
                    last.then_inc(e_done, 1)

            pe.wait_ge(xg_loaded, 16)
            for g in range(2):
                transpose_rows(0, g)
            with pe.Fori(0, N_EXP) as tile:
                expert_tile(tile)
            over = pe.value_load(ctrl_u[0:1, 0:1], min_val=0, max_val=TILES - OVER)
            with pe.If(over > 0):
                with pe.Fori(0, TILES - OVER) as i:
                    expert_tile(i + OVER)

        @block.scalar
        def _(act):
            halves = [0]

            def split_before(done):
                for m in range(halves[0], next_splits(done)):
                    n = SPLIT[m]
                    width = CK * (MISC if PANEL["misc"][0] <= n < PANEL["uq0"][0] else 512)
                    act.wait_ge(w_loaded[n % SLOTS], 16 * (n // SLOTS + 1))
                    if m >= SPLIT_SLOTS:
                        act.wait_ge(chunks_done, SPLIT[m - SPLIT_SLOTS] + 1)
                    nc.scalar.activation(parts[:, w_high[m % SPLIT_SLOTS]:w_high[m % SPLIT_SLOTS] + width],
                                         at(RING + n % SLOTS * CHUNK, width), ACT.Copy).then_inc(high_ready, 1)
                    halves[0] = m + 1

            for t in range(NT):
                act.dma_start(xt[:, t, :], x[0, t * P:(t + 1) * P, :]).then_inc(x_loaded[t], 16)
            for t in range(NT):
                act.wait_ge(x_loaded[t], 16)
                nc.scalar.activation(junk[:, t, :], xt[:, t, :], ACT.Square, accum_out=ssum[:, t:t + 1]) \
                    .then_inc(squared, 1)
            act.wait_ge(mean_ready, 1)
            nc.scalar.activation(mean, mean, ACT.Sqrt).then_inc(rooted, 1)
            split_before(0)
            act.wait_ge(small_loaded, 16 * 2)
            for k in range(KD):
                act.wait_ge(xT_ps, k + 1)
                nc.scalar.activation(hT[0][:, k, :], banks[k % 8][:, :], ACT.Copy, scale=g1c[:, k:k + 1]) \
                    .then_inc(hT_act, 1)
            for done in range(1, PANEL["cq"][1] + 1):
                split_before(done)
            act.wait_ge(lb_arg, 1)
            nc.scalar.activation(lb, lb, ACT.Exp).then_inc(lb_exp, 1)
            for f in range(4):
                act.wait_ge(cq_raw, f + 1)
                nc.scalar.activation(cq_sq[:, f, :], cqT[:, f, :], ACT.Square).then_inc(cq_squared, 1)
            split_before(PANEL["misc"][0] + 4)
            act.wait_ge(mean_ready, 2)
            nc.scalar.activation(cq_rms, cq_rms, ACT.Sqrt).then_inc(rooted, 1)

            def gate_panel(name):
                start, chunks, bank = PANEL[name]
                n = GATE_NO[name]
                split_before(start + chunks)
                act.wait_ge(chunks_done, start + chunks)
                if n:
                    act.wait_ge(gate_stored, 16 * n)
                for f in range(4):
                    nc.scalar.activation(stage[:, f, :], banks[bank + f][:, :], ACT.Sigmoid).then_inc(gate_sigmoid, 1)
                act.wait_ge(gate_sigmoid, 4 * (n + 1))
                act.dma_start(gates_d[n // 4, n % 4], at(U + 15872, PANEL_GATE)).then_inc(gate_stored, 16)

            ends = gate_ends(att_fill, ATT_GATES)
            i_n = m = 0

            def copy_probs(m, t):
                act.wait_ge(probsT_ps, m + 1)
                if m >= 2:
                    act.wait_ge(att_ps, m - 1)
                nc.scalar.activation(probsT[:, m % 2, 0:(t + 1) * P], banks[6][:, 0:(t + 1) * P], ACT.Copy) \
                    .then_inc(probsT_sb, 1)

            def copy_att(m, t, h):
                act.wait_ge(att_ps, m + 1)
                nc.scalar.activation(yattT[:, h, t * P:(t + 1) * P], banks[7][:, 0:P], ACT.Copy).then_inc(att_sb, 1)

            att = [s for s in STEPS if s[0] == "att"]
            for n, (kind, t, h) in enumerate(STEPS):
                keys = (t + 1) * P
                split_before(filled(att_fill, "ga0", n))
                if kind == "idx":
                    act.wait_ge(logits_ps, n + 1)
                    if i_n >= 2:
                        act.wait_ge(scored, i_n - 1)
                    nc.scalar.activation(relu[:, i_n % 2, 0:keys], banks[4 + n % 2][:, 0:keys], ACT.Relu) \
                        .then_inc(relu_done, 1)
                    i_n += 1
                else:
                    if h == 0 and t < 3:
                        for k in range(1, 3):
                            split_before(filled(att_fill, "ga0", n + k))
                    act.wait_ge(nmax_ready, m + 1)
                    if m >= 2:
                        act.wait_ge(probsT_ps, m - 1)
                    nc.scalar.activation(probs[:, m % 2, 0:keys], masked[:, m % 2, 0:keys], ACT.Exp,
                                         bias=nmax[:, m:m + 1], scale=HEAD_D ** -0.5,
                                         accum_out=rsum[:, m:m + 1]).then_inc(exp_done, 1)
                    split_before(filled(att_fill, "ga0", n + 1))
                    if m >= 1:
                        copy_probs(m - 1, att[m - 1][1])
                    if m >= 2:
                        copy_att(m - 2, att[m - 2][1], att[m - 2][2])
                    m += 1
                for name in ends.get(n, []):
                    gate_panel(name)
            copy_probs(m - 1, att[m - 1][1])
            copy_att(m - 2, att[m - 2][1], att[m - 2][2])
            copy_att(m - 1, att[m - 1][1], att[m - 1][2])
            for name in ends.get(None, []):
                gate_panel(name)

            def tree_exps(u):
                f, pair = u % 8 // 2, u % 2
                buf = qk[u % 2]
                act.wait_ge(tree_arg, u + 1)
                nc.scalar.activation(buf[:, 0:8, :], buf[:, 0:8, :], ACT.Exp)
                nc.scalar.activation(buf[:, 8, :], hc[:, f, pair * 256:pair * 256 + 256], ACT.Exp)
                ends_at = hc[:, f, pair * 256:pair * 256 + 256].rearrange("p (c t) -> p c t", c=2)[:, :, P - 1]
                nc.scalar.activation(decay[:, u % 2 * 2:u % 2 * 2 + 2], ends_at, ACT.Exp).then_inc(tree_exp, 1)

            for b in range(2):
                start, chunks, bank = PANEL[f"hq{b}"]
                split_before(start + chunks)
                act.wait_ge(chunks_done, start + chunks)
                for f in range(4):
                    nc.scalar.activation(hq[:, f, :], banks[bank + f][:, :], ACT.Silu).then_inc(hq_ready, 1)
                start, chunks, bank = PANEL[f"hf{b}"]
                split_before(start + chunks)
                act.wait_ge(chunks_done, start + chunks)
                for f in range(4):
                    nc.scalar.activation(hk[:, f, :], banks[bank + f][:, :], ACT.Sigmoid).then_inc(hf_sigmoid, 1)
                for done in range(3):
                    split_before(PANEL[f"hi{b}"][0] + done)
                act.wait_ge(hf_ready, b + 1)
                nc.scalar.activation(hc, hc, ACT.Ln).then_inc(hf_ln, 1)
                start, chunks, bank = PANEL[f"hi{b}"]
                split_before(start + chunks)
                act.wait_ge(chunks_done, start + chunks)
                for t in range(NT):
                    nc.scalar.activation(hv[:, t, :], banks[bank + t][:, :], ACT.Copy).then_inc(hv_sb, 1)
                ends = gate_ends(rec_fill, REC_GATES[b])
                tree_exps(8 * b)

                def copy_rec(h):
                    act.wait_ge(rec_ps, 4 * h + 4)
                    nc.scalar.activation(yrecT[:, h, :], banks[7][:, :], ACT.Copy).then_inc(rec_sb, 1)

                for i in range(16):
                    n = 16 * b + i
                    split_before(filled(rec_fill, REC_GATES[b][0], i))
                    if n % 4 < 3:
                        act.wait_ge(keT_ps, n // 4 * 3 + n % 4 + 1)
                        nc.scalar.activation(keT[:, n % 2, :], banks[6][:, 0:P], ACT.Copy).then_inc(keT_sb, 1)
                    if i % 4 == 0 and i:
                        copy_rec(n // 4 - 1)
                    if i % 2 == 0 and i < 14:
                        tree_exps(n // 2 + 1)
                    for name in ends.get(i, []):
                        gate_panel(name)
                copy_rec(4 * b + 3)
                for name in ends.get(None, []):
                    gate_panel(name)

            for h in range(G_HEADS):
                act.wait_ge(rec_sb, h + 1)
                nc.scalar.activation(at(U + h * T, T), yrecT[:, h, :], ACT.Square).then_inc(rec_squared, 1)
            gate_panel("gb3")
            split_before(PANEL["hg0"][0])
            act.wait_ge(mean_ready, 3)
            nc.scalar.activation(lev[:, 0:T], lev[:, 0:T], ACT.Sqrt).then_inc(rooted, 1)
            hg_tmp = [hc, hv]
            for b in range(2):
                start, chunks, bank = PANEL[f"hg{b}"]
                split_before(start + chunks)
                act.wait_ge(chunks_done, start + chunks)
                for f in range(4):
                    nc.scalar.activation(hg_tmp[b][:, f, :], banks[bank + f][:, :], ACT.Silu).then_inc(hg_silu, 1)
            act.wait_ge(hg_ready, 8)
            act.dma_start(g2b, g_norm2[0].partition_broadcast(P)).then_inc(late_loaded, 16)
            act.wait_ge(gate_stored, 16 * 8)
            act.dma_start(gfb, g_final.partition_broadcast(P)).then_inc(late_loaded, 16)
            for b in range(4):
                if b:
                    act.wait_ge(merged_sum, 4 * b)
                act.dma_start(at(U + 8192, PANEL_GATE), gates_d[0, b]).then_inc(gate_loaded, 16)
                act.dma_start(at(U + 10240, PANEL_GATE), gates_d[1, b]).then_inc(gate_loaded, 16)
                if b == 3:
                    split_before(PANEL["wo0"][0])
                for f in range(4):
                    k = 4 * b + f
                    act.wait_ge(merged_sum, k + 1)
                    nc.scalar.activation(hT[0][:, k, :], mT[:, k, :], ACT.Copy).then_inc(merged_high, 1)
            act.wait_ge(chunks_done, PANEL["wo0"][0])
            for t in range(NT):
                act.dma_start(x1[:, t, :], x[0, t * P:(t + 1) * P, :]).then_inc(x_loaded[t], 16)
            act.wait_ge(merged_sum, 16)
            act.dma_start(wr[:, :, 0:N_GROUPS], w_grp[0].rearrange("(k p) n -> p k n", p=P)).then_inc(late_loaded, 16)
            act.dma_start(wr[:, :, N_GROUPS:36], w_exp[0].rearrange("(k p) n -> p k n", p=P)).then_inc(late_loaded, 16)
            act.dma_start(rowc[:, 36:36 + 4 * 32], t_route).then_inc(late_loaded, 16)
            act.dma_start(rowc[:, 0:N_GROUPS], b_grp[0].partition_broadcast(P)).then_inc(late_loaded, 16)
            act.dma_start(rowc[:, N_GROUPS:36], b_exp[0].partition_broadcast(P)).then_inc(late_loaded, 16)
            for done in range(PANEL["wo0"][0], FRONT + 1):
                split_before(done)
            act.wait_ge(x1_ready, 16)
            for t in range(NT):
                nc.scalar.activation(h2[:, t, :], x1[:, t, :], ACT.Square, accum_out=ssum[:, t:t + 1]) \
                    .then_inc(squared, 1)
            act.wait_ge(mean_ready, 4)
            nc.scalar.activation(mean, mean, ACT.Sqrt).then_inc(rooted, 1)
            for t in range(NT):
                act.wait_ge(h2_ready, t + 1)
                if t != 2:
                    act.dma_start(h2_d[t * P:(t + 1) * P, :], h2[:, t, :]).then_inc(h2_stored, 16)
            for k in range(1, KD, 2):
                act.wait_ge(h2T_ps, k + 1)
                if k >= 4:
                    act.wait_ge(router_ps, k - 3)
                nc.scalar.activation(h2T[:, k % 4, :], banks[k % 4][:, :], ACT.Copy).then_inc(h2T_act, 1)
            act.wait_ge(route_arg, 1)
            for t in range(NT):
                nc.scalar.activation(gexp[:, t, :], lg[:, t, 0:4], ACT.Exp, bias=gneg[:, t:t + 1],
                                     accum_out=gsum[:, t:t + 1]).then_inc(route_exp, 1)
            act.wait_ge(route_arg, 2)
            nc.scalar.activation(diff, diff, ACT.Exp).then_inc(route_exp, 1)

            def transposed_rows(tile, g):
                act.wait_ge(xgT_ps, tile * 2 + (g + 1))
                nc.scalar.activation(xgT[0][:, 8 * g:8 * g + 8, :],
                                     banks[2 + g][:, :].rearrange("p (k n) -> p k n", k=8), ACT.Copy) \
                    .then_inc(xgT_high, 1)

            def split_chunks_of(tile, first, end, last=False):
                for c in range(first, min(end, E_CHUNKS) if last else end):
                    this, cc = (tile, c) if c < E_CHUNKS else (tile + 1, c - E_CHUNKS)
                    act.wait_ge(e_loaded[cc % E_SLOTS],
                                this * 16 * (E_CHUNKS // E_SLOTS) + 16 * (cc // E_SLOTS + 1))
                    if not (isinstance(this, int) and this == 0 and cc < E_SPLIT_SLOTS):
                        act.wait_ge(e_done, this * E_CHUNKS + (cc - E_SPLIT_SLOTS + 1))
                    nc.scalar.activation(e_high[cc % E_SPLIT_SLOTS], e_ring[cc % E_SLOTS], ACT.Copy) \
                        .then_inc(e_high_ready, 1)

            def expert_tile(tile, last=False):
                used = tile * E_CHUNKS
                split_chunks_of(tile, E_SPLIT_SLOTS, 8 + AHEAD)
                act.wait_ge(e_done, used + 8)
                nc.scalar.activation(act_e, banks[0][0:R, :], ACT.Silu).then_inc(silu_done, 1)
                split_chunks_of(tile, 8 + AHEAD, 16 + AHEAD)
                transposed_rows(tile + 1, 0)
                act.wait_ge(actT_ps, tile + 1)
                nc.scalar.activation(actT[0], banks[0][:, 0:4 * R].rearrange("p (k n) -> p k n", k=4), ACT.Copy) \
                    .then_inc(actT_high, 1)
                transposed_rows(tile + 1, 1)
                act.wait_ge(yb_sent, tile * 16 + 16)
                for cb in range(4):
                    split_chunks_of(tile, 16 + 2 * cb + AHEAD, 16 + 2 * cb + 2 + AHEAD, last)
                    if cb % 2 == 0:
                        act.wait_ge(e_done, used + (16 + 2 * cb + 2))
                        nc.scalar.activation(yb[:, cb * 512:(cb + 1) * 512], banks[4 + cb][0:R, :], ACT.Copy) \
                            .then_inc(y_act, 1)
                split_chunks_of(tile, E_CHUNKS + AHEAD, E_CHUNKS + E_SPLIT_SLOTS, last)

            act.wait_ge(chunks_done, FRONT)
            split_chunks_of(0, 0, E_SPLIT_SLOTS)
            for g in range(2):
                transposed_rows(0, g)
            with act.Fori(0, N_EXP - 1) as tile:
                expert_tile(tile)
            expert_tile(N_EXP - 1, True)
            over = act.value_load(ctrl_u[0:1, 0:1], min_val=0, max_val=TILES - OVER)
            with act.If(over > 0):
                split_chunks_of(OVER, 0, E_SPLIT_SLOTS)
                with act.Fori(0, TILES - OVER - 1) as i:
                    expert_tile(i + OVER)
                expert_tile(TILES - 1, True)
            for t in range(NT):
                act.wait_ge(fin_args, t + 1)
                nc.scalar.activation(yfin[t][:, 0, :], x1[:, t, :], ACT.Square, accum_out=fsum[:, t:t + 1]) \
                    .then_inc(squared, 1)
                act.wait_ge(fin_mean, t + 1)
                nc.scalar.activation(fmean[:, t:t + 1], fmean[:, t:t + 1], ACT.Sqrt).then_inc(fin_act, 1)

        @block.vector
        def _(dve):
            V = nc.vector
            seq = [0]

            def then(ins):
                seq[0] += 1
                ins.then_inc(v_seq, 1)
                dve.wait_ge(v_seq, seq[0])

            def here(ins, s, n):
                ins.then_inc(s, 1)
                dve.wait_ge(s, n)

            halves = [0]

            def split_before(done):
                for m in range(halves[0], next_splits(done)):
                    n = SPLIT[m]
                    width = CK * (MISC if PANEL["misc"][0] <= n < PANEL["uq0"][0] else 512)
                    high = parts[:, w_high[m % SPLIT_SLOTS]:w_high[m % SPLIT_SLOTS] + width]
                    low = parts[:, w_low[m % SPLIT_SLOTS]:w_low[m % SPLIT_SLOTS] + width]
                    dve.wait_ge(high_ready, m + 1)
                    V.tensor_tensor(low, at(RING + n % SLOTS * CHUNK, width), high.bitcast(F32), ALU.subtract) \
                        .then_inc(low_ready, 1)
                    halves[0] = m + 1

            dve.wait_ge(squared, 4)
            V.tensor_scalar(mean, ssum, 1.0 / D, EPS, ALU.mult, ALU.add).then_inc(mean_ready, 1)
            dve.wait_ge(rooted, 1)
            then(V.reciprocal(rinv, mean))
            for t in range(NT):
                V.tensor_scalar(xt[:, t, :], xt[:, t, :], rinv[:, t:t + 1], None, ALU.mult).then_inc(h_ready, 1)
            dve.wait_ge(small_loaded, 16 * 2)
            split_before(0)
            for k in range(KD):
                dve.wait_ge(hT_act, k + 1)
                V.scalar_tensor_tensor(out=hT[1][:, k, :], in0=banks[k % 8][:, :], scalar=g1c[:, k:k + 1],
                                       in1=hT[0][:, k, :].bitcast(F32), op0=ALU.mult, op1=ALU.subtract) \
                    .then_inc(hT_dve, 1)
            V.tensor_tensor(lb, lbx[:, 8:16], lbx[:, 0:8], ALU.subtract).then_inc(lb_arg, 1)
            for done in range(1, PANEL["cq"][1] + 1):
                split_before(done)
            dve.wait_ge(chunks_done, PANEL["cq"][1])
            for f in range(4):
                V.tensor_copy(cqT[:, f, :], banks[f][:, :]).then_inc(cq_raw, 1)
            split_before(PANEL["misc"][0] + 4)
            dve.wait_ge(ssq_ps, 1)
            V.tensor_scalar(cq_rms, banks[0][:, :], 1.0 / Q_RANK, EPS, ALU.mult, ALU.add).then_inc(mean_ready, 1)
            dve.wait_ge(rooted, 2)
            then(V.reciprocal(cq_rms, cq_rms))
            for f in range(4):
                V.scalar_tensor_tensor(out=cqT[:, f, :], in0=cqT[:, f, :], scalar=gqc[:, f:f + 1], in1=cq_rms,
                                       op0=ALU.mult, op1=ALU.mult).then_inc(cq_norm, 1)

            dve.wait_ge(rope_loaded, 16)
            turned = [0]

            def rope(ps):
                n = turned[0]
                turned[0] += 1
                if n >= 2:
                    dve.wait_ge(roped, n - 1)
                V.tensor_tensor(rope_a[:, n % 2, :], ps[:, :], cos2, ALU.mult)
                V.tensor_tensor(rope_b[0:64, n % 2, :], ps[64:128, :], sin2[64:128, :], ALU.mult)
                V.tensor_tensor(rope_b[64:128, n % 2, :], ps[0:64, :], sin2[0:64, :], ALU.mult).then_inc(rope_mul, 1)

            split_before(PANEL["uq0"][0])
            dve.wait_ge(chunks_done, PANEL["uq0"][0])
            rope(banks[4])
            rope(banks[5])
            V.tensor_copy(vtok, banks[6][:, :].rearrange("p (t n) -> p t n", t=NT)).then_inc(v_copied, 1)
            V.tensor_scalar(wi, banks[7][:, 0:64].rearrange("p (t n) -> p t n", t=NT),
                            IDX_HEADS ** -0.5 * IDX_D ** -0.5, None, ALU.mult).then_inc(v_copied, 1)
            for name in ("uq0", "uq1", "qi0", "qi1", "qi2", "qi3"):
                start, chunks, bank = PANEL[name]
                split_before(start + chunks)
                dve.wait_ge(chunks_done, start + chunks)
                for f in range(4):
                    rope(banks[bank + f])
            dve.wait_ge(roped, turned[0])
            dve.wait_ge(causal_loaded, 16)
            dve.wait_ge(v_copied, 2)

            i_n = m = normed = 0

            def normalise(m, t):
                dve.wait_ge(exp_done, m + 1)
                then(V.reciprocal(rrec[:, m:m + 1], rsum[:, m:m + 1]))
                keys = (t + 1) * P
                V.tensor_scalar(probs[:, m % 2, 0:keys], probs[:, m % 2, 0:keys], rrec[:, m:m + 1], None,
                                ALU.mult).then_inc(probs_ready, 1)

            att = [s for s in STEPS if s[0] == "att"]
            for n, (kind, t, h) in enumerate(STEPS):
                keys = (t + 1) * P
                split_before(filled(att_fill, "ga0", n))
                if kind == "idx":
                    if m > normed and h == 2:
                        normalise(m - 1, att[m - 1][1])
                        normed = m
                    dve.wait_ge(relu_done, i_n + 1)
                    acc = causal[:, T - keys:T] if h == 0 else score[:, 0:keys]
                    here(V.scalar_tensor_tensor(out=score[:, 0:keys], in0=relu[:, i_n % 2, 0:keys],
                                                scalar=wi[:, t, h:h + 1], in1=acc, op0=ALU.mult, op1=ALU.add),
                         scored, i_n + 1)
                    i_n += 1
                    if h == IDX_HEADS - 1:
                        for r in range(TOPK // 8):
                            ahead = att_fill[n] + att_fill[n + 1] + att_fill[n + 2]
                            before_n = PANEL["ga0"][0] + sum(att_fill[:n]) // CK
                            split_before(min(before_n + r * ahead // (TOPK // 8) // CK + 1,
                                             filled(att_fill, "ga0", n + 3)))
                            then(V.max(out=top8, in_=score[:, 0:keys]))
                            then(V.match_replace(out=score[:, 0:keys], in_to_replace=top8,
                                                 in_values=score[:, 0:keys], imm_value=TAKEN))
                        then(V.tensor_scalar(bias[:, t % 2, 0:keys], score[:, 0:keys], (FILL + TAKEN) / 2, OUT,
                                             ALU.is_gt, ALU.mult))
                else:
                    dve.wait_ge(logits_ps, n + 1)
                    b = causal[:, T - keys:T] if t == 0 else bias[:, t % 2, 0:keys]
                    here(V.tensor_tensor_reduce(out=masked[:, m % 2, 0:keys], in0=banks[4 + n % 2][:, 0:keys], in1=b,
                                                scale=1.0, scalar=FILL, op0=ALU.add, op1=ALU.max,
                                                accum_out=smax[:, m:m + 1]), att_masked, m + 1)
                    V.tensor_scalar(nmax[:, m:m + 1], smax[:, m:m + 1], -HEAD_D ** -0.5, None, ALU.mult) \
                        .then_inc(nmax_ready, 1)
                    if m > normed:
                        normalise(m - 1, att[m - 1][1])
                        normed = m
                    m += 1
            normalise(m - 1, att[m - 1][1])
            split_before(filled(att_fill, "ga0", len(STEPS)))

            def tree_args(u):
                f, pair = u % 8 // 2, u % 2
                buf, tok = qk[u % 2], slice(pair * 256, pair * 256 + 256)
                if u >= 2:
                    dve.wait_ge(rec_ps, 2 * (u - 1))
                for m in range(LEVELS):
                    h = P >> (m + 1)
                    c = hc[:, f, tok].rearrange("p (b s h) -> p b s h", s=2, h=h)
                    o = buf[:, m, :].rearrange("p (b s h) -> p b s h", s=2, h=h)
                    mid = c[:, :, 0, h - 1:h].to_broadcast([P, 256 // (2 * h), h])
                    V.tensor_tensor(o[:, :, 1, :], c[:, :, 1, :], mid, ALU.subtract)
                    V.tensor_tensor(o[:, :, 0, :], mid, c[:, :, 0, :], ALU.subtract)
                c = hc[:, f, tok].rearrange("p (b t) -> p b t", t=P)
                V.tensor_tensor(buf[:, 7, :].rearrange("p (b t) -> p b t", t=P),
                                c[:, :, P - 1:P].to_broadcast([P, 2, P]), c, ALU.subtract).then_inc(tree_arg, 1)

            for b in range(2):
                def split_while(name):
                    for done in range(PANEL[name][0], sum(PANEL[name][:2]) + 1):
                        split_before(done)

                split_while(f"hq{b}")
                split_while(f"hf{b}")
                dve.wait_ge(hf_sigmoid, 4 * (b + 1))
                if b == 0:
                    dve.wait_ge(lb_exp, 1)
                    then(V.tensor_scalar(lb, lb, 1.0, None, ALU.add))
                    then(V.reciprocal(lb, lb))
                    then(V.tensor_scalar(one_lb, lb, -1.0, 1.0, ALU.mult, ALU.add))
                for f in range(4):
                    h = 4 * b + f
                    ins = V.tensor_scalar(hc[:, f, :], hk[:, f, :], one_lb[:, h:h + 1], lb[:, h:h + 1],
                                          ALU.mult, ALU.add)
                then(ins)
                here(V.tensor_scalar(hk, hc, -1.0, 1.0, ALU.mult, ALU.add), hf_ready, b + 1)
                for done in range(3):
                    split_before(PANEL[f"hi{b}"][0] + done)
                dve.wait_ge(hf_ln, b + 1)
                for f in range(4):
                    split_before(PANEL[f"hi{b}"][0] + 3 + f // 2)
                    ins = V.tensor_tensor_scan(out=hc[:, f, :], data0=restart, data1=hc[:, f, :], initial=0.0,
                                               op0=ALU.mult, op1=ALU.add)
                then(ins)
                split_while(f"hi{b}")
                tree_args(8 * b)
                for i in range(16):
                    n = 16 * b + i
                    c = n % 4
                    split_before(filled(rec_fill, REC_GATES[b][0], i))
                    for half in range(2):
                        dve.wait_ge(tree_ps, 2 * n + half + 1)
                        here(V.tensor_tensor(lev[:, half * 512:(half + 1) * 512], banks[4 + half][:, :],
                                             level_mask[:, half * 512:(half + 1) * 512], ALU.mult),
                             tree_masked, 2 * n + half + 1)
                    if n >= 2:
                        dve.wait_ge(rec_ps, n - 1)
                    here(V.tensor_reduce(intra[:, n % 2, :], lev.rearrange("p (m t) -> p t m", m=8), AX.X, ALU.add),
                         intra_ready, n + 1)
                    if i % 2 == 0 and i < 14:
                        tree_args(n // 2 + 1)
                    split_before(filled(rec_fill, REC_GATES[b][0], i + 1))
                    if c < 3:
                        dve.wait_ge(state_ps, n // 4 * 3 + c + 1)
                        if n:
                            dve.wait_ge(rec_ps, n)
                        if c == 0:
                            V.tensor_copy(state[:, 1, :], banks[6][:, 0:P]).then_inc(state_ready, 1)
                        else:
                            k = n // 2 % 2 * 2 + n % 2
                            V.scalar_tensor_tensor(out=state[:, (c + 1) % 2, :], in0=state[:, c % 2, :],
                                                   scalar=decay[:, k:k + 1], in1=banks[6][:, 0:P],
                                                   op0=ALU.mult, op1=ALU.add).then_inc(state_ready, 1)
            split_before(PANEL["hg0"][0])
            dve.wait_ge(recsq_ps, 1)
            then(V.tensor_scalar(lev[:, 0:T], banks[4][:, :], 1.0 / G_WIDTH, EPS, ALU.mult, ALU.add))
            here(V.tensor_copy(lev[:, T:T + 1], lev[:, 0:1]), mean_ready, 3)
            dve.wait_ge(rooted, 3)
            then(V.reciprocal(lev[:, 0:T], lev[:, 0:T]))
            for h in range(G_HEADS):
                ins = V.scalar_tensor_tensor(out=yrecT[:, h, :], in0=yrecT[:, h, :], scalar=ghc[:, h:h + 1],
                                             in1=lev[:, 0:T], op0=ALU.mult, op1=ALU.mult)
            here(ins, rec_normed, 1)
            hg_tmp = [hc, hv]
            for b in range(2):
                for f in range(4):
                    h = 4 * b + f
                    e = hg_tmp[b][:, f, :]
                    split_before(PANEL[f"hg{b}"][0] + PANEL[f"hg{b}"][1])
                    dve.wait_ge(hg_silu, h + 1)
                    V.tensor_tensor(yrecT[:, h, :], yrecT[:, h, :], e, ALU.mult).then_inc(hg_ready, 1)

            for b in range(4):
                dve.wait_ge(gate_loaded, 32 * (b + 1))
                for k, (name, g) in enumerate((("pa", gate_a), ("pb", gate_b))):
                    start, chunks, bank = PANEL[f"{name}{b}"]
                    split_before(start + chunks)
                    dve.wait_ge(chunks_done, start + chunks)
                    for f in range(4):
                        if k == 0:
                            V.tensor_tensor(mT[:, 4 * b + f, :], banks[bank + f][:, :], g[:, f, :], ALU.mult) \
                                .then_inc(merge_read, 1)
                        else:
                            here(V.tensor_tensor(g[:, f, :], banks[bank + f][:, :], g[:, f, :], ALU.mult),
                                 merge_read, 8 * b + 4 + f + 1)
                            V.tensor_tensor(mT[:, 4 * b + f, :], mT[:, 4 * b + f, :], g[:, f, :], ALU.add) \
                                .then_inc(merged_sum, 1)
                for f in range(4):
                    k = 4 * b + f
                    dve.wait_ge(merged_high, k + 1)
                    V.tensor_tensor(hT[1][:, k, :], mT[:, k, :], hT[0][:, k, :].bitcast(F32), ALU.subtract) \
                        .then_inc(merged_ready, 1)
            for b in range(4):
                start, chunks, bank = PANEL[f"wo{b}"]
                for done in range(start, start + chunks + 1):
                    split_before(done)
                for t in range(NT if b == 0 else 0):
                    dve.wait_ge(x_loaded[t], 32)
                dve.wait_ge(chunks_done, start + chunks)
                for t in range(NT):
                    cols = x1[:, t, b * 512:(b + 1) * 512]
                    V.tensor_tensor(cols, banks[bank + t][:, :], cols, ALU.add).then_inc(x1_ready, 1)
            dve.wait_ge(squared, 8)
            V.tensor_scalar(mean, ssum, 1.0 / D, EPS, ALU.mult, ALU.add).then_inc(mean_ready, 1)
            dve.wait_ge(rooted, 4)
            then(V.reciprocal(rinv, mean))
            dve.wait_ge(late_loaded, 16 * 7)
            for t in range(NT):
                V.scalar_tensor_tensor(out=h2[:, t, :], in0=x1[:, t, :], scalar=rinv[:, t:t + 1], in1=g2b,
                                       op0=ALU.mult, op1=ALU.mult).then_inc(h2_ready, 1)
            for k in range(0, KD, 2):
                dve.wait_ge(h2T_ps, k + 1)
                if k >= 4:
                    dve.wait_ge(router_ps, k - 3)
                V.tensor_copy(h2T[:, k % 4, :], banks[k % 4][:, :]).then_inc(h2T_dve, 1)

            def over_tokens(v, n):
                return v.unsqueeze(1).to_broadcast([P, NT, n])

            iota32, e_r = rowc[:, 36:68], rowc[:, 68:100]
            step_r = rowc[:, 100:132]
            then(V.memset(lg, FILL))
            dve.wait_ge(router_ps, KD)
            for t in range(NT):
                V.tensor_tensor(lg[:, t, 0:4], banks[4 + t][:, 0:4], rowc[:, 0:4], ALU.add)
                ins = V.tensor_tensor(le[:, t, :], banks[4 + t][:, 4:36], rowc[:, 4:36], ALU.add)
            then(ins)
            for t in range(NT):
                ins = V.max(out=g8[:, t, :], in_=lg[:, t, :])
            then(ins)
            for t in range(NT):
                V.max_index(out=gi8[:, t, :], in_max=g8[:, t, :], in_values=lg[:, t, :])
            here(V.tensor_scalar(gneg, g8[:, :, 0], -1.0, None, ALU.mult), route_arg, 1)
            then(V.tensor_copy(gidx, gi8[:, :, 0]))
            then(V.tensor_tensor(gout, over_tokens(iota32[:, 0:4], 4), gidx.unsqueeze(2).to_broadcast([P, NT, 4]),
                                 ALU.not_equal))
            then(V.tensor_scalar(gout, gout, OUT, None, ALU.mult))
            then(V.tensor_tensor(le.rearrange("p t (g e) -> p t g e", g=4), le.rearrange("p t (g e) -> p t g e", g=4),
                                 gout.unsqueeze(3).to_broadcast([P, NT, 4, 8]), ALU.add))
            for t in range(NT):
                ins = V.max(out=e8[:, t, :], in_=le[:, t, :])
            then(ins)
            for t in range(NT):
                ins = V.max_index(out=ei8[:, t, :], in_max=e8[:, t, :], in_values=le[:, t, :])
            then(ins)
            here(V.tensor_tensor(diff, e8[:, :, 1], e8[:, :, 0], ALU.subtract), route_arg, 2)
            for c in range(2):
                then(V.tensor_copy(eidx[:, c, :], ei8[:, :, c]))
                then(V.tensor_tensor(pick[:, c], over_tokens(iota32, 32),
                                     eidx[:, c, :].unsqueeze(2).to_broadcast([P, NT, 32]), ALU.is_equal))
            here(V.tensor_tensor(both, pick[:, 0], pick[:, 1], ALU.add), picked, 1)
            dve.wait_ge(route_exp, 5)
            then(V.tensor_scalar(den, diff, 1.0, None, ALU.add))
            then(V.tensor_tensor(den, den, gsum, ALU.mult))
            then(V.reciprocal(gate1, den))
            then(V.tensor_tensor(gate2, gate1, diff, ALU.mult))
            dve.wait_ge(x1_ready, 16)
            V.tensor_copy(gate1k, gate1)
            V.tensor_copy(gate2k, gate2)
            dve.wait_ge(rank_ps, 1)
            V.tensor_copy(rank, banks[1][:, 0:NT * N_EXP].rearrange("p (t e) -> p t e", t=NT))
            then(V.tensor_copy(count, banks[1][:, NT * N_EXP:(NT + 1) * N_EXP]))
            then(V.tensor_scalar(extra, count, float(R), None, ALU.is_gt))
            for k in range(2, T // R):
                then(V.scalar_tensor_tensor(out=extra, in0=count, scalar=float(k * R), in1=extra, op0=ALU.is_gt,
                                            op1=ALU.add))
            then(V.memset(ones_e, 1.0))
            then(V.tensor_tensor_scan(out=upto, data0=ones_e, data1=extra, initial=0.0, op0=ALU.mult, op1=ALU.add))
            then(V.tensor_tensor(base, upto, extra, ALU.subtract))
            then(V.scalar_tensor_tensor(out=delta, in0=base, scalar=float(R), in1=step_r, op0=ALU.mult, op1=ALU.add))
            then(V.scalar_tensor_tensor(out=pos, in0=rank, scalar=float(R), in1=over_tokens(delta, 32),
                                        op0=ALU.is_ge, op1=ALU.mult))
            then(V.tensor_tensor(pos, pos, rank, ALU.add))
            then(V.tensor_tensor(pos, pos, over_tokens(e_r, 32), ALU.add))
            for c in range(2):
                then(V.tensor_tensor(posp, pos, pick[:, c], ALU.mult))
                then(V.tensor_reduce(slot[:, c, :], posp, AX.X, ALU.add))
            then(V.tensor_copy(slot_u.rearrange("p (c t) -> p c t", c=2), slot))
            V.tensor_copy(ctrl_f[:, 0:1], upto[:, N_EXP - 1:N_EXP])
            for k in range(TILES - OVER):
                then(V.tensor_scalar(posp[:, 0, :], upto, float(k), None, ALU.is_le))
                then(V.tensor_reduce(ctrl_f[:, 1 + k:2 + k], posp[:, 0, :], AX.X, ALU.add))
            then(V.tensor_scalar(ctrl_f[:, 1:16], ctrl_f[:, 1:16], float(N_EXP - 1), None, ALU.min))
            here(V.tensor_copy(ctrl_u[:, 0:16], ctrl_f[:, 0:16]), placed, 1)
            V.memset(act_all, 0.0).then_inc(slots_ready, 1)

            def transposed_rows(tile, g):
                dve.wait_ge(xgT_high, tile * 2 + (g + 1))
                V.tensor_tensor(xgT[1][:, 8 * g:8 * g + 8, :], banks[2 + g][:, :].rearrange("p (k n) -> p k n", k=8),
                                xgT[0][:, 8 * g:8 * g + 8, :].bitcast(F32), ALU.subtract).then_inc(xgT_low, 1)

            def split_chunks_of(tile, first, end, last=False):
                for c in range(first, min(end, E_CHUNKS) if last else end):
                    this, cc = (tile, c) if c < E_CHUNKS else (tile + 1, c - E_CHUNKS)
                    dve.wait_ge(e_high_ready, this * E_CHUNKS + (cc + 1))
                    V.tensor_tensor(e_low[cc % E_SPLIT_SLOTS], e_ring[cc % E_SLOTS],
                                    e_high[cc % E_SPLIT_SLOTS].bitcast(F32), ALU.subtract).then_inc(e_low_ready, 1)

            def expert_tile(tile, last=False):
                used = tile * E_CHUNKS

                split_chunks_of(tile, E_SPLIT_SLOTS, 8 + AHEAD)
                split_chunks_of(tile, 8 + AHEAD, 16 + AHEAD)
                dve.wait_ge(silu_done, tile + 1)
                dve.wait_ge(e_done, used + 16)
                V.tensor_tensor(act_h, banks[1][0:R, :], act_e, ALU.mult).then_inc(act_ready, 1)
                transposed_rows(tile + 1, 0)
                dve.wait_ge(actT_high, tile + 1)
                V.tensor_tensor(actT[1], banks[0][:, 0:4 * R].rearrange("p (k n) -> p k n", k=4),
                                actT[0].bitcast(F32), ALU.subtract).then_inc(actT_low, 1)
                transposed_rows(tile + 1, 1)
                dve.wait_ge(yb_sent, tile * 16 + 16)
                for cb in range(4):
                    split_chunks_of(tile, 16 + 2 * cb + AHEAD, 16 + 2 * cb + 2 + AHEAD, last)
                    if cb % 2:
                        dve.wait_ge(e_done, used + (16 + 2 * cb + 2))
                        V.tensor_copy(yb[:, cb * 512:(cb + 1) * 512], banks[4 + cb][0:R, :]).then_inc(y_dve, 1)
                split_chunks_of(tile, E_CHUNKS + AHEAD, E_CHUNKS + E_SPLIT_SLOTS, last)

            split_chunks_of(0, 0, E_SPLIT_SLOTS)
            for g in range(2):
                transposed_rows(0, g)
            with dve.Fori(0, N_EXP - 1) as tile:
                expert_tile(tile)
            expert_tile(N_EXP - 1, True)
            over = dve.value_load(ctrl_u[0:1, 0:1], min_val=0, max_val=TILES - OVER)
            with dve.If(over > 0):
                split_chunks_of(OVER, 0, E_SPLIT_SLOTS)
                with dve.Fori(0, TILES - OVER - 1) as i:
                    expert_tile(i + OVER)
                expert_tile(TILES - 1, True)

            for t in range(NT):
                dve.wait_ge(yfin_loaded[t], 16)
                then(V.scalar_tensor_tensor(out=x1[:, t, :], in0=yfin[t][:, 0, :], scalar=gate1k[:, t:t + 1],
                                            in1=x1[:, t, :], op0=ALU.mult, op1=ALU.add))
                here(V.scalar_tensor_tensor(out=x1[:, t, :], in0=yfin[t][:, 1, :], scalar=gate2k[:, t:t + 1],
                                            in1=x1[:, t, :], op0=ALU.mult, op1=ALU.add), fin_args, t + 1)
                dve.wait_ge(squared, 9 + t)
                V.tensor_scalar(fmean[:, t:t + 1], fsum[:, t:t + 1], 1.0 / D, EPS, ALU.mult, ALU.add) \
                    .then_inc(fin_mean, 1)
                dve.wait_ge(fin_act, t + 1)
                then(V.reciprocal(fmean[:, t:t + 1], fmean[:, t:t + 1]))
                V.scalar_tensor_tensor(out=x1[:, t, :], in0=x1[:, t, :], scalar=fmean[:, t:t + 1], in1=gfb,
                                       op0=ALU.mult, op1=ALU.mult).then_inc(fin_dve, 1)


INPUTS = ["x", "w_in", "w_uq", "w_qidx", "w_pa", "w_pb", "w_o", "g_norm2", "w_grp", "b_grp", "w_exp", "b_exp", "w_gate", "w_up", "w_down", "g_final"]


def tables():
    f = np.float32
    i = np.arange(P)
    levels = []
    for m in range(LEVELS):
        h = P >> (m + 1)
        same = i[:, None] // (2 * h) == i[None, :] // (2 * h)
        levels.append(same & (i[:, None] % (2 * h) < h) & (i[None, :] % (2 * h) >= h))
    levels.append(i[:, None] == i[None, :])
    restart = np.broadcast_to((np.arange(T) % P != 0).astype(f), (P, T))
    const = np.concatenate([np.eye(P), np.ones((P, P)), i[:, None] < i[None, :], *levels, restart], 1).astype(f)
    inv = (1.0 / (f(10000.0) ** (np.arange(0, HEAD_D, 2, dtype=f) / f(HEAD_D)))).astype(f)
    ang = (np.arange(T, dtype=f)[None, :] * inv[:, None]).astype(f)
    cos, sin = np.cos(ang), np.sin(ang)
    rope = np.concatenate([np.concatenate([cos, cos], 0), np.concatenate([sin, -sin], 0)], 1).astype(f)
    causal = np.zeros((P, T), f)
    causal[:, T - P:][i[None, :] > i[:, None]] = FILL
    e = np.arange(N_EXP, dtype=f)
    route = np.concatenate([e, e * R, (OVER - 1 - e) * R, 0 * e])
    route = np.broadcast_to(route, (P, 4 * N_EXP)).astype(f)
    rows = np.zeros((P, 2, NT, 2), np.uint32)
    for c in range(2):
        for t in range(NT):
            rows[:, c, t, 0] = t * P + i
            rows[:, c, t, 1] = 2 * (t * P + i) + c
    return {"t_const": const, "t_rope": rope, "t_causal": causal, "t_route": np.ascontiguousarray(route),
            "t_rows": rows.reshape(P, -1)}


def layout(inputs):
    arrays = {n: np.ascontiguousarray(inputs[n]) for n in INPUTS}
    for n in ("w_in", "w_uq", "w_qidx", "w_pa", "w_pb", "w_o", "w_gate", "w_up", "w_down"):
        arrays[n] = arrays[n][0]
    columns = [np.asarray(inputs[n])[0] for n in ("g_norm1", "g_cq", "g_hnorm")] + list(np.asarray(inputs["lb_logits"]))
    arrays["gains"] = np.ascontiguousarray(np.concatenate([c.reshape(-1, P) for c in columns], 0).T)
    arrays.update(tables())
    return arrays


def kernel(**inputs):
    import concourse.bacc as bacc
    from concourse.bass_utils import run_bass_kernel_spmd

    arrays = layout(inputs)
    nc = bacc.Bacc("TRN2", target_bir_lowering=False, num_devices=1)
    args = {n: nc.dram_tensor(n, a.shape, mybir.dt.from_np(a.dtype), kind="ExternalInput").ap()
            for n, a in arrays.items()}
    out = nc.dram_tensor("out", (1, T, D), F32, kind="ExternalOutput").ap()
    build(nc, **args, out=out)
    r = run_bass_kernel_spmd(nc, [arrays], core_ids=[0])
    return r.results[0]["out"]
```

```python
import math
from contextlib import ExitStack

import numpy as np

import concourse.bass as bass
from concourse import mybir

F32 = mybir.dt.float32
F32R = mybir.dt.float32r
U32 = mybir.dt.uint32
ALU = mybir.AluOpType
ACT = mybir.ActivationFunctionType
AX = mybir.AxisListType

P = 128
D, T = 2048, 512
KD, NT = D // P, T // P
A_HEADS, HEAD_D = 8, 128
Q_RANK = 512
IDX_HEADS, IDX_D = 16, 128
TOPK = 128
G_HEADS = 8
N_GROUPS, PER_GROUP = 4, 8
N_EXP = N_GROUPS * PER_GROUP
D_EXP = 512
EPS = 1e-6
A_WIDTH = A_HEADS * HEAD_D
G_WIDTH = G_HEADS * 128
FILL = -3.0e38
TAKEN = -3.4e38
OUT = -1.0e30

C_CQ = 0
C_K = C_CQ + Q_RANK
C_HQ = C_K + 3 * 128 + IDX_HEADS
C_HF, C_HI, C_HG = C_HQ + G_WIDTH, C_HQ + 2 * G_WIDTH, C_HQ + 3 * G_WIDTH
C_GA = C_HQ + 4 * G_WIDTH
C_GB = C_GA + D
D_IN = C_GB + D
MISC = C_HQ - C_K

CK = 2
CHUNK = CK * 512
SLOTS = 4
SPLIT_SLOTS = 2
E_SLOTS = 12
E_SPLIT_SLOTS = 6
AHEAD = 5
E_CHUNKS = 2 * KD // CK + D_EXP // P // CK * (D // 512)
PANEL_GATE = 4 * 512
R = 64
TILES = N_EXP + 2 * T // R - 1
OVER = N_EXP
LEVELS = 7
NO_ROW = 60000

RING = 0
YATT = RING + SLOTS * CHUNK
YREC = YATT + A_HEADS * T
U = YREC + G_HEADS * T
TAB = U + 17920
SMALL = TAB + 3 * P + 8 * P + T
TOTAL = SMALL + 592
HIGH, LOW = 0, KD * T
W_PARTS = 2 * KD * T
TOTAL_PARTS = W_PARTS + 2 * SPLIT_SLOTS * CHUNK


def panels():
    order = [("cq", 4, 0), ("misc", 4, 4), ("uq0", 1, 0), ("uq1", 1, 4),
             ("qi0", 1, 0), ("qi1", 1, 4), ("qi2", 1, 0), ("qi3", 1, 4),
             ("ga0", 4, 0), ("ga1", 4, 0), ("ga2", 4, 0), ("ga3", 4, 0),
             ("hq0", 4, 0), ("hf0", 4, 4), ("hi0", 4, 0), ("gb0", 4, 0), ("gb1", 4, 0), ("gb2", 4, 0),
             ("hq1", 4, 0), ("hf1", 4, 4), ("hi1", 4, 0), ("gb3", 4, 0), ("hg0", 4, 0), ("hg1", 4, 0)]
    for b in range(4):
        order += [(f"pa{b}", 2, 4), (f"pb{b}", 2, 0)]
    order += [(f"wo{b}", 4, 4 - 4 * (b % 2)) for b in range(4)]
    found, start = {}, 0
    for name, chunks, bank in order:
        chunks *= 4 // CK
        found[name] = (start, chunks, bank)
        start += chunks
    return found, start


def split_chunks(panel):
    return [n for name, (start, chunks, _) in panel.items() if name[:2] not in ("uq", "qi")
            for n in range(start, start + chunks)]


def attention_steps():
    idx = lambda t: [("idx", t, h) for h in range(IDX_HEADS)]
    att = lambda t: [("att", t, h) for h in range(A_HEADS)]
    return idx(1) + att(0) + idx(2) + att(1) + idx(3) + att(2) + att(3)


def build(nc, x, gains, w_in, w_uq, w_qidx, w_pa, w_pb, w_o, g_norm2,
          w_grp, b_grp, w_exp, b_exp, w_gate, w_up, w_down, g_final, t_const, t_rope, t_causal,
          t_route, t_rows, out):
    PANEL, FRONT = panels()
    SPLIT = split_chunks(PANEL)
    SPLIT_NO = {n: m for m, n in enumerate(SPLIT)}
    STEPS = attention_steps()
    IDX_N = sum(s[0] == "idx" for s in STEPS)
    ATT_N = sum(s[0] == "att" for s in STEPS)

    gates_d = nc.dram_tensor("gates", (10, P, PANEL_GATE), F32, kind="Internal").ap()
    h2_d = nc.dram_tensor("h2_rows", (T, D), F32, kind="Internal").ap()
    y2_d = nc.dram_tensor("expert_rows", (2 * T, D), F32, kind="Internal").ap()
    slots_d = nc.dram_tensor("slot_rows", ((TILES + 1) * R, 2), U32, kind="Internal").ap()

    ctx = ExitStack()
    with ctx:
        mem = ctx.enter_context(nc.sbuf_tensor("mem", [P, TOTAL], F32))
        parts = ctx.enter_context(nc.sbuf_tensor("parts", [P, TOTAL_PARTS], F32R))
        ctx.enter_context(nc.allow_non_contiguous_dma("columns of gains, and slot tables"))
        banks = [ctx.enter_context(nc.psum_tensor(f"bank{i}", [P, 512], F32)) for i in range(8)]

        def at(start, *shape):
            n = math.prod(shape)
            v = mem[:, start:start + n]
            if len(shape) == 2:
                v = v.rearrange("p (a b) -> p a b", a=shape[0])
            if len(shape) == 3:
                v = v.rearrange("p (a b c) -> p a b c", a=shape[0], b=shape[1])
            return v

        def sem(name):
            return ctx.enter_context(nc.semaphore(name))

        def part(start, k, n):
            return parts[:, start:start + k * n].rearrange("p (k n) -> p k n", k=k)

        ring = [at(RING + s * CHUNK, CK, 512) for s in range(SLOTS)]
        hT = [part(HIGH, KD, T), part(LOW, KD, T)]
        yT, mergedT = hT, hT
        w_high = [W_PARTS + s * CHUNK for s in range(SPLIT_SLOTS)]
        w_low = [W_PARTS + (SPLIT_SLOTS + s) * CHUNK for s in range(SPLIT_SLOTS)]
        yattT = at(YATT, A_HEADS, T)
        yrecT = at(YREC, G_HEADS, T)
        ident, ones, before = at(TAB, P), at(TAB + P, P), at(TAB + 2 * P, P)
        level_mask, restart = at(TAB + 3 * P, 8 * P), at(TAB + 11 * P, T)
        cur = [SMALL]

        def small(n):
            cur[0] += n
            assert cur[0] <= TOTAL
            return mem[:, cur[0] - n:cur[0]]

        g1c, gqc, ghc, lbx = small(KD), small(Q_RANK // P), small(G_HEADS), small(2 * G_HEADS)
        lb, one_lb = small(G_HEADS), small(G_HEADS)
        ssum, mean, rinv = small(NT), small(NT), small(NT)
        wi = small(NT * IDX_HEADS).rearrange("p (t h) -> p t h", t=NT)
        smax, nmax, rsum, rrec = small(32), small(32), small(32), small(32)
        top8, decay = small(8), small(4)
        ssum_parts = small(4 * NT).rearrange("p (t b) -> p t b", t=NT)
        xt = at(U + 4096, NT, D)
        junk = at(YATT, NT, D)
        qT, qiT = at(U, A_HEADS, T), at(U + 4096, IDX_HEADS, T)
        cqT = at(U + 12288, 4, T)
        kT, kiT, vtok = at(U + 14336, T), at(U + 14848, T), at(U + 15360, NT, P)
        stage = at(U + 15872, 4, 512)
        cos2, sin2 = at(YATT, T), at(YATT + T, T)
        cq_sq, cq_rms = at(YATT + 2 * T, 4, T), at(YATT + 6 * T, T)
        vT, wiT = at(YATT + 2 * T, T), at(YATT + 3 * T, T)
        rope_a, rope_b = at(YREC, 2, T), at(YREC + 2 * T, 2, T)
        relu, score = at(YREC, 2, T), at(YREC + 2 * T, T)
        masked, probs = at(YREC + 3 * T, 2, T), at(YREC + 5 * T, 2, T)
        causal = at(YREC + 7 * T, T)
        bias, probsT = at(U + 12288, 2, T), at(U + 13312, 2, T)
        hq, hk, hc, hv = (at(U + 2048 * i, 4, T) for i in range(4))
        QK = 9 * 256
        qk = [at(U + 8192 + QK * i, 9, 256) for i in range(2)]
        lev = at(U + 12800, 8 * P)
        intra, keT, state = (at(U + 13824 + 256 * i, 2, P) for i in range(3))
        mT = at(U, KD, T)
        gate_a, gate_b = at(U + 8192, 4, 512), at(U + 10240, 4, 512)
        g2b, gfb = at(U + 12288, D), at(U + 14336, D)
        x1 = at(YATT, NT, D)
        h2 = at(U, NT, D)
        h2T = at(U + 8192, 4, T)
        wr = at(U + 10240, KD, 36)
        logitsT = at(TAB + 3 * P, T)
        rt = U + 10240 + KD * 36
        xg_all, act_all = at(U, D), at(U + 10752, 512)
        xg, yb = xg_all[0:R], at(U + 2 * D, D)[0:R]
        xgT = [part(0, KD, R), part(D, KD, R)]
        act_e, act_h = at(U + 10240, 512)[0:R], act_all[0:R]
        actT = [part(2 * D, 4, R), part(2 * D + 512, 4, R)]
        e_ring = [at(a, CK, 512) for a in [RING + s * CHUNK for s in range(SLOTS)] +
                  [U + a for a in (12288, 13312, 2048, 3072, 6144, 7168, 8192, 9216)]]
        e_parts = 2 * D + 1024
        e_high = [part(e_parts + 2 * s * CHUNK, CK, 512) for s in range(E_SPLIT_SLOTS)]
        e_low = [part(e_parts + (2 * s + 1) * CHUNK, CK, 512) for s in range(E_SPLIT_SLOTS)]
        assert e_parts + 2 * E_SPLIT_SLOTS * CHUNK <= TOTAL_PARTS
        yfin = [at(a, 2, D) for a in (RING, U, U + 2 * D, U + 4 * D)]

        w_loaded = [sem(f"w_loaded{s}") for s in range(SLOTS)]
        x_loaded = [sem(f"x_loaded{t}") for t in range(NT)]
        small_loaded, rope_loaded, causal_loaded = sem("small_loaded"), sem("rope_loaded"), sem("causal_loaded")
        hg_loaded = [sem(f"hg_loaded{b}") for b in range(2)]
        gate_stored, gate_loaded, late_loaded = sem("gate_stored"), sem("gate_loaded"), sem("late_loaded")
        h2_stored, slots_cleared, slots_written = sem("h2_stored"), sem("slots_cleared"), sem("slots_written")
        slots_loaded, yb_sent, xg_loaded = sem("slots_loaded"), sem("yb_sent"), sem("xg_loaded")
        e_loaded = [sem(f"e_loaded{s}") for s in range(E_SLOTS)]
        yfin_loaded = [sem(f"yfin_loaded{i}") for i in range(4)]
        out_stored = sem("out_stored")
        chunks_done, xT_ps, ssq_ps, v_ps = sem("chunks_done"), sem("xT_ps"), sem("ssq_ps"), sem("v_ps")
        logits_ps, probsT_ps, att_ps = sem("logits_ps"), sem("probsT_ps"), sem("att_ps")
        tree_ps, keT_ps, state_ps, rec_ps = sem("tree_ps"), sem("keT_ps"), sem("state_ps"), sem("rec_ps")
        recsq_ps, h2T_ps, router_ps, rank_ps = sem("recsq_ps"), sem("h2T_ps"), sem("router_ps"), sem("rank_ps")
        xgT_ps, actT_ps, e_done = sem("xgT_ps"), sem("actT_ps"), sem("e_done")
        squared, rooted, hT_act, cq_squared = sem("squared"), sem("rooted"), sem("hT_act"), sem("cq_squared")
        relu_done, exp_done, probsT_sb, att_sb = sem("relu_done"), sem("exp_done"), sem("probsT_sb"), sem("att_sb")
        gate_sigmoid, hq_ready, hf_sigmoid, hf_ln, hv_sb = (sem("gate_sigmoid"), sem("hq_ready"), sem("hf_sigmoid"),
                                                        sem("hf_ln"), sem("hv_sb"))
        tree_exp, keT_sb, rec_sb, rec_squared = sem("tree_exp"), sem("keT_sb"), sem("rec_sb"), sem("rec_squared")
        h2T_act, route_exp = sem("h2T_act"), sem("route_exp")
        xgT_high, silu_done, actT_high, y_act = sem("xgT_high"), sem("silu_done"), sem("actT_high"), sem("y_act")
        fin_act, lb_exp = sem("fin_act"), sem("lb_exp")
        high_ready, merged_high, y_high = sem("high_ready"), sem("merged_high"), sem("y_high")
        e_high_ready = sem("e_high_ready")
        v_seq = sem("v_seq")
        mean_ready, h_ready, hT_dve = sem("mean_ready"), sem("h_ready"), sem("hT_dve")
        cq_raw, cq_norm, v_copied, rope_mul = sem("cq_raw"), sem("cq_norm"), sem("v_copied"), sem("rope_mul")
        scored, att_masked, nmax_ready, probs_ready = (sem("scored"), sem("att_masked"), sem("nmax_ready"),
                                                       sem("probs_ready"))
        hf_ready, tree_arg = sem("hf_ready"), sem("tree_arg")
        tree_masked, intra_ready, state_ready = sem("tree_masked"), sem("intra_ready"), sem("state_ready")
        hg_mul, hg_ready, merge_read, merged_ready = (sem("hg_mul"), sem("hg_ready"), sem("merge_read"),
                                                      sem("merged_ready"))
        x1_ready, h2_ready, h2T_dve = sem("x1_ready"), sem("h2_ready"), sem("h2T_dve")
        route_arg, picked, placed, slots_ready = sem("route_arg"), sem("picked"), sem("placed"), sem("slots_ready")
        xgT_low, act_ready, y_dve, fin_dve = sem("xgT_low"), sem("act_ready"), sem("y_dve"), sem("fin_dve")
        actT_low = sem("actT_low")
        fin_args, fin_mean, lb_arg = sem("fin_args"), sem("fin_mean"), sem("lb_arg")
        x_mean, x_rooted = sem("x_mean"), sem("x_rooted")
        v_raw, y_low, logitsT_ready, logits_done = sem("v_raw"), sem("y_low"), sem("logitsT_ready"), sem("logits_done")
        low_ready, merged_sum, e_low_ready = sem("low_ready"), sem("merged_sum"), sem("e_low_ready")
        roped, qk_ready, xg_clear = sem("roped"), sem("qk_ready"), sem("xg_clear")
        slots_filled, tile_rows = sem("slots_filled"), sem("tile_rows")

        cur = [rt]

        def route(*shape):
            n = math.prod(shape)
            cur[0] += n
            return at(cur[0] - n, *shape)

        rowc = route(36 + 4 * 32)
        lg, le = route(NT, 8), route(NT, N_EXP)
        g8, gi8 = route(NT, 8), route(NT, 8).bitcast(U32)
        gneg, gsum, gexp, gidx = route(NT), route(NT), route(NT, 4), route(NT)
        gout = route(NT, 4)
        e8, ei8 = route(NT, 8), route(NT, 8).bitcast(U32)
        eidx = route(2, NT)
        diff, den, gate1, gate2 = route(NT), route(NT), route(NT), route(NT)
        pick = route(2, NT, N_EXP)
        both = route(NT, N_EXP)
        rank, count = route(NT, N_EXP), route(N_EXP)
        extra, upto, base, delta = route(N_EXP), route(N_EXP), route(N_EXP), route(N_EXP)
        pos, posp = route(NT, N_EXP), route(NT, N_EXP)
        slot = route(2, NT)
        assert cur[0] <= U + 12288
        cur = [U + 16384]
        slot_u = route(2 * NT).bitcast(U32)
        rows_u = route(2 * NT, 2).bitcast(U32)
        fill_u = route((TILES + 1) * R // P * 2).bitcast(U32)
        assert (TILES + 1) * R % P == 0
        table_u = route(TILES + 1, 2).bitcast(U32)
        gather_u, scatter_u = route(1).bitcast(U32), route(1).bitcast(U32)
        ctrl_f, ctrl_u = route(16), route(16).bitcast(U32)
        ones_e, passed = route(N_EXP), route(1)
        gate1k, gate2k = route(NT), route(NT)
        fsum, fmean = route(NT), route(NT)
        assert cur[0] <= TAB

        block = ctx.enter_context(nc.Block())

        def step_count(kind, n):
            return sum(s[0] == kind for s in STEPS[:n])

        att_fill = [2] + [0] * len(STEPS)
        for n, (kind, t, h) in enumerate(STEPS):
            if kind == "idx":
                continue
            elif t < 3:
                att_fill[n + 1] = {0: 6 if t == 0 else 5, 1: 8, 3: 1, 4: int(t == 2), 5: 1, 7: 1}.get(h, 0)
            else:
                att_fill[n + 1] = 2 - h % 2
        rec_fill = [6] + [3, 3, 2, 2] + [3, 3, 3, 3, 2, 2] * 2

        ATT_GATES, REC_GATES = ["ga0", "ga1", "ga2", "ga3"], [["gb0", "gb1", "gb2"], ["gb3", "hg0", "hg1"]]
        assert sum(att_fill) == KD * len(ATT_GATES) and sum(rec_fill) == KD * len(REC_GATES[0])

        def filled(fill, first, n):
            return PANEL[first][0] + sum(fill[:n + 1]) // CK

        def before_waiting(n):
            return PANEL["ga0"][0] + -(-sum(att_fill[:n + 2]) // CK) - SPLIT_SLOTS

        def next_splits(done):
            taken = sum(n < done for n in SPLIT)
            return sum(n < done + SLOTS for n in SPLIT[:taken + SPLIT_SLOTS])

        GATE_NO = {n: i for i, n in enumerate(["ga0", "ga1", "ga2", "ga3", "gb0", "gb1", "gb2", "gb3",
                                                     "hg0", "hg1"])}

        @block.sync
        def _(sp):
            def load(n, width, src):
                if n - SLOTS in SPLIT_NO:
                    sp.wait_ge(low_ready, SPLIT_NO[n - SLOTS] + 1)
                elif n >= SLOTS:
                    sp.wait_ge(chunks_done, n - SLOTS + 1)
                dst = at(RING + n % SLOTS * CHUNK, CK, width)
                sp.dma_start(dst, src.rearrange("(k p) n -> p k n", p=P)).then_inc(w_loaded[n % SLOTS], 16)

            col = {"cq": (w_in, C_CQ, 512), "misc": (w_in, C_K, MISC)}
            for b in range(4):
                if b < 2:
                    col[f"uq{b}"] = (w_uq, 512 * b, 512)
                    for name, c0 in (("hq", C_HQ), ("hf", C_HF), ("hi", C_HI), ("hg", C_HG)):
                        col[f"{name}{b}"] = (w_in, c0 + 512 * b, 512)
                col[f"qi{b}"] = (w_qidx, 512 * b, 512)
                col[f"ga{b}"], col[f"gb{b}"] = (w_in, C_GA + 512 * b, 512), (w_in, C_GB + 512 * b, 512)
                col[f"pa{b}"], col[f"pb{b}"] = (w_pa, 512 * b, 512), (w_pb, 512 * b, 512)
                col[f"wo{b}"] = (w_o, 512 * b, 512)
            for name, (start, chunks, _) in PANEL.items():
                w, c0, width = col[name]
                for g in range(chunks):
                    load(start + g, width, w[g * CK * P:(g + 1) * CK * P, c0:c0 + width])

            def expert_weights(tile, expert):
                for c in range(E_CHUNKS):
                    s = c % E_SLOTS
                    if isinstance(tile, int) and tile == 0 and c < E_SLOTS:
                        for r, v in ROOM[c]:
                            sp.wait_ge(r, v)
                    else:
                        sp.wait_ge(e_low_ready, tile * E_CHUNKS + (c - E_SLOTS + 1))
                    if c < 16:
                        w = w_gate if c < 8 else w_up
                        src = w[bass.ds(expert, 1), c % 8 * CK * P:(c % 8 + 1) * CK * P, :]
                    else:
                        cb, half = (c - 16) // 2, c % 2
                        src = w_down[bass.ds(expert, 1), half * CK * P:(half + 1) * CK * P, cb * 512:(cb + 1) * 512]
                    sp.dma_start(e_ring[s], src.rearrange("e (k p) n -> p (e k) n", p=P)).then_inc(e_loaded[s], 16)
                    if isinstance(tile, int) and c == E_SLOTS - 1:
                        sp.wait_ge(slots_written, 16 * 2 * NT)
                        sp.dma_start(table_u[0:R], slots_d.rearrange("(n p) c -> p n c", p=R)) \
                            .then_inc(slots_loaded, 16)
                        sp.wait_ge(xg_loaded, 16)

            ROOM = [[(low_ready, len(SPLIT))]] * 4 + [[(h2_ready, 4 * NT)]] * 2 + \
                [[(h2_stored, 48), (h2T_ps, KD)]] * 4 + [[(router_ps, KD)]] * 2
            expert_weights(0, 0)
            with sp.Fori(1, N_EXP) as tile:
                expert_weights(tile, tile)
            sp.wait_ge(slots_ready, 1)
            over = sp.value_load(ctrl_u[0:1, 0:1], min_val=0, max_val=TILES - OVER)
            with sp.If(over > 0):
                with sp.Fori(0, TILES - OVER) as i:
                    e = sp.value_load(ctrl_u[0:1, bass.ds(i + 1, 1)], min_val=0, max_val=N_EXP - 1)
                    expert_weights(i + OVER, e)
                sp.wait_ge(yb_sent, 16 * (1 + TILES))
                sp.wait_ge(xg_loaded, 16 * (1 + TILES))
            sp.wait_ge(yb_sent, 16 * (1 + N_EXP))
            sp.wait_ge(xg_loaded, 16 * (1 + N_EXP))
            for t in range(NT):
                sp.dma_start(yfin[t], y2_d[2 * P * t:2 * P * (t + 1), :].rearrange("(p c) d -> p c d", c=2)) \
                    .then_inc(yfin_loaded[t], 16)
            for t in range(NT):
                sp.wait_ge(fin_dve, t + 1)
                sp.dma_start(out[0, t * P:(t + 1) * P, :], x1[:, t, :]).then_inc(out_stored, 16)
            sp.wait_ge(out_stored, 16 * NT)

        @block.gpsimd
        def _(pool):
            pool.dma_start(mem[:, TAB:SMALL], t_const).then_inc(small_loaded, 16)
            pool.dma_start(mem[:, SMALL:SMALL + KD + 4 + 3 * G_HEADS], gains).then_inc(small_loaded, 16)
            pool.wait_ge(squared, 4)
            pool.dma_start(at(YATT, 2 * T), t_rope).then_inc(rope_loaded, 16)
            pool.dma_start(causal, t_causal).then_inc(causal_loaded, 16)

            outs = [kT, kiT] + [qT[:, h, :] for h in range(A_HEADS)] + [qiT[:, h, :] for h in range(IDX_HEADS)]
            for n, o in enumerate(outs):
                pool.wait_ge(rope_mul, n + 1)
                nc.gpsimd.tensor_tensor(o, rope_a[:, n % 2, :], rope_b[:, n % 2, :], ALU.add).then_inc(roped, 1)

            for n in range(16):
                b, f, pair = n // 8, n % 8 // 2, n % 2
                buf, tok = qk[n % 2], slice(pair * 256, pair * 256 + 256)
                pool.wait_ge(tree_exp, n + 1)
                for m in range(LEVELS):
                    h = P >> (m + 1)
                    v = buf[:, m, :].rearrange("p (b s h) -> p b s h", s=2, h=h)
                    q4 = hq[:, f, tok].rearrange("p (b s h) -> p b s h", s=2, h=h)
                    k4 = hk[:, f, tok].rearrange("p (b s h) -> p b s h", s=2, h=h)
                    nc.gpsimd.tensor_tensor(v[:, :, 1, :], v[:, :, 1, :], q4[:, :, 1, :], ALU.mult)
                    nc.gpsimd.tensor_tensor(v[:, :, 0, :], v[:, :, 0, :], k4[:, :, 0, :], ALU.mult)
                nc.gpsimd.tensor_tensor(buf[:, 7, :], buf[:, 7, :], hk[:, f, tok], ALU.mult)
                nc.gpsimd.tensor_tensor(buf[:, 8, :], buf[:, 8, :], hq[:, f, tok], ALU.mult).then_inc(qk_ready, 1)

            pool.wait_ge(x1_ready, 16)
            nc.gpsimd.memset(passed, 0.0)
            nc.gpsimd.memset(fill_u, NO_ROW).then_inc(slots_filled, 1)
            pool.wait_ge(slots_filled, 1)
            pool.dma_start(slots_d.rearrange("(p n) c -> p (n c)", p=P), fill_u).then_inc(slots_cleared, 16)
            pool.dma_start(rows_u, t_rows.rearrange("p (n c) -> p n c", c=2)).then_inc(slots_cleared, 16)
            pool.wait_ge(h2_ready, 3 * NT + 3)
            pool.dma_start(h2_d[2 * P:3 * P, :], h2[:, 2, :]).then_inc(yb_sent, 16)
            pool.wait_ge(h2T_ps, KD)
            pool.wait_ge(h2_stored, 48)
            pool.wait_ge(yb_sent, 16)
            nc.gpsimd.memset(xg, 0.0).then_inc(xg_clear, 1)
            pool.wait_ge(slots_cleared, 32)
            pool.wait_ge(placed, 1)
            for n in range(2 * NT):
                pool.indirect_dma_start(out=slots_d,
                                        out_offset=bass.IndirectOffsetOnAxis(ap=slot_u[:, n:n + 1], axis=0),
                                        in_=rows_u[:, n, :], in_offset=None).then_inc(slots_written, 16)
            pool.wait_ge(slots_loaded, 16)
            pool.wait_ge(xg_clear, 1)

            last_row, last_result = pool.to_reg(T - 1), pool.to_reg(2 * T - 1)

            def gather():
                pool.indirect_dma_start(out=xg, out_offset=None, in_=h2_d,
                                        in_offset=bass.IndirectOffsetOnAxis(ap=gather_u[0:R], axis=0),
                                        bounds_check=last_row, oob_is_err=False).then_inc(xg_loaded, 16)

            nc.gpsimd.tensor_copy(gather_u[0:R], table_u[0:R, 0:1, 0]).then_inc(tile_rows, 1)
            pool.wait_ge(tile_rows, 1)
            gather()

            def indices_ready(n):
                pool.wait_ge(tile_rows, n)
                nc.gpsimd.tensor_tensor(passed, passed, passed, ALU.mult).then_inc(tile_rows, 1)

            def send_tile(tile):
                pool.wait_ge(xgT_ps, tile * 2 + 2)
                nc.gpsimd.tensor_copy(gather_u[0:R], table_u[0:R, bass.ds(tile + 1, 1), 0]).then_inc(tile_rows, 1)
                indices_ready(tile * 4 + 2)
                gather()
                pool.wait_ge(yb_sent, tile * 16 + 16)
                pool.wait_ge(y_act, tile * 2 + 2)
                pool.wait_ge(y_dve, tile * 2 + 2)
                nc.gpsimd.tensor_copy(scatter_u[0:R], table_u[0:R, bass.ds(tile, 1), 1]).then_inc(tile_rows, 1)
                indices_ready(tile * 4 + 4)
                pool.indirect_dma_start(out=y2_d, out_offset=bass.IndirectOffsetOnAxis(ap=scatter_u[0:R], axis=0),
                                        in_=yb, in_offset=None,
                                        bounds_check=last_result, oob_is_err=False).then_inc(yb_sent, 16)

            with pool.Fori(0, N_EXP) as tile:
                send_tile(tile)
            over = pool.value_load(ctrl_u[0:1, 0:1], min_val=0, max_val=TILES - OVER)
            with pool.If(over > 0):
                with pool.Fori(0, TILES - OVER) as i:
                    send_tile(i + OVER)

        @block.tensor
        def _(pe):
            def chunk(n):
                if n not in SPLIT_NO:
                    pe.wait_ge(w_loaded[n % SLOTS], 16 * (n // SLOTS + 1))
                    return [ring[n % SLOTS]]
                m = SPLIT_NO[n]
                pe.wait_ge(low_ready, m + 1)
                return [part(w_high[m % SPLIT_SLOTS], CK, 512), part(w_low[m % SPLIT_SLOTS], CK, 512)]

            def pairs(w, x):
                return [(w[0], x[0]), (w[0], x[1]), (w[1], x[0])] if len(w) == 2 else [(w[0], x[0])]

            EMPTY = {
                "cq": [(hT_dve, 12)], "misc": [(hT_dve, 16)],
                "uq0": [(cq_norm, 4)], "uq1": [(rope_mul, 2), (v_copied, 2)],
                "qi0": [(rope_mul, 6)], "qi1": [(rope_mul, 10)], "qi2": [(rope_mul, 14)], "qi3": [(rope_mul, 18)],
                "ga0": [(rope_mul, 22)], "ga1": [(gate_sigmoid, 4)], "ga2": [(gate_sigmoid, 8)],
                "ga3": [(gate_sigmoid, 12)],
                "hq0": [(gate_sigmoid, 16)], "hf0": [(att_masked, ATT_N), (att_sb, ATT_N)],
                "hi0": [(hq_ready, 4)], "gb0": [(hv_sb, 4)], "gb1": [(gate_sigmoid, 20)],
                "gb2": [(gate_sigmoid, 24)],
                "hq1": [(gate_sigmoid, 28)], "hf1": [(tree_masked, 32), (state_ready, 12), (rec_sb, 4)],
                "hi1": [(hq_ready, 8)], "gb3": [(hv_sb, 8)], "hg0": [(gate_sigmoid, 32)],
                "hg1": [(gate_sigmoid, 36)], "pa0": [(tree_masked, 64), (state_ready, 24), (rec_sb, 8)],
                "pb0": [(gate_sigmoid, 40), (mean_ready, 2)],
            }
            for b in range(1, 4):
                EMPTY[f"pa{b}"], EMPTY[f"pb{b}"] = [(merge_read, 8 * b - 4)], [(merge_read, 8 * b)]
            EMPTY["wo0"], EMPTY["wo1"] = [(merge_read, 28)], [(merge_read, 32)]
            EMPTY["wo2"], EMPTY["wo3"] = [(x1_ready, 4)], [(x1_ready, 8)]

            def by_feature(name, rhs, ready=None):
                start, chunks, bank = PANEL[name]
                for s, v in EMPTY[name]:
                    pe.wait_ge(s, v - 3 if s is gate_sigmoid else v)
                for g in range(chunks):
                    w = chunk(start + g)
                    for s, v in (ready(g) if ready else []):
                        pe.wait_ge(s, v)
                    for kk in range(CK):
                        k = CK * g + kk
                        for f in range(4):
                            if k == 0 and f and EMPTY[name][0][0] is gate_sigmoid:
                                pe.wait_ge(gate_sigmoid, EMPTY[name][0][1] - 3 + f)
                            products = pairs(w, rhs)
                            for i, (ww, xx) in enumerate(products):
                                last = nc.tensor.matmul(banks[bank + f][:, :], lhsT=ww[:, kk, f * P:(f + 1) * P],
                                                        rhs=xx[:, k, :], start=k == 0 and i == 0,
                                                        stop=k == CK * chunks - 1 and i == len(products) - 1)
                        if kk == CK - 1:
                            last.then_inc(chunks_done, 1)
                        yield

            def by_token(name, lhs, ready=None):
                start, chunks, bank = PANEL[name]
                for s, v in EMPTY[name]:
                    pe.wait_ge(s, v)
                for g in range(chunks):
                    w = chunk(start + g)
                    for s, v in (ready(g) if ready else []):
                        pe.wait_ge(s, v)
                    for kk in range(CK):
                        k = CK * g + kk
                        for t in range(NT):
                            products = pairs(w, lhs)
                            for i, (ww, xx) in enumerate(products):
                                last = nc.tensor.matmul(banks[bank + t][:, :], lhsT=xx[:, k, t * P:(t + 1) * P],
                                                        rhs=ww[:, kk, :], start=k == 0 and i == 0,
                                                        stop=k == CK * chunks - 1 and i == len(products) - 1)
                    last.then_inc(chunks_done, 1)

            def finish(work):
                for _ in work:
                    pass

            def some(work, n):
                for _ in range(n):
                    next(work, None)

            pe.wait_ge(small_loaded, 16 * 2)
            for t in range(NT):
                pe.wait_ge(h_ready, t + 1)
                for k in range(8):
                    last = nc.tensor.transpose(banks[k][:, t * P:(t + 1) * P], xt[:, t, k * P:(k + 1) * P], ident)
                    if t == NT - 1:
                        last.then_inc(xT_ps, 1)
            for k in range(8, KD):
                pe.wait_ge(hT_dve, k - 7)
                for t in range(NT):
                    last = nc.tensor.transpose(banks[k % 8][:, t * P:(t + 1) * P], xt[:, t, k * P:(k + 1) * P], ident)
                last.then_inc(xT_ps, 1)

            finish(by_feature("cq", hT, lambda g: [(hT_dve, CK * g + CK)]))

            start, _, _ = PANEL["misc"]
            for s, v in EMPTY["misc"]:
                pe.wait_ge(s, v)
            for g in range(KD // CK):
                chunk(start + g)
                slot = SPLIT_NO[start + g] % SPLIT_SLOTS
                w = [part(w_high[slot], CK, MISC), part(w_low[slot], CK, MISC)]
                for kk in range(CK):
                    k = CK * g + kk
                    for i, (ww, xx) in enumerate(pairs(w, hT)):
                        first, end = k == 0 and i == 0, k == KD - 1 and i == 2
                        nc.tensor.matmul(banks[4][:, :], lhsT=ww[:, kk, 0:P], rhs=xx[:, k, :], start=first, stop=end)
                        nc.tensor.matmul(banks[5][:, :], lhsT=ww[:, kk, 2 * P:3 * P], rhs=xx[:, k, :],
                                         start=first, stop=end)
                        nc.tensor.matmul(banks[6][:, :], lhsT=ww[:, kk, P:2 * P], rhs=xx[:, k, :], start=first,
                                         stop=end)
                        last = nc.tensor.matmul(banks[7][0:IDX_HEADS, :], lhsT=ww[:, kk, 3 * P:3 * P + IDX_HEADS],
                                                rhs=xx[:, k, :], start=first, stop=end)
                last.then_inc(chunks_done, 1)
                if g == 3:
                    pe.wait_ge(cq_squared, 4)
                    for f in range(4):
                        last = nc.tensor.matmul(banks[0][:, :], lhsT=ones, rhs=cq_sq[:, f, :],
                                                start=f == 0, stop=f == 3)
                    last.then_inc(ssq_ps, 1)

            uq0 = by_feature("uq0", [cqT])
            some(uq0, 1)
            pe.wait_ge(v_raw, 2)
            for bank, rows in ((6, vT), (7, wiT)):
                for t in range(NT):
                    last = nc.tensor.transpose(banks[bank][:, t * P:(t + 1) * P], rows[:, t * P:(t + 1) * P], ident)
            last.then_inc(v_ps, 1)
            finish(uq0)
            for name in ("uq1", "qi0", "qi1", "qi2", "qi3"):
                finish(by_feature(name, [cqT]))

            def gates(names):
                for name in names:
                    yield from by_feature(name, hT)

            filler = gates(ATT_GATES)
            m = 0

            def transpose_probs(m, t):
                pe.wait_ge(probs_ready, m + 1)
                if m >= 1:
                    pe.wait_ge(probsT_sb, m)
                for s in range(t + 1):
                    last = nc.tensor.transpose(banks[6][:, s * P:(s + 1) * P], probs[:, m % 2, s * P:(s + 1) * P],
                                               ident)
                last.then_inc(probsT_ps, 1)

            def values(m, t):
                pe.wait_ge(probsT_sb, m + 1)
                if m >= 1:
                    pe.wait_ge(att_sb, m)
                for s in range(t + 1):
                    last = nc.tensor.matmul(banks[7][:, 0:P], lhsT=vtok[:, s, :],
                                            rhs=probsT[:, m % 2, s * P:(s + 1) * P], start=s == 0, stop=s == t)
                last.then_inc(att_ps, 1)

            att_tile = [s[1] for s in STEPS if s[0] == "att"]
            some(filler, att_fill[0])
            pe.wait_ge(roped, 2 + A_HEADS + IDX_HEADS)
            for n, (kind, t, h) in enumerate(STEPS):
                if n >= 2:
                    if STEPS[n - 2][0] == "idx":
                        pe.wait_ge(relu_done, step_count("idx", n - 1))
                    else:
                        pe.wait_ge(att_masked, step_count("att", n - 1))
                keys, q, kk = (t + 1) * P, (qiT if kind == "idx" else qT), (kiT if kind == "idx" else kT)
                nc.tensor.matmul(banks[4 + n % 2][:, 0:keys], lhsT=q[:, h, t * P:(t + 1) * P], rhs=kk[:, 0:keys],
                                 start=True, stop=True).then_inc(logits_ps, 1)
                some(filler, att_fill[n + 1])
                if kind == "att":
                    if m >= 1:
                        transpose_probs(m - 1, att_tile[m - 1])
                    if m >= 2:
                        values(m - 2, att_tile[m - 2])
                    m += 1
            transpose_probs(m - 1, att_tile[m - 1])
            values(m - 2, att_tile[m - 2])
            values(m - 1, att_tile[m - 1])
            finish(filler)

            for b in range(2):
                finish(by_feature(f"hq{b}", hT))
                finish(by_feature(f"hf{b}", hT))
                by_token(f"hi{b}", hT)
                filler = gates(REC_GATES[b])
                some(filler, rec_fill[0])
                pe.wait_ge(hf_sigmoid, 4 * (b + 1))
                pe.wait_ge(hv_sb, 4 * (b + 1))

                def outputs(n):
                    f, c = n % 16 // 4, n % 4
                    pe.wait_ge(intra_ready, n + 1)
                    if c == 0 and n >= 4:
                        pe.wait_ge(rec_sb, n // 4)
                    last = nc.tensor.matmul(banks[7][:, c * P:(c + 1) * P], lhsT=hv[:, c, f * P:(f + 1) * P],
                                            rhs=intra[:, n % 2, :], start=True, stop=c == 0)
                    if c:
                        pe.wait_ge(state_ready, n // 4 * 3 + c)
                        last = nc.tensor.matmul(banks[7][:, c * P:(c + 1) * P], lhsT=state[:, c % 2, :],
                                                rhs=qk[n // 2 % 2][:, 8, n % 2 * P:(n % 2 + 1) * P],
                                                start=False, stop=True)
                    last.then_inc(rec_ps, 1)

                for i in range(16):
                    n = 16 * b + i
                    f, c = i // 4, i % 4
                    buf, tok = qk[n // 2 % 2], slice(n % 2 * P, (n % 2 + 1) * P)
                    pe.wait_ge(qk_ready, n // 2 + 1)
                    pe.wait_ge(hf_ready, b + 1)
                    if n >= 1:
                        pe.wait_ge(tree_masked, 2 * n)
                    for m in range(4):
                        last = nc.tensor.matmul(banks[4][:, m * P:(m + 1) * P], lhsT=buf[:, m, tok],
                                                rhs=buf[:, m, tok], start=True, stop=True)
                    last.then_inc(tree_ps, 1)
                    for m in range(4, LEVELS):
                        nc.tensor.matmul(banks[5][:, (m - 4) * P:(m - 3) * P], lhsT=buf[:, m, tok],
                                         rhs=buf[:, m, tok], start=True, stop=True)
                    nc.tensor.matmul(banks[5][:, 3 * P:4 * P], lhsT=hk[:, f, c * P:(c + 1) * P],
                                     rhs=hq[:, f, c * P:(c + 1) * P], start=True, stop=True).then_inc(tree_ps, 1)
                    if c < 3:
                        if n // 4 * 3 + c >= 1:
                            pe.wait_ge(state_ready, n // 4 * 3 + c)
                        nc.tensor.transpose(banks[6][:, 0:P], buf[:, 7, tok], ident).then_inc(keT_ps, 1)
                    if i >= 1:
                        outputs(n - 1)
                    some(filler, rec_fill[i + 1])
                    if c < 3:
                        pe.wait_ge(keT_sb, n // 4 * 3 + c + 1)
                        nc.tensor.matmul(banks[6][:, 0:P], lhsT=keT[:, n % 2, :], rhs=hv[:, c, f * P:(f + 1) * P],
                                         start=True, stop=True).then_inc(state_ps, 1)
                outputs(16 * b + 15)
                finish(filler)

            attended, recurred = [y[:, 0:8, :] for y in yT], [y[:, 8:16, :] for y in yT]

            def branch(name, y, first):
                return by_feature(name, y, (lambda g: [(y_low, first + CK * g + CK)]) if name[2] == "0" else None)

            pa0 = branch("pa0", attended, 0)
            some(pa0, 2)
            pe.wait_ge(rec_squared, G_HEADS)
            pe.wait_ge(gate_sigmoid, 37)
            for h in range(G_HEADS):
                last = nc.tensor.matmul(banks[0][:, :], lhsT=ones, rhs=at(U + h * T, T), start=h == 0,
                                        stop=h == G_HEADS - 1)
            last.then_inc(recsq_ps, 1)
            finish(pa0)

            for b in range(4):
                if b:
                    finish(branch(f"pa{b}", attended, 0))
                finish(branch(f"pb{b}", recurred, 8))
            for b in range(4):
                by_token(f"wo{b}", mergedT, (lambda g: [(merged_ready, CK * g + CK)]) if b == 0 else None)

            def wait_copied(k):
                if k < 4:
                    pe.wait_ge(h2T_act, k + 1)
                elif k % 2:
                    pe.wait_ge(h2T_act, 4 + (k - 4) // 2 + 1)
                else:
                    pe.wait_ge(h2T_dve, (k - 4) // 2 + 1)

            def router(k):
                wait_copied(k)
                nc.tensor.matmul(banks[4][0:36, :], lhsT=wr[:, k, :], rhs=h2T[:, k % 4, :], start=k == 0,
                                 stop=k == KD - 1).then_inc(router_ps, 1)

            pe.wait_ge(late_loaded, 16 * 5)
            pe.wait_ge(x1_ready, 16)
            for k in range(KD):
                if k >= 4:
                    wait_copied(k - 4)
                for t in range(NT):
                    if k % 4 == 0:
                        pe.wait_ge(h2_ready, k + t + 1)
                    last = nc.tensor.transpose(banks[k % 4][:, t * P:(t + 1) * P], h2[:, t, k * P:(k + 1) * P], ident)
                last.then_inc(h2T_ps, 1)
                if k >= 2:
                    router(k - 2)
            router(KD - 2)
            router(KD - 1)
            pe.wait_ge(logitsT_ready, 2)
            for t in range(NT):
                last = nc.tensor.transpose(banks[5][:, t * P:(t + 1) * P], logitsT[:, t * P:(t + 1) * P], ident)
            last.then_inc(logits_done, 1)
            pe.wait_ge(picked, 1)
            for t in range(NT):
                for u in range(t + 1):
                    last = nc.tensor.matmul(banks[1][:, t * N_EXP:(t + 1) * N_EXP], lhsT=before if u == t else ones,
                                            rhs=both[:, u, :], start=u == 0, stop=u == t)
            for u in range(NT):
                last = nc.tensor.matmul(banks[1][:, NT * N_EXP:(NT + 1) * N_EXP], lhsT=ones, rhs=both[:, u, :],
                                        start=u == 0, stop=u == NT - 1)
            last.then_inc(rank_ps, 1)

            def transpose_r(bank, i, rows):
                n = P if i == 0 else R
                return nc.tensor.transpose(bank[:, i * R:i * R + n], rows[0:n], ident[0:n, 0:n])

            def transpose_rows(tile, g):
                for kk in range(8):
                    k = 8 * g + kk
                    last = transpose_r(banks[2 + g], kk, xg_all[:, k * P:(k + 1) * P])
                last.then_inc(xgT_ps, 1)

            def products(bank, x, k, slot, kk, ks):
                both = pairs([e_high[slot], e_low[slot]], x)
                for i, (ww, xx) in enumerate(both):
                    last = nc.tensor.matmul(banks[bank][0:R, :], lhsT=xx[:, k, :], rhs=ww[:, kk, :],
                                            start=k == 0 and i == 0, stop=k == ks - 1 and i == len(both) - 1)
                return last

            def expert_tile(tile):
                for c in range(16):
                    pe.wait_ge(e_low_ready, tile * E_CHUNKS + (c + 1))
                    if c in (0, 4):
                        pe.wait_ge(xgT_low, tile * 2 + (c // 4 + 1))
                    for kk in range(CK):
                        last = products(c // 8, xgT, CK * (c % 8) + kk, c % E_SPLIT_SLOTS, kk, KD)
                    last.then_inc(e_done, 1)
                pe.wait_ge(xg_loaded, tile * 16 + 32)
                transpose_rows(tile + 1, 0)
                pe.wait_ge(act_ready, tile + 1)
                for f in range(4):
                    last = transpose_r(banks[0], f, act_all[:, f * P:(f + 1) * P])
                last.then_inc(actT_ps, 1)
                transpose_rows(tile + 1, 1)
                pe.wait_ge(actT_low, tile + 1)
                for c in range(16, E_CHUNKS):
                    pe.wait_ge(e_low_ready, tile * E_CHUNKS + (c + 1))
                    for kk in range(CK):
                        last = products(4 + (c - 16) // 2, actT, CK * (c % 2) + kk, c % E_SPLIT_SLOTS, kk, 4)
                    last.then_inc(e_done, 1)

            pe.wait_ge(xg_loaded, 16)
            for g in range(2):
                transpose_rows(0, g)
            with pe.Fori(0, N_EXP) as tile:
                expert_tile(tile)
            over = pe.value_load(ctrl_u[0:1, 0:1], min_val=0, max_val=TILES - OVER)
            with pe.If(over > 0):
                with pe.Fori(0, TILES - OVER) as i:
                    expert_tile(i + OVER)

        @block.scalar
        def _(act):
            halves = [0]

            def split_before(done):
                for m in range(halves[0], next_splits(done)):
                    n = SPLIT[m]
                    width = CK * (MISC if PANEL["misc"][0] <= n < PANEL["uq0"][0] else 512)
                    act.wait_ge(w_loaded[n % SLOTS], 16 * (n // SLOTS + 1))
                    if m >= SPLIT_SLOTS:
                        act.wait_ge(chunks_done, SPLIT[m - SPLIT_SLOTS] + 1)
                    nc.scalar.activation(parts[:, w_high[m % SPLIT_SLOTS]:w_high[m % SPLIT_SLOTS] + width],
                                         at(RING + n % SLOTS * CHUNK, width), ACT.Copy).then_inc(high_ready, 1)
                    halves[0] = m + 1

            for t in range(NT):
                act.dma_start(xt[:, t, :], x[0, t * P:(t + 1) * P, :]).then_inc(x_loaded[t], 16)
            def root(t):
                act.wait_ge(x_mean, t + 1)
                nc.scalar.activation(mean[:, t:t + 1], mean[:, t:t + 1], ACT.Sqrt).then_inc(x_rooted, 1)

            for t in range(NT):
                act.wait_ge(x_loaded[t], 16)
                nc.scalar.activation(junk[:, t, :], xt[:, t, :], ACT.Square, accum_out=ssum[:, t:t + 1]) \
                    .then_inc(squared, 1)
                if t:
                    root(t - 1)
            root(NT - 1)
            split_before(0)
            act.wait_ge(small_loaded, 16 * 2)
            for k in range(KD):
                act.wait_ge(xT_ps, k + 1)
                nc.scalar.activation(hT[0][:, k, :], banks[k % 8][:, :], ACT.Copy, scale=g1c[:, k:k + 1]) \
                    .then_inc(hT_act, 1)
            for done in range(1, PANEL["cq"][1] + 1):
                split_before(done)
            act.wait_ge(lb_arg, 1)
            nc.scalar.activation(lb, lb, ACT.Exp).then_inc(lb_exp, 1)
            for f in range(4):
                act.wait_ge(cq_raw, f + 1)
                nc.scalar.activation(cq_sq[:, f, :], cqT[:, f, :], ACT.Square).then_inc(cq_squared, 1)
            split_before(PANEL["misc"][0] + 4)
            act.wait_ge(mean_ready, 1)
            nc.scalar.activation(cq_rms, cq_rms, ACT.Sqrt).then_inc(rooted, 1)

            def gate_panel(name):
                start, chunks, bank = PANEL[name]
                n = GATE_NO[name]
                split_before(start + chunks)
                act.wait_ge(chunks_done, start + chunks)
                if n:
                    act.wait_ge(gate_stored, 16 * n)
                for f in range(4):
                    nc.scalar.activation(stage[:, f, :], banks[bank + f][:, :],
                                         ACT.Silu if name[:2] == "hg" else ACT.Sigmoid).then_inc(gate_sigmoid, 1)
                act.wait_ge(gate_sigmoid, 4 * (n + 1))
                act.dma_start(gates_d[n], at(U + 15872, PANEL_GATE)).then_inc(gate_stored, 16)

            waiting = []

            def keep_up(done):
                while waiting and sum(PANEL[waiting[0]][:2]) <= done:
                    gate_panel(waiting.pop(0))
                split_before(done)

            waiting += ATT_GATES
            i_n = m = 0

            def copy_probs(m, t):
                act.wait_ge(probsT_ps, m + 1)
                if m >= 2:
                    act.wait_ge(att_ps, m - 1)
                nc.scalar.activation(probsT[:, m % 2, 0:(t + 1) * P], banks[6][:, 0:(t + 1) * P], ACT.Copy) \
                    .then_inc(probsT_sb, 1)

            def copy_att(m, t, h):
                act.wait_ge(att_ps, m + 1)
                nc.scalar.activation(yattT[:, h, t * P:(t + 1) * P], banks[7][:, 0:P], ACT.Copy).then_inc(att_sb, 1)

            att = [s for s in STEPS if s[0] == "att"]
            for n, (kind, t, h) in enumerate(STEPS):
                keys = (t + 1) * P
                keep_up(filled(att_fill, "ga0", n))
                if kind == "idx":
                    act.wait_ge(logits_ps, n + 1)
                    if i_n >= 2:
                        act.wait_ge(scored, i_n - 1)
                    nc.scalar.activation(relu[:, i_n % 2, 0:keys], banks[4 + n % 2][:, 0:keys], ACT.Relu) \
                        .then_inc(relu_done, 1)
                    i_n += 1
                else:
                    if h == 0 and t < 3:
                        for k in range(2):
                            keep_up(before_waiting(n + k))
                    act.wait_ge(nmax_ready, m + 1)
                    if m >= 2:
                        act.wait_ge(probsT_ps, m - 1)
                    nc.scalar.activation(probs[:, m % 2, 0:keys], masked[:, m % 2, 0:keys], ACT.Exp,
                                         bias=nmax[:, m:m + 1], scale=HEAD_D ** -0.5,
                                         accum_out=rsum[:, m:m + 1]).then_inc(exp_done, 1)
                    keep_up(filled(att_fill, "ga0", n + 1))
                    if m >= 1:
                        copy_probs(m - 1, att[m - 1][1])
                    if m >= 2:
                        copy_att(m - 2, att[m - 2][1], att[m - 2][2])
                    m += 1
            copy_probs(m - 1, att[m - 1][1])
            copy_att(m - 2, att[m - 2][1], att[m - 2][2])
            copy_att(m - 1, att[m - 1][1], att[m - 1][2])
            keep_up(filled(att_fill, "ga0", len(STEPS)))

            def tree_exps(u):
                f, pair = u % 8 // 2, u % 2
                buf = qk[u % 2]
                act.wait_ge(tree_arg, u + 1)
                nc.scalar.activation(buf[:, 0:8, :], buf[:, 0:8, :], ACT.Exp)
                nc.scalar.activation(buf[:, 8, :], hc[:, f, pair * 256:pair * 256 + 256], ACT.Exp)
                ends_at = hc[:, f, pair * 256:pair * 256 + 256].rearrange("p (c t) -> p c t", c=2)[:, :, P - 1]
                nc.scalar.activation(decay[:, u % 2 * 2:u % 2 * 2 + 2], ends_at, ACT.Exp).then_inc(tree_exp, 1)

            for b in range(2):
                start, chunks, bank = PANEL[f"hq{b}"]
                split_before(start + chunks)
                act.wait_ge(chunks_done, start + chunks)
                for f in range(4):
                    nc.scalar.activation(hq[:, f, :], banks[bank + f][:, :], ACT.Silu).then_inc(hq_ready, 1)
                start, chunks, bank = PANEL[f"hf{b}"]
                split_before(start + chunks)
                act.wait_ge(chunks_done, start + chunks)
                for f in range(4):
                    nc.scalar.activation(hk[:, f, :], banks[bank + f][:, :], ACT.Sigmoid).then_inc(hf_sigmoid, 1)
                for done in range(3):
                    split_before(PANEL[f"hi{b}"][0] + done)
                act.wait_ge(hf_ready, b + 1)
                nc.scalar.activation(hc, hc, ACT.Ln).then_inc(hf_ln, 1)
                start, chunks, bank = PANEL[f"hi{b}"]
                split_before(start + chunks)
                act.wait_ge(chunks_done, start + chunks)
                for t in range(NT):
                    nc.scalar.activation(hv[:, t, :], banks[bank + t][:, :], ACT.Copy).then_inc(hv_sb, 1)
                waiting += REC_GATES[b]
                tree_exps(8 * b)

                def copy_rec(h):
                    act.wait_ge(rec_ps, 4 * h + 4)
                    nc.scalar.activation(yrecT[:, h, :], banks[7][:, :], ACT.Copy).then_inc(rec_sb, 1)

                for i in range(16):
                    n = 16 * b + i
                    keep_up(filled(rec_fill, REC_GATES[b][0], i))
                    if n % 4 < 3:
                        act.wait_ge(keT_ps, n // 4 * 3 + n % 4 + 1)
                        nc.scalar.activation(keT[:, n % 2, :], banks[6][:, 0:P], ACT.Copy).then_inc(keT_sb, 1)
                    if i % 4 == 0 and i:
                        copy_rec(n // 4 - 1)
                    if i % 2 == 0 and i < 14:
                        tree_exps(n // 2 + 1)
                copy_rec(4 * b + 3)
                if b == 0:
                    keep_up(filled(rec_fill, REC_GATES[b][0], 16))

            def load_gates(b):
                act.dma_start(at(U + 8192, PANEL_GATE), gates_d[b]).then_inc(gate_loaded, 16)
                act.dma_start(at(U + 10240, PANEL_GATE), gates_d[4 + b]).then_inc(gate_loaded, 16)

            def output_high(k, src):
                nc.scalar.activation(yT[0][:, k, :], src, ACT.Copy).then_inc(y_high, 1)

            act.wait_ge(chunks_done, PANEL["pa0"][0])
            act.wait_ge(att_sb, ATT_N)
            for h in range(A_HEADS):
                if h == 2:
                    keep_up(PANEL["pa0"][0])
                output_high(h, yattT[:, h, :])
            for h in range(G_HEADS):
                act.wait_ge(rec_sb, h + 1)
                nc.scalar.activation(at(U + h * T, T), yrecT[:, h, :], ACT.Square).then_inc(rec_squared, 1)
            split_before(PANEL["pa0"][0] + 1)
            act.wait_ge(gate_stored, 16 * 10)
            for b in range(2):
                act.dma_start(at(U + 4096 + b * PANEL_GATE, PANEL_GATE), gates_d[8 + b]).then_inc(hg_loaded[b], 16)
            load_gates(0)
            act.wait_ge(mean_ready, 2)
            nc.scalar.activation(lev[:, 0:T], lev[:, 0:T], ACT.Sqrt).then_inc(rooted, 1)
            split_before(PANEL["pa0"][0] + 3)
            for h in range(G_HEADS):
                if h == 2:
                    split_before(PANEL["pb0"][0])
                act.wait_ge(hg_ready, h + 1)
                output_high(A_HEADS + h, yrecT[:, h, :])
            act.wait_ge(hg_ready, 8)
            act.dma_start(g2b, g_norm2[0].partition_broadcast(P)).then_inc(late_loaded, 16)
            act.dma_start(gfb, g_final.partition_broadcast(P)).then_inc(late_loaded, 16)
            for b in range(4):
                if b:
                    split_before(PANEL[f"pa{b}"][0])
                    act.wait_ge(merged_sum, 4 * b)
                    load_gates(b)
                if b == 0:
                    act.wait_ge(y_low, 16)
                else:
                    act.dma_start(x1[:, b - 1, :], x[0, (b - 1) * P:b * P, :]).then_inc(x_loaded[b - 1], 16)
            act.dma_start(x1[:, 3, :], x[0, 3 * P:4 * P, :]).then_inc(x_loaded[3], 16)
            split_before(PANEL["pb3"][0])
            act.wait_ge(chunks_done, PANEL["pb3"][0])
            for k in range(KD):
                if k == 4:
                    split_before(PANEL["pb3"][0] + 1)
                if k == 8:
                    split_before(PANEL["wo0"][0])
                    act.wait_ge(chunks_done, PANEL["wo0"][0])
                act.wait_ge(merged_sum, k + 1)
                nc.scalar.activation(mergedT[0][:, k, :], mT[:, k, :], ACT.Copy).then_inc(merged_high, 1)
            act.wait_ge(merged_sum, 16)
            act.dma_start(wr[:, :, 0:N_GROUPS], w_grp[0].rearrange("(k p) n -> p k n", p=P)).then_inc(late_loaded, 16)
            act.dma_start(wr[:, :, N_GROUPS:36], w_exp[0].rearrange("(k p) n -> p k n", p=P)).then_inc(late_loaded, 16)
            act.dma_start(rowc[:, 36:36 + 4 * 32], t_route).then_inc(late_loaded, 16)
            act.dma_start(rowc[:, 0:N_GROUPS], b_grp[0].partition_broadcast(P)).then_inc(late_loaded, 16)
            act.dma_start(rowc[:, N_GROUPS:36], b_exp[0].partition_broadcast(P)).then_inc(late_loaded, 16)
            for b in range(4):
                for done in range(PANEL[f"wo{b}"][0], sum(PANEL[f"wo{b}"][:2]) + 1):
                    split_before(done)
                for t in range(NT):
                    act.wait_ge(x1_ready, NT * b + t + 1)
                    cols = slice(b * 512, (b + 1) * 512)
                    nc.scalar.activation(h2[:, t, cols], x1[:, t, cols], ACT.Square,
                                         accum_out=ssum_parts[:, t, b:b + 1]).then_inc(squared, 1)
            act.wait_ge(mean_ready, 3)
            nc.scalar.activation(mean, mean, ACT.Sqrt).then_inc(rooted, 1)
            for k in (0, 1, 2, 3, *range(5, KD, 2)):
                if k == 5:
                    for t in (0, 1, 3):
                        act.wait_ge(h2_ready, 3 * NT + t + 1)
                        act.dma_start(h2_d[t * P:(t + 1) * P, :], h2[:, t, :]).then_inc(h2_stored, 16)
                act.wait_ge(h2T_ps, k + 1)
                if k >= 4:
                    act.wait_ge(router_ps, k - 3)
                nc.scalar.activation(h2T[:, k % 4, :], banks[k % 4][:, :], ACT.Copy).then_inc(h2T_act, 1)
            act.wait_ge(route_arg, 1)
            for t in range(NT):
                nc.scalar.activation(gexp[:, t, :], lg[:, t, 0:4], ACT.Exp, bias=gneg[:, t:t + 1],
                                     accum_out=gsum[:, t:t + 1]).then_inc(route_exp, 1)
            act.wait_ge(route_arg, 2)
            nc.scalar.activation(diff, diff, ACT.Exp).then_inc(route_exp, 1)

            def transposed_rows(tile, g):
                act.wait_ge(xgT_ps, tile * 2 + (g + 1))
                nc.scalar.activation(xgT[0][:, 8 * g:8 * g + 8, :],
                                     banks[2 + g][:, :].rearrange("p (k n) -> p k n", k=8), ACT.Copy) \
                    .then_inc(xgT_high, 1)

            def split_chunks_of(tile, first, end, last=False):
                for c in range(first, min(end, E_CHUNKS) if last else end):
                    this, cc = (tile, c) if c < E_CHUNKS else (tile + 1, c - E_CHUNKS)
                    act.wait_ge(e_loaded[cc % E_SLOTS],
                                this * 16 * (E_CHUNKS // E_SLOTS) + 16 * (cc // E_SLOTS + 1))
                    if not (isinstance(this, int) and this == 0 and cc < E_SPLIT_SLOTS):
                        act.wait_ge(e_done, this * E_CHUNKS + (cc - E_SPLIT_SLOTS + 1))
                    nc.scalar.activation(e_high[cc % E_SPLIT_SLOTS], e_ring[cc % E_SLOTS], ACT.Copy) \
                        .then_inc(e_high_ready, 1)

            def expert_tile(tile, last=False):
                used = tile * E_CHUNKS
                split_chunks_of(tile, E_SPLIT_SLOTS, 8 + AHEAD)
                act.wait_ge(e_done, used + 8)
                nc.scalar.activation(act_e, banks[0][0:R, :], ACT.Silu).then_inc(silu_done, 1)
                split_chunks_of(tile, 8 + AHEAD, 16 + AHEAD)
                transposed_rows(tile + 1, 0)
                act.wait_ge(actT_ps, tile + 1)
                nc.scalar.activation(actT[0], banks[0][:, 0:4 * R].rearrange("p (k n) -> p k n", k=4), ACT.Copy) \
                    .then_inc(actT_high, 1)
                transposed_rows(tile + 1, 1)
                act.wait_ge(yb_sent, tile * 16 + 16)
                for cb in range(4):
                    split_chunks_of(tile, 16 + 2 * cb + AHEAD, 16 + 2 * cb + 2 + AHEAD, last)
                    if cb % 2 == 0:
                        act.wait_ge(e_done, used + (16 + 2 * cb + 2))
                        nc.scalar.activation(yb[:, cb * 512:(cb + 1) * 512], banks[4 + cb][0:R, :], ACT.Copy) \
                            .then_inc(y_act, 1)
                split_chunks_of(tile, E_CHUNKS + AHEAD, E_CHUNKS + E_SPLIT_SLOTS, last)

            act.wait_ge(chunks_done, FRONT)
            split_chunks_of(0, 0, E_SPLIT_SLOTS)
            for g in range(2):
                transposed_rows(0, g)
            with act.Fori(0, N_EXP - 1) as tile:
                expert_tile(tile)
            expert_tile(N_EXP - 1, True)
            over = act.value_load(ctrl_u[0:1, 0:1], min_val=0, max_val=TILES - OVER)
            with act.If(over > 0):
                split_chunks_of(OVER, 0, E_SPLIT_SLOTS)
                with act.Fori(0, TILES - OVER - 1) as i:
                    expert_tile(i + OVER)
                expert_tile(TILES - 1, True)
            for t in range(NT):
                act.wait_ge(fin_args, t + 1)
                nc.scalar.activation(yfin[t][:, 0, :], x1[:, t, :], ACT.Square, accum_out=fsum[:, t:t + 1]) \
                    .then_inc(squared, 1)
                act.wait_ge(fin_mean, t + 1)
                nc.scalar.activation(fmean[:, t:t + 1], fmean[:, t:t + 1], ACT.Sqrt).then_inc(fin_act, 1)

        @block.vector
        def _(dve):
            V = nc.vector
            seq = [0]

            def then(ins):
                seq[0] += 1
                ins.then_inc(v_seq, 1)
                dve.wait_ge(v_seq, seq[0])

            def here(ins, s, n):
                ins.then_inc(s, 1)
                dve.wait_ge(s, n)

            halves = [0]

            def split_before(done):
                for m in range(halves[0], next_splits(done)):
                    n = SPLIT[m]
                    width = CK * (MISC if PANEL["misc"][0] <= n < PANEL["uq0"][0] else 512)
                    high = parts[:, w_high[m % SPLIT_SLOTS]:w_high[m % SPLIT_SLOTS] + width]
                    low = parts[:, w_low[m % SPLIT_SLOTS]:w_low[m % SPLIT_SLOTS] + width]
                    dve.wait_ge(high_ready, m + 1)
                    V.tensor_tensor(low, at(RING + n % SLOTS * CHUNK, width), high.bitcast(F32), ALU.subtract) \
                        .then_inc(low_ready, 1)
                    halves[0] = m + 1

            for t in range(NT):
                dve.wait_ge(squared, t + 1)
                V.tensor_scalar(mean[:, t:t + 1], ssum[:, t:t + 1], 1.0 / D, EPS, ALU.mult, ALU.add) \
                    .then_inc(x_mean, 1)
                dve.wait_ge(x_rooted, t + 1)
                then(V.reciprocal(rinv[:, t:t + 1], mean[:, t:t + 1]))
                V.tensor_scalar(xt[:, t, :], xt[:, t, :], rinv[:, t:t + 1], None, ALU.mult).then_inc(h_ready, 1)
            dve.wait_ge(small_loaded, 16 * 2)
            split_before(0)
            for k in range(KD):
                dve.wait_ge(hT_act, k + 1)
                V.scalar_tensor_tensor(out=hT[1][:, k, :], in0=banks[k % 8][:, :], scalar=g1c[:, k:k + 1],
                                       in1=hT[0][:, k, :].bitcast(F32), op0=ALU.mult, op1=ALU.subtract) \
                    .then_inc(hT_dve, 1)
            V.tensor_tensor(lb, lbx[:, 8:16], lbx[:, 0:8], ALU.subtract).then_inc(lb_arg, 1)
            for done in range(1, PANEL["cq"][1] + 1):
                split_before(done)
            dve.wait_ge(chunks_done, PANEL["cq"][1])
            for f in range(4):
                V.tensor_copy(cqT[:, f, :], banks[f][:, :]).then_inc(cq_raw, 1)
            split_before(PANEL["misc"][0] + 4)
            dve.wait_ge(ssq_ps, 1)
            V.tensor_scalar(cq_rms, banks[0][:, :], 1.0 / Q_RANK, EPS, ALU.mult, ALU.add).then_inc(mean_ready, 1)
            dve.wait_ge(rooted, 1)
            then(V.reciprocal(cq_rms, cq_rms))
            for f in range(4):
                V.scalar_tensor_tensor(out=cqT[:, f, :], in0=cqT[:, f, :], scalar=gqc[:, f:f + 1], in1=cq_rms,
                                       op0=ALU.mult, op1=ALU.mult).then_inc(cq_norm, 1)

            dve.wait_ge(rope_loaded, 16)
            turned = [0]

            def rope(ps):
                n = turned[0]
                turned[0] += 1
                if n >= 2:
                    dve.wait_ge(roped, n - 1)
                V.tensor_tensor(rope_a[:, n % 2, :], ps[:, :], cos2, ALU.mult)
                V.tensor_tensor(rope_b[0:64, n % 2, :], ps[64:128, :], sin2[64:128, :], ALU.mult)
                V.tensor_tensor(rope_b[64:128, n % 2, :], ps[0:64, :], sin2[0:64, :], ALU.mult).then_inc(rope_mul, 1)

            split_before(PANEL["uq0"][0])
            dve.wait_ge(chunks_done, PANEL["uq0"][0])
            rope(banks[4])
            rope(banks[5])
            V.memset(wiT, 0.0).then_inc(v_raw, 1)
            dve.wait_ge(v_raw, 1)
            V.tensor_copy(vT, banks[6][:, :])
            V.tensor_copy(wiT[0:IDX_HEADS], banks[7][0:IDX_HEADS, :]).then_inc(v_raw, 1)
            dve.wait_ge(v_ps, 1)
            V.tensor_copy(vtok, banks[6][:, :].rearrange("p (t n) -> p t n", t=NT)).then_inc(v_copied, 1)
            V.tensor_scalar(wi, banks[7][:, :].rearrange("p (t n) -> p t n", t=NT)[:, :, 0:IDX_HEADS],
                            IDX_HEADS ** -0.5 * IDX_D ** -0.5, None, ALU.mult).then_inc(v_copied, 1)
            for name in ("uq0", "uq1", "qi0", "qi1", "qi2", "qi3"):
                start, chunks, bank = PANEL[name]
                split_before(start + chunks)
                dve.wait_ge(chunks_done, start + chunks)
                for f in range(4):
                    rope(banks[bank + f])
            dve.wait_ge(roped, turned[0])
            dve.wait_ge(causal_loaded, 16)
            dve.wait_ge(v_copied, 2)

            i_n = m = normed = 0

            def normalise(m, t):
                dve.wait_ge(exp_done, m + 1)
                then(V.reciprocal(rrec[:, m:m + 1], rsum[:, m:m + 1]))
                keys = (t + 1) * P
                V.tensor_scalar(probs[:, m % 2, 0:keys], probs[:, m % 2, 0:keys], rrec[:, m:m + 1], None,
                                ALU.mult).then_inc(probs_ready, 1)

            att = [s for s in STEPS if s[0] == "att"]
            for n, (kind, t, h) in enumerate(STEPS):
                keys = (t + 1) * P
                split_before(filled(att_fill, "ga0", n))
                if kind == "idx":
                    if m > normed and h == 2:
                        normalise(m - 1, att[m - 1][1])
                        normed = m
                    dve.wait_ge(relu_done, i_n + 1)
                    acc = causal[:, T - keys:T] if h == 0 else score[:, 0:keys]
                    here(V.scalar_tensor_tensor(out=score[:, 0:keys], in0=relu[:, i_n % 2, 0:keys],
                                                scalar=wi[:, t, h:h + 1], in1=acc, op0=ALU.mult, op1=ALU.add),
                         scored, i_n + 1)
                    i_n += 1
                    if h == IDX_HEADS - 1:
                        for r in range(TOPK // 8):
                            now, last = filled(att_fill, "ga0", n), before_waiting(n + 2)
                            split_before(min(now + r * (last - now) // (TOPK // 8) + 1, last))
                            then(V.max(out=top8, in_=score[:, 0:keys]))
                            then(V.match_replace(out=score[:, 0:keys], in_to_replace=top8,
                                                 in_values=score[:, 0:keys], imm_value=TAKEN))
                        then(V.tensor_scalar(bias[:, t % 2, 0:keys], score[:, 0:keys], (FILL + TAKEN) / 2, OUT,
                                             ALU.is_gt, ALU.mult))
                else:
                    dve.wait_ge(logits_ps, n + 1)
                    b = causal[:, T - keys:T] if t == 0 else bias[:, t % 2, 0:keys]
                    here(V.tensor_tensor_reduce(out=masked[:, m % 2, 0:keys], in0=banks[4 + n % 2][:, 0:keys], in1=b,
                                                scale=1.0, scalar=FILL, op0=ALU.add, op1=ALU.max,
                                                accum_out=smax[:, m:m + 1]), att_masked, m + 1)
                    V.tensor_scalar(nmax[:, m:m + 1], smax[:, m:m + 1], -HEAD_D ** -0.5, None, ALU.mult) \
                        .then_inc(nmax_ready, 1)
                    if m > normed:
                        normalise(m - 1, att[m - 1][1])
                        normed = m
                    m += 1
            normalise(m - 1, att[m - 1][1])
            split_before(filled(att_fill, "ga0", len(STEPS)))

            def tree_args(u):
                f, pair = u % 8 // 2, u % 2
                buf, tok = qk[u % 2], slice(pair * 256, pair * 256 + 256)
                if u >= 2:
                    dve.wait_ge(rec_ps, 2 * (u - 1))
                for m in range(LEVELS):
                    h = P >> (m + 1)
                    c = hc[:, f, tok].rearrange("p (b s h) -> p b s h", s=2, h=h)
                    o = buf[:, m, :].rearrange("p (b s h) -> p b s h", s=2, h=h)
                    mid = c[:, :, 0, h - 1:h].to_broadcast([P, 256 // (2 * h), h])
                    V.tensor_tensor(o[:, :, 1, :], c[:, :, 1, :], mid, ALU.subtract)
                    V.tensor_tensor(o[:, :, 0, :], mid, c[:, :, 0, :], ALU.subtract)
                c = hc[:, f, tok].rearrange("p (b t) -> p b t", t=P)
                V.tensor_tensor(buf[:, 7, :].rearrange("p (b t) -> p b t", t=P),
                                c[:, :, P - 1:P].to_broadcast([P, 2, P]), c, ALU.subtract).then_inc(tree_arg, 1)

            for b in range(2):
                def split_while(name):
                    for done in range(PANEL[name][0], sum(PANEL[name][:2]) + 1):
                        split_before(done)

                split_while(f"hq{b}")
                split_while(f"hf{b}")
                dve.wait_ge(hf_sigmoid, 4 * (b + 1))
                if b == 0:
                    dve.wait_ge(lb_exp, 1)
                    then(V.tensor_scalar(lb, lb, 1.0, None, ALU.add))
                    then(V.reciprocal(lb, lb))
                    then(V.tensor_scalar(one_lb, lb, -1.0, 1.0, ALU.mult, ALU.add))
                for f in range(4):
                    h = 4 * b + f
                    ins = V.tensor_scalar(hc[:, f, :], hk[:, f, :], one_lb[:, h:h + 1], lb[:, h:h + 1],
                                          ALU.mult, ALU.add)
                then(ins)
                here(V.tensor_scalar(hk, hc, -1.0, 1.0, ALU.mult, ALU.add), hf_ready, b + 1)
                for done in range(3):
                    split_before(PANEL[f"hi{b}"][0] + done)
                dve.wait_ge(hf_ln, b + 1)
                for f in range(4):
                    split_before(PANEL[f"hi{b}"][0] + 3 + f // 2)
                    ins = V.tensor_tensor_scan(out=hc[:, f, :], data0=restart, data1=hc[:, f, :], initial=0.0,
                                               op0=ALU.mult, op1=ALU.add)
                then(ins)
                split_while(f"hi{b}")
                tree_args(8 * b)
                for i in range(16):
                    n = 16 * b + i
                    c = n % 4
                    split_before(filled(rec_fill, REC_GATES[b][0], i))
                    for half in range(2):
                        dve.wait_ge(tree_ps, 2 * n + half + 1)
                        here(V.tensor_tensor(lev[:, half * 512:(half + 1) * 512], banks[4 + half][:, :],
                                             level_mask[:, half * 512:(half + 1) * 512], ALU.mult),
                             tree_masked, 2 * n + half + 1)
                    if n >= 2:
                        dve.wait_ge(rec_ps, n - 1)
                    here(V.tensor_reduce(intra[:, n % 2, :], lev.rearrange("p (m t) -> p t m", m=8), AX.X, ALU.add),
                         intra_ready, n + 1)
                    if i % 2 == 0 and i < 14:
                        tree_args(n // 2 + 1)
                    split_before(filled(rec_fill, REC_GATES[b][0], i + 1))
                    if c < 3:
                        dve.wait_ge(state_ps, n // 4 * 3 + c + 1)
                        if n:
                            dve.wait_ge(rec_ps, n)
                        if c == 0:
                            V.tensor_copy(state[:, 1, :], banks[6][:, 0:P]).then_inc(state_ready, 1)
                        else:
                            k = n // 2 % 2 * 2 + n % 2
                            V.scalar_tensor_tensor(out=state[:, (c + 1) % 2, :], in0=state[:, c % 2, :],
                                                   scalar=decay[:, k:k + 1], in1=banks[6][:, 0:P],
                                                   op0=ALU.mult, op1=ALU.add).then_inc(state_ready, 1)
            def output_low(k, src):
                dve.wait_ge(y_high, k + 1)
                V.tensor_tensor(yT[1][:, k, :], src, yT[0][:, k, :].bitcast(F32), ALU.subtract).then_inc(y_low, 1)

            dve.wait_ge(chunks_done, PANEL["pa0"][0])
            for h in range(A_HEADS):
                output_low(h, yattT[:, h, :])
            split_before(PANEL["pa0"][0] + 1)
            def gated(b):
                dve.wait_ge(hg_loaded[b], 16)
                for f in range(4):
                    h = 4 * b + f
                    V.scalar_tensor_tensor(out=yrecT[:, h, :], in0=yrecT[:, h, :], scalar=ghc[:, h:h + 1],
                                           in1=(hc, hv)[b][:, f, :], op0=ALU.mult, op1=ALU.mult).then_inc(hg_mul, 1)

            dve.wait_ge(rec_squared, G_HEADS)
            gated(0)
            dve.wait_ge(recsq_ps, 1)
            then(V.tensor_scalar(lev[:, 0:T], banks[0][:, :], 1.0 / G_WIDTH, EPS, ALU.mult, ALU.add))
            here(V.tensor_copy(lev[:, T:T + 1], lev[:, 0:1]), mean_ready, 2)
            gated(1)
            dve.wait_ge(rooted, 2)
            then(V.reciprocal(lev[:, 0:T], lev[:, 0:T]))
            split_before(PANEL["pa0"][0] + 2)
            dve.wait_ge(hg_mul, G_HEADS)
            for h in range(G_HEADS):
                V.tensor_tensor(yrecT[:, h, :], yrecT[:, h, :], lev[:, 0:T], ALU.mult).then_inc(hg_ready, 1)
            split_before(PANEL["pa0"][0] + 3)
            for h in range(G_HEADS):
                if h == 2:
                    split_before(PANEL["pb0"][0])
                output_low(A_HEADS + h, yrecT[:, h, :])

            def merged_low(k):
                dve.wait_ge(merged_high, k + 1)
                V.tensor_tensor(mergedT[1][:, k, :], mT[:, k, :], mergedT[0][:, k, :].bitcast(F32), ALU.subtract) \
                    .then_inc(merged_ready, 1)

            for b in range(4):
                split_before(sum(PANEL[f"pa{b}"][:2]))
                dve.wait_ge(gate_loaded, 32 * (b + 1))
                for k, (name, g) in enumerate((("pa", gate_a), ("pb", gate_b))):
                    start, chunks, bank = PANEL[f"{name}{b}"]
                    if k == 1 and b == 3:
                        for kk in range(8):
                            if kk == 4:
                                split_before(start + 1)
                            merged_low(kk)
                    split_before(start + chunks)
                    dve.wait_ge(chunks_done, start + chunks)
                    for f in range(4):
                        if k == 0:
                            V.tensor_tensor(mT[:, 4 * b + f, :], banks[bank + f][:, :], g[:, f, :], ALU.mult) \
                                .then_inc(merge_read, 1)
                        else:
                            here(V.tensor_tensor(g[:, f, :], banks[bank + f][:, :], g[:, f, :], ALU.mult),
                                 merge_read, 8 * b + 4 + f + 1)
                            V.tensor_tensor(mT[:, 4 * b + f, :], mT[:, 4 * b + f, :], g[:, f, :], ALU.add) \
                                .then_inc(merged_sum, 1)
            split_before(PANEL["wo0"][0])
            for k in range(8, KD):
                merged_low(k)
            for b in range(4):
                start, chunks, bank = PANEL[f"wo{b}"]
                for done in range(start, start + chunks + 1):
                    split_before(done)
                for t in range(NT if b == 0 else 0):
                    dve.wait_ge(x_loaded[t], 32)
                dve.wait_ge(chunks_done, start + chunks)
                for t in range(NT):
                    cols = x1[:, t, b * 512:(b + 1) * 512]
                    V.tensor_tensor(cols, banks[bank + t][:, :], cols, ALU.add).then_inc(x1_ready, 1)
            dve.wait_ge(squared, 4 + 4 * NT)
            then(V.tensor_reduce(ssum, ssum_parts, AX.X, ALU.add))
            V.tensor_scalar(mean, ssum, 1.0 / D, EPS, ALU.mult, ALU.add).then_inc(mean_ready, 1)
            dve.wait_ge(rooted, 3)
            then(V.reciprocal(rinv, mean))
            dve.wait_ge(late_loaded, 16 * 7)
            for b in range(4):
                for t in range(NT):
                    cols = slice(b * 512, (b + 1) * 512)
                    V.scalar_tensor_tensor(out=h2[:, t, cols], in0=x1[:, t, cols], scalar=rinv[:, t:t + 1],
                                           in1=g2b[:, cols], op0=ALU.mult, op1=ALU.mult).then_inc(h2_ready, 1)
            here(V.memset(logitsT, 0.0), logitsT_ready, 1)
            for k in range(4, KD, 2):
                dve.wait_ge(h2T_ps, k + 1)
                if k >= 4:
                    dve.wait_ge(router_ps, k - 3)
                V.tensor_copy(h2T[:, k % 4, :], banks[k % 4][:, :]).then_inc(h2T_dve, 1)

            def over_tokens(v, n):
                return v.unsqueeze(1).to_broadcast([P, NT, n])

            iota32, e_r = rowc[:, 36:68], rowc[:, 68:100]
            step_r = rowc[:, 100:132]
            then(V.memset(lg, FILL))
            dve.wait_ge(router_ps, KD)
            V.tensor_copy(logitsT[0:36], banks[4][0:36, :]).then_inc(logitsT_ready, 1)
            dve.wait_ge(logits_done, 1)
            logits = banks[5][:, :].rearrange("p (t n) -> p t n", t=NT)
            V.tensor_tensor(lg[:, :, 0:4], logits[:, :, 0:4], over_tokens(rowc[:, 0:4], 4), ALU.add)
            then(V.tensor_tensor(le, logits[:, :, 4:36], over_tokens(rowc[:, 4:36], 32), ALU.add))
            for t in range(NT):
                ins = V.max(out=g8[:, t, :], in_=lg[:, t, :])
            then(ins)
            for t in range(NT):
                V.max_index(out=gi8[:, t, :], in_max=g8[:, t, :], in_values=lg[:, t, :])
            here(V.tensor_scalar(gneg, g8[:, :, 0], -1.0, None, ALU.mult), route_arg, 1)
            then(V.tensor_copy(gidx, gi8[:, :, 0]))
            then(V.tensor_tensor(gout, over_tokens(iota32[:, 0:4], 4), gidx.unsqueeze(2).to_broadcast([P, NT, 4]),
                                 ALU.not_equal))
            then(V.tensor_scalar(gout, gout, OUT, None, ALU.mult))
            then(V.tensor_tensor(le.rearrange("p t (g e) -> p t g e", g=4), le.rearrange("p t (g e) -> p t g e", g=4),
                                 gout.unsqueeze(3).to_broadcast([P, NT, 4, 8]), ALU.add))
            for t in range(NT):
                ins = V.max(out=e8[:, t, :], in_=le[:, t, :])
            then(ins)
            for t in range(NT):
                ins = V.max_index(out=ei8[:, t, :], in_max=e8[:, t, :], in_values=le[:, t, :])
            then(ins)
            here(V.tensor_tensor(diff, e8[:, :, 1], e8[:, :, 0], ALU.subtract), route_arg, 2)
            for c in range(2):
                then(V.tensor_copy(eidx[:, c, :], ei8[:, :, c]))
                then(V.tensor_tensor(pick[:, c], over_tokens(iota32, 32),
                                     eidx[:, c, :].unsqueeze(2).to_broadcast([P, NT, 32]), ALU.is_equal))
            here(V.tensor_tensor(both, pick[:, 0], pick[:, 1], ALU.add), picked, 1)
            dve.wait_ge(route_exp, 5)
            then(V.tensor_scalar(den, diff, 1.0, None, ALU.add))
            then(V.tensor_tensor(den, den, gsum, ALU.mult))
            then(V.reciprocal(gate1, den))
            then(V.tensor_tensor(gate2, gate1, diff, ALU.mult))
            dve.wait_ge(x1_ready, 16)
            V.tensor_copy(gate1k, gate1)
            V.tensor_copy(gate2k, gate2)
            dve.wait_ge(rank_ps, 1)
            V.tensor_copy(rank, banks[1][:, 0:NT * N_EXP].rearrange("p (t e) -> p t e", t=NT))
            then(V.tensor_copy(count, banks[1][:, NT * N_EXP:(NT + 1) * N_EXP]))
            then(V.tensor_scalar(extra, count, float(R), None, ALU.is_gt))
            for k in range(2, T // R):
                then(V.scalar_tensor_tensor(out=extra, in0=count, scalar=float(k * R), in1=extra, op0=ALU.is_gt,
                                            op1=ALU.add))
            then(V.memset(ones_e, 1.0))
            then(V.tensor_tensor_scan(out=upto, data0=ones_e, data1=extra, initial=0.0, op0=ALU.mult, op1=ALU.add))
            then(V.tensor_tensor(base, upto, extra, ALU.subtract))
            then(V.scalar_tensor_tensor(out=delta, in0=base, scalar=float(R), in1=step_r, op0=ALU.mult, op1=ALU.add))
            then(V.scalar_tensor_tensor(out=pos, in0=rank, scalar=float(R), in1=over_tokens(delta, 32),
                                        op0=ALU.is_ge, op1=ALU.mult))
            then(V.tensor_tensor(pos, pos, rank, ALU.add))
            then(V.tensor_tensor(pos, pos, over_tokens(e_r, 32), ALU.add))
            for c in range(2):
                then(V.tensor_tensor(posp, pos, pick[:, c], ALU.mult))
                then(V.tensor_reduce(slot[:, c, :], posp, AX.X, ALU.add))
            here(V.tensor_copy(slot_u.rearrange("p (c t) -> p c t", c=2), slot), placed, 1)
            V.tensor_copy(ctrl_f[:, 0:1], upto[:, N_EXP - 1:N_EXP])
            for k in range(TILES - OVER):
                then(V.tensor_scalar(posp[:, 0, :], upto, float(k), None, ALU.is_le))
                then(V.tensor_reduce(ctrl_f[:, 1 + k:2 + k], posp[:, 0, :], AX.X, ALU.add))
            then(V.tensor_scalar(ctrl_f[:, 1:16], ctrl_f[:, 1:16], float(N_EXP - 1), None, ALU.min))
            V.tensor_copy(ctrl_u[:, 0:16], ctrl_f[:, 0:16])
            V.memset(act_all, 0.0).then_inc(slots_ready, 1)

            def transposed_rows(tile, g):
                dve.wait_ge(xgT_high, tile * 2 + (g + 1))
                V.tensor_tensor(xgT[1][:, 8 * g:8 * g + 8, :], banks[2 + g][:, :].rearrange("p (k n) -> p k n", k=8),
                                xgT[0][:, 8 * g:8 * g + 8, :].bitcast(F32), ALU.subtract).then_inc(xgT_low, 1)

            def split_chunks_of(tile, first, end, last=False):
                for c in range(first, min(end, E_CHUNKS) if last else end):
                    this, cc = (tile, c) if c < E_CHUNKS else (tile + 1, c - E_CHUNKS)
                    dve.wait_ge(e_high_ready, this * E_CHUNKS + (cc + 1))
                    V.tensor_tensor(e_low[cc % E_SPLIT_SLOTS], e_ring[cc % E_SLOTS],
                                    e_high[cc % E_SPLIT_SLOTS].bitcast(F32), ALU.subtract).then_inc(e_low_ready, 1)

            def expert_tile(tile, last=False):
                used = tile * E_CHUNKS

                split_chunks_of(tile, E_SPLIT_SLOTS, 8 + AHEAD)
                split_chunks_of(tile, 8 + AHEAD, 16 + AHEAD)
                dve.wait_ge(silu_done, tile + 1)
                dve.wait_ge(e_done, used + 16)
                V.tensor_tensor(act_h, banks[1][0:R, :], act_e, ALU.mult).then_inc(act_ready, 1)
                transposed_rows(tile + 1, 0)
                dve.wait_ge(actT_high, tile + 1)
                V.tensor_tensor(actT[1], banks[0][:, 0:4 * R].rearrange("p (k n) -> p k n", k=4),
                                actT[0].bitcast(F32), ALU.subtract).then_inc(actT_low, 1)
                transposed_rows(tile + 1, 1)
                dve.wait_ge(yb_sent, tile * 16 + 16)
                for cb in range(4):
                    split_chunks_of(tile, 16 + 2 * cb + AHEAD, 16 + 2 * cb + 2 + AHEAD, last)
                    if cb % 2:
                        dve.wait_ge(e_done, used + (16 + 2 * cb + 2))
                        V.tensor_copy(yb[:, cb * 512:(cb + 1) * 512], banks[4 + cb][0:R, :]).then_inc(y_dve, 1)
                split_chunks_of(tile, E_CHUNKS + AHEAD, E_CHUNKS + E_SPLIT_SLOTS, last)

            split_chunks_of(0, 0, E_SPLIT_SLOTS)
            for g in range(2):
                transposed_rows(0, g)
            with dve.Fori(0, N_EXP - 1) as tile:
                expert_tile(tile)
            expert_tile(N_EXP - 1, True)
            over = dve.value_load(ctrl_u[0:1, 0:1], min_val=0, max_val=TILES - OVER)
            with dve.If(over > 0):
                split_chunks_of(OVER, 0, E_SPLIT_SLOTS)
                with dve.Fori(0, TILES - OVER - 1) as i:
                    expert_tile(i + OVER)
                expert_tile(TILES - 1, True)

            def add_rows(t):
                dve.wait_ge(yfin_loaded[t], 16)
                then(V.scalar_tensor_tensor(out=x1[:, t, :], in0=yfin[t][:, 0, :], scalar=gate1k[:, t:t + 1],
                                            in1=x1[:, t, :], op0=ALU.mult, op1=ALU.add))
                here(V.scalar_tensor_tensor(out=x1[:, t, :], in0=yfin[t][:, 1, :], scalar=gate2k[:, t:t + 1],
                                            in1=x1[:, t, :], op0=ALU.mult, op1=ALU.add), fin_args, t + 1)

            add_rows(0)
            for t in range(NT):
                if t + 1 < NT:
                    add_rows(t + 1)
                dve.wait_ge(squared, 4 + 4 * NT + t + 1)
                V.tensor_scalar(fmean[:, t:t + 1], fsum[:, t:t + 1], 1.0 / D, EPS, ALU.mult, ALU.add) \
                    .then_inc(fin_mean, 1)
                dve.wait_ge(fin_act, t + 1)
                then(V.reciprocal(fmean[:, t:t + 1], fmean[:, t:t + 1]))
                V.scalar_tensor_tensor(out=x1[:, t, :], in0=x1[:, t, :], scalar=fmean[:, t:t + 1], in1=gfb,
                                       op0=ALU.mult, op1=ALU.mult).then_inc(fin_dve, 1)


INPUTS = ["x", "w_in", "w_uq", "w_qidx", "w_pa", "w_pb", "w_o", "g_norm2", "w_grp", "b_grp",
          "w_exp", "b_exp", "w_gate", "w_up", "w_down", "g_final"]


def tables():
    f = np.float32
    i = np.arange(P)
    levels = []
    for m in range(LEVELS):
        h = P >> (m + 1)
        same = i[:, None] // (2 * h) == i[None, :] // (2 * h)
        levels.append(same & (i[:, None] % (2 * h) < h) & (i[None, :] % (2 * h) >= h))
    levels.append(i[:, None] == i[None, :])
    restart = np.broadcast_to((np.arange(T) % P != 0).astype(f), (P, T))
    const = np.concatenate([np.eye(P), np.ones((P, P)), i[:, None] < i[None, :], *levels, restart], 1).astype(f)
    inv = (1.0 / (f(10000.0) ** (np.arange(0, HEAD_D, 2, dtype=f) / f(HEAD_D)))).astype(f)
    ang = (np.arange(T, dtype=f)[None, :] * inv[:, None]).astype(f)
    cos, sin = np.cos(ang), np.sin(ang)
    rope = np.concatenate([np.concatenate([cos, cos], 0), np.concatenate([sin, -sin], 0)], 1).astype(f)
    causal = np.zeros((P, T), f)
    causal[:, T - P:][i[None, :] > i[:, None]] = FILL
    e = np.arange(N_EXP, dtype=f)
    route = np.concatenate([e, e * R, (OVER - 1 - e) * R, 0 * e])
    route = np.broadcast_to(route, (P, 4 * N_EXP)).astype(f)
    rows = np.zeros((P, 2, NT, 2), np.uint32)
    for c in range(2):
        for t in range(NT):
            rows[:, c, t, 0] = t * P + i
            rows[:, c, t, 1] = 2 * (t * P + i) + c
    return {"t_const": const, "t_rope": rope, "t_causal": causal, "t_route": np.ascontiguousarray(route),
            "t_rows": rows.reshape(P, -1)}


def layout(inputs):
    arrays = {n: np.ascontiguousarray(inputs[n]) for n in INPUTS}
    for n in ("w_in", "w_uq", "w_qidx", "w_pa", "w_pb", "w_o", "w_gate", "w_up", "w_down"):
        arrays[n] = arrays[n][0]
    columns = [np.asarray(inputs[n])[0] for n in ("g_norm1", "g_cq", "g_hnorm")] + list(np.asarray(inputs["lb_logits"]))
    arrays["gains"] = np.ascontiguousarray(np.concatenate([c.reshape(-1, P) for c in columns], 0).T)
    arrays.update(tables())
    return arrays


def kernel(**inputs):
    import concourse.bacc as bacc
    from concourse.bass_utils import run_bass_kernel_spmd

    arrays = layout(inputs)
    nc = bacc.Bacc("TRN2", target_bir_lowering=False, num_devices=1)
    args = {n: nc.dram_tensor(n, a.shape, mybir.dt.from_np(a.dtype), kind="ExternalInput").ap()
            for n, a in arrays.items()}
    out = nc.dram_tensor("out", (1, T, D), F32, kind="ExternalOutput").ap()
    build(nc, **args, out=out)
    r = run_bass_kernel_spmd(nc, [arrays], core_ids=[0])
    return r.results[0]["out"]
```
